# Optimizing a Trainium2 kernel written in Bass

```python
import math
import jax
import jax.numpy as jnp
from jax import lax
import numpy as np

D_MODEL = 1024
BATCH = 1
SEQ = 256
DEPTH = 2

HEAD_DIM = 64
CHUNK = 64
FOX_HEADS = 4
FOX_BLOCK = 128
GLA_HEADS = 4
GLA_LOWRANK = 16
GLA_TAU = 16.0
RET_HEADS = 4
ROPE_THETA = 10000.0
SSD_HEADS = 8
SSD_GROUPS = 2
SSD_STATE = 64
SSD_CONV = 4
SSD_INNER = SSD_HEADS * HEAD_DIM
SSD_CONV_CH = SSD_INNER + 2 * SSD_GROUPS * SSD_STATE
FOX_W = FOX_HEADS * HEAD_DIM
GLA_W = GLA_HEADS * HEAD_DIM
RET_W = RET_HEADS * HEAD_DIM
N_BRANCH = 4
FFN_HIDDEN = ((8 * D_MODEL + 3 * 256 - 1) // (3 * 256)) * 256
NORM_EPS = 1e-6
IN_SPLITS = (FOX_W, FOX_W, FOX_W, FOX_HEADS,
             GLA_W, GLA_W, GLA_W, GLA_LOWRANK, GLA_W,
             RET_W, RET_W, RET_W, RET_W,
             SSD_INNER, SSD_CONV_CH, SSD_HEADS,
             N_BRANCH * D_MODEL)
N_IN = sum(IN_SPLITS)


def rms_norm(x, g):
    xf = x.astype(jnp.float32)
    y = xf * lax.rsqrt(jnp.mean(xf * xf, axis=-1, keepdims=True) + NORM_EPS)
    return (y * g.astype(jnp.float32)).astype(x.dtype)

def split_cols(u, sizes):
    return jnp.split(u, np.cumsum(sizes)[:-1].tolist(), axis=-1)

def rotary_tables(positions):
    half = HEAD_DIM // 2
    inv = ROPE_THETA ** (-jnp.arange(half, dtype=jnp.float32) / half)
    ang = positions.astype(jnp.float32)[..., None] * inv
    return jnp.cos(ang)[:, :, None, :], jnp.sin(ang)[:, :, None, :]

def apply_rotary(x, cos, sin):
    half = x.shape[-1] // 2
    xf = x.astype(jnp.float32)
    x1, x2 = xf[..., :half], xf[..., half:]
    return jnp.concatenate([x1 * cos - x2 * sin, x1 * sin + x2 * cos], axis=-1).astype(x.dtype)

def causal_depthwise_conv(x, w, b):
    k_w, ch = w.shape
    y = lax.conv_general_dilated(x, w[:, None, :], window_strides=(1,), padding=[(k_w - 1, 0)],
                                 dimension_numbers=('NWC', 'WIO', 'NWC'), feature_group_count=ch)
    return y + b

def forgetting_attention(q, k, v, f_logit, q_gain, k_gain):
    bsz, seq, nh, dh = q.shape
    nb = seq // FOX_BLOCK
    qf = rms_norm(q, q_gain).astype(jnp.float32) * (dh ** -0.5)
    kf = rms_norm(k, k_gain).astype(jnp.float32)
    vf = v.astype(jnp.float32)
    c = jnp.cumsum(jax.nn.log_sigmoid(f_logit.astype(jnp.float32)), axis=1)
    qb = qf.reshape(bsz, nb, FOX_BLOCK, nh, dh).transpose(1, 0, 3, 2, 4)
    cb = c.reshape(bsz, nb, FOX_BLOCK, nh).transpose(1, 0, 3, 2)
    ck = c.transpose(0, 2, 1)
    kpos = jnp.arange(seq)

    def block(args):
        q_blk, c_blk, i = args
        s = jnp.einsum('bhqd,bkhd->bhqk', q_blk, kf) + c_blk[..., :, None] - ck[..., None, :]
        qpos = i * FOX_BLOCK + jnp.arange(FOX_BLOCK)
        s = jnp.where(kpos[None, :] <= qpos[:, None], s, -jnp.inf)
        p = jax.nn.softmax(s, axis=-1)
        return jnp.einsum('bhqk,bkhd->bqhd', p, vf)

    o = lax.map(block, (qb, cb, jnp.arange(nb)))
    return o.transpose(1, 0, 2, 3, 4).reshape(bsz, seq, nh * dh).astype(v.dtype)

def gla_chunked(q, k, v, log_a):
    bsz, seq, nh, dk = q.shape
    dv = v.shape[-1]
    nc = seq // CHUNK
    qf = (q.astype(jnp.float32) * (dk ** -0.5)).reshape(bsz, nc, CHUNK, nh, dk)
    kf = k.astype(jnp.float32).reshape(bsz, nc, CHUNK, nh, dk)
    vf = v.astype(jnp.float32).reshape(bsz, nc, CHUNK, nh, dv)
    b = jnp.cumsum(log_a.astype(jnp.float32).reshape(bsz, nc, CHUNK, nh, dk), axis=2)
    b_last = b[:, :, -1]
    q_dec = qf * jnp.exp(b)
    k_inv = kf * jnp.exp(-b)
    k_end = kf * jnp.exp(b_last[:, :, None] - b)
    mask = jnp.tril(jnp.ones((CHUNK, CHUNK), dtype=bool))
    attn = jnp.where(mask, jnp.einsum('bcthd,bcshd->bchts', q_dec, k_inv), 0.0)
    o_intra = jnp.einsum('bchts,bcshv->bcthv', attn, vf)
    kv = jnp.einsum('bcshd,bcshv->bchdv', k_end, vf)

    def step(state, inp):
        kv_c, dec_c = inp
        return state * dec_c[..., None] + kv_c, state

    s0 = jnp.zeros((bsz, nh, dk, dv), jnp.float32)
    _, s_in = lax.scan(step, s0, (jnp.moveaxis(kv, 1, 0), jnp.moveaxis(jnp.exp(b_last), 1, 0)))
    s_in = jnp.moveaxis(s_in, 0, 1)
    o_inter = jnp.einsum('bcthd,bchdv->bcthv', q_dec, s_in)
    return (o_intra + o_inter).reshape(bsz, seq, nh, dv).astype(v.dtype)

def retention_chunked(q, k, v, log_gamma):
    bsz, seq, nh, dk = q.shape
    dv = v.shape[-1]
    nc = seq // CHUNK
    qf = q.astype(jnp.float32).reshape(bsz, nc, CHUNK, nh, dk)
    kf = (k.astype(jnp.float32) * (dk ** -0.5)).reshape(bsz, nc, CHUNK, nh, dk)
    vf = v.astype(jnp.float32).reshape(bsz, nc, CHUNK, nh, dv)
    idx = jnp.arange(CHUNK, dtype=jnp.float32)
    rel = idx[:, None] - idx[None, :]
    decay = jnp.where(rel >= 0, jnp.exp(jnp.maximum(rel, 0.0)[None] * log_gamma[:, None, None]), 0.0)
    scores = jnp.einsum('bcthd,bcshd->bchts', qf, kf) * decay
    o_intra = jnp.einsum('bchts,bcshv->bcthv', scores, vf)
    q_w = jnp.exp((idx + 1.0)[:, None] * log_gamma)
    k_w = jnp.exp((CHUNK - 1.0 - idx)[:, None] * log_gamma)
    kv = jnp.einsum('bcshd,sh,bcshv->bchdv', kf, k_w, vf)
    chunk_decay = jnp.exp(CHUNK * log_gamma)

    def step(state, kv_c):
        return state * chunk_decay[:, None, None] + kv_c, state

    s0 = jnp.zeros((bsz, nh, dk, dv), jnp.float32)
    _, s_in = lax.scan(step, s0, jnp.moveaxis(kv, 1, 0))
    s_in = jnp.moveaxis(s_in, 0, 1)
    o_inter = jnp.einsum('bcthd,th,bchdv->bcthv', qf, q_w, s_in)
    return (o_intra + o_inter).reshape(bsz, seq, nh, dv).astype(v.dtype)

def ssd_chunked(x, dt, a, bmat, cmat):
    bsz, seq, nh, hp = x.shape
    ng, ns = bmat.shape[2], bmat.shape[3]
    r = nh // ng
    nc = seq // CHUNK
    xf = x.astype(jnp.float32).reshape(bsz, nc, CHUNK, ng, r, hp)
    dtf = dt.astype(jnp.float32).reshape(bsz, nc, CHUNK, ng, r)
    bf = bmat.astype(jnp.float32).reshape(bsz, nc, CHUNK, ng, ns)
    cf = cmat.astype(jnp.float32).reshape(bsz, nc, CHUNK, ng, ns)
    xdt = xf * dtf[..., None]
    cs = jnp.cumsum(dtf * a.astype(jnp.float32).reshape(ng, r), axis=2)
    cs_h = jnp.moveaxis(cs, 2, -1)
    mask = jnp.tril(jnp.ones((CHUNK, CHUNK), dtype=bool))
    seg = cs_h[..., :, None] - cs_h[..., None, :]
    decay = jnp.exp(jnp.where(mask, seg, -jnp.inf))
    cb = jnp.einsum('bctgn,bcsgn->bcgts', cf, bf)
    y_intra = jnp.einsum('bcgts,bcgrts,bcsgrp->bctgrp', cb, decay, xdt)
    cs_last = cs[:, :, -1]
    w_end = jnp.exp(cs_last[:, :, None] - cs)
    contrib = jnp.einsum('bcsgn,bcsgr,bcsgrp->bcgrpn', bf, w_end, xdt)

    def step(h, inp):
        c_c, d_c = inp
        return h * d_c[..., None, None] + c_c, h

    h0 = jnp.zeros((bsz, ng, r, hp, ns), jnp.float32)
    _, h_in = lax.scan(step, h0, (jnp.moveaxis(contrib, 1, 0), jnp.moveaxis(jnp.exp(cs_last), 1, 0)))
    h_in = jnp.moveaxis(h_in, 0, 1)
    y_inter = jnp.einsum('bctgn,bcgrpn,bctgr->bctgrp', cf, h_in, jnp.exp(cs))
    return (y_intra + y_inter).reshape(bsz, seq, nh, hp).astype(x.dtype)

def mixer_block(h, cos, sin, w_in, fox_bf, fox_qn, fox_kn, gla_w2, gla_b, gla_norm, ret_norm,
                conv_w, conv_b, dt_bias, a_log, d_skip, ssd_norm, w_up_a, w_up_b, w_up_c, w_up_d, w_out):
    bsz, seq, _ = h.shape
    u = h @ w_in
    (fq, fk, fv, ff, gq, gk, gv, glr, gr, rq, rk, rv, rg, z, xbc, dt, gates) = split_cols(u, IN_SPLITS)
    heads = lambda t: t.reshape(bsz, seq, -1, HEAD_DIM)
    y_a = forgetting_attention(heads(fq), heads(fk), heads(fv), ff + fox_bf, fox_qn, fox_kn)
    log_a = jax.nn.log_sigmoid((glr @ gla_w2 + gla_b).astype(jnp.float32)) / GLA_TAU
    o_b = gla_chunked(heads(gq), heads(gk), heads(gv), heads(log_a))
    y_b = (rms_norm(o_b, gla_norm) * jax.nn.silu(heads(gr))).reshape(bsz, seq, GLA_W)
    log_gamma = jnp.log(1.0 - 2.0 ** (-5.0 - jnp.arange(RET_HEADS, dtype=jnp.float32)))
    o_c = retention_chunked(apply_rotary(heads(rq), cos, sin), apply_rotary(heads(rk), cos, sin), heads(rv), log_gamma)
    y_c = (rms_norm(o_c, ret_norm) * jax.nn.silu(heads(rg))).reshape(bsz, seq, RET_W)
    xbc = jax.nn.silu(causal_depthwise_conv(xbc, conv_w, conv_b))
    xs, bm, cm = jnp.split(xbc, [SSD_INNER, SSD_INNER + SSD_GROUPS * SSD_STATE], axis=-1)
    dt = jax.nn.softplus((dt + dt_bias).astype(jnp.float32))
    a = -jnp.exp(a_log.astype(jnp.float32))
    xs_h = heads(xs)
    o_d = ssd_chunked(xs_h, dt, a, bm.reshape(bsz, seq, SSD_GROUPS, SSD_STATE), cm.reshape(bsz, seq, SSD_GROUPS, SSD_STATE))
    o_d = o_d + d_skip[:, None] * xs_h
    y_d = (o_d.reshape(bsz, seq, SSD_INNER) * jax.nn.silu(z)).reshape(bsz, seq, SSD_GROUPS, -1)
    y_d = rms_norm(y_d, ssd_norm.reshape(SSD_GROUPS, -1)).reshape(bsz, seq, SSD_INNER)
    g = jax.nn.sigmoid(gates.reshape(bsz, seq, N_BRANCH, D_MODEL))
    merged = (g[:, :, 0] * (y_a @ w_up_a) + g[:, :, 1] * (y_b @ w_up_b)
              + g[:, :, 2] * (y_c @ w_up_c) + g[:, :, 3] * (y_d @ w_up_d))
    return merged @ w_out

def swiglu(h, w_in, w_out):
    gate, up = jnp.split(h @ w_in, 2, axis=-1)
    return (jax.nn.silu(gate) * up) @ w_out

def first_inputs(seed: int = 0) -> dict:
    key = jax.random.key(seed)
    ks = jax.random.split(key, 26)
    f32 = jnp.float32
    L = DEPTH

    def normal(k, shape, fan_in):
        return jax.random.normal(k, shape, f32) * (fan_in ** -0.5)

    def gain(k, shape):
        return 1.0 + 0.02 * jax.random.normal(k, shape, f32)

    x = jax.random.normal(ks[0], (BATCH, SEQ, D_MODEL), f32)
    start = jax.random.randint(ks[1], (BATCH, 1), 0, 1024, dtype=jnp.int32)
    positions = start + jnp.arange(SEQ, dtype=jnp.int32)[None, :]
    dt0 = jnp.exp(jax.random.uniform(ks[14], (L, SSD_HEADS), f32, math.log(1e-3), math.log(1e-1)))
    return {
        'x': x,
        'positions': positions,
        'ln1': gain(ks[2], (L, D_MODEL)),
        'ln2': gain(ks[3], (L, D_MODEL)),
        'w_in': normal(ks[4], (L, D_MODEL, N_IN), D_MODEL),
        'fox_bf': jax.random.uniform(ks[5], (L, FOX_HEADS), f32, 1.0, 5.0),
        'fox_qn': gain(ks[6], (L, HEAD_DIM)),
        'fox_kn': gain(ks[7], (L, HEAD_DIM)),
        'gla_w2': normal(ks[8], (L, GLA_LOWRANK, GLA_W), GLA_LOWRANK),
        'gla_b': 0.1 * jax.random.normal(ks[9], (L, GLA_W), f32),
        'gla_norm': gain(ks[10], (L, HEAD_DIM)),
        'ret_norm': gain(ks[11], (L, HEAD_DIM)),
        'ssd_conv_w': normal(ks[12], (L, SSD_CONV, SSD_CONV_CH), SSD_CONV),
        'ssd_conv_b': 0.01 * jax.random.normal(ks[13], (L, SSD_CONV_CH), f32),
        'ssd_dt_bias': dt0 + jnp.log(-jnp.expm1(-dt0)),
        'ssd_a_log': jnp.log(jax.random.uniform(ks[15], (L, SSD_HEADS), f32, 1.0, 16.0)),
        'ssd_d': 1.0 + 0.1 * jax.random.normal(ks[16], (L, SSD_HEADS), f32),
        'ssd_norm': gain(ks[17], (L, SSD_INNER)),
        'w_up_a': normal(ks[18], (L, FOX_W, D_MODEL), FOX_W),
        'w_up_b': normal(ks[19], (L, GLA_W, D_MODEL), GLA_W),
        'w_up_c': normal(ks[20], (L, RET_W, D_MODEL), RET_W),
        'w_up_d': normal(ks[21], (L, SSD_INNER, D_MODEL), SSD_INNER),
        'w_out': normal(ks[22], (L, D_MODEL, D_MODEL), D_MODEL),
        'w_ffn_in': normal(ks[23], (L, D_MODEL, 2 * FFN_HIDDEN), D_MODEL),
        'w_ffn_out': normal(ks[24], (L, FFN_HIDDEN, D_MODEL), FFN_HIDDEN),
    }

def first_block(x, positions, ln1, ln2, w_in, fox_bf, fox_qn, fox_kn, gla_w2, gla_b, gla_norm, ret_norm,
              ssd_conv_w, ssd_conv_b, ssd_dt_bias, ssd_a_log, ssd_d, ssd_norm,
              w_up_a, w_up_b, w_up_c, w_up_d, w_out, w_ffn_in, w_ffn_out):
    cos, sin = rotary_tables(positions)
    for l in range(DEPTH):
        h = rms_norm(x, ln1[l])
        x = x + mixer_block(h, cos, sin, w_in[l], fox_bf[l], fox_qn[l], fox_kn[l], gla_w2[l], gla_b[l],
                            gla_norm[l], ret_norm[l], ssd_conv_w[l], ssd_conv_b[l], ssd_dt_bias[l],
                            ssd_a_log[l], ssd_d[l], ssd_norm[l], w_up_a[l], w_up_b[l], w_up_c[l],
                            w_up_d[l], w_out[l])
        h = rms_norm(x, ln2[l])
        x = x + swiglu(h, w_ffn_in[l], w_ffn_out[l])
    return x


GRID_W = 64
CTX_LEN = 256
N_MIXERS = 4
N_MOD = 9
D_FF = 2816
EPS = 1e-6
ROPE_BASE = 10000.0
ROPE_DIM = 64
Q_BLOCK = 128
NEG_INF = -1e30

MLA_HEADS = 8
MLA_Q_RANK = 512
MLA_KV_RANK = 256
MLA_NOPE = 128
MLA_ROPE = ROPE_DIM
MLA_V = 128

SWA_Q_HEADS = 16
SWA_KV_HEADS = 4
SWA_GROUP = SWA_Q_HEADS // SWA_KV_HEADS
SWA_HEAD_DIM = ROPE_DIM
SWA_WINDOW = 128

NA_HEADS = 16
NA_HEAD_DIM = D_MODEL // NA_HEADS
NA_KH = 8
NA_KW = 16

DIFF_HEADS = 8
DIFF_HEAD_DIM = ROPE_DIM


def rms_norm_2(x, g):
    xf = x.astype(jnp.float32)
    y = xf * lax.rsqrt(jnp.mean(xf * xf, axis=-1, keepdims=True) + EPS)
    return (y * g.astype(jnp.float32)).astype(x.dtype)

def modulate(h, shift, scale):
    return h * (1.0 + scale) + shift

def swiglu_2(h, w_in, w_out):
    g, u = jnp.split(h @ w_in, 2, axis=-1)
    return (jax.nn.silu(g) * u) @ w_out

def axial_rope_tables(L, dim):
    t = jnp.arange(L, dtype=jnp.int32)
    row = (t // GRID_W).astype(jnp.float32)
    col = (t % GRID_W).astype(jnp.float32)
    n_freq = dim // 4
    inv = jnp.exp(-math.log(ROPE_BASE) * jnp.arange(n_freq, dtype=jnp.float32) / n_freq)
    ang = jnp.concatenate([row[:, None] * inv, col[:, None] * inv], axis=-1)
    return jnp.cos(ang), jnp.sin(ang)

def apply_rope(x, cos, sin):
    half = x.shape[-1] // 2
    x1 = x[..., :half].astype(jnp.float32)
    x2 = x[..., half:].astype(jnp.float32)
    return jnp.concatenate([x1 * cos - x2 * sin, x1 * sin + x2 * cos], axis=-1).astype(x.dtype)

def softmax32(s):
    return jax.nn.softmax(s.astype(jnp.float32), axis=-1)

def joint_softmax(*scores):
    sizes = [s.shape[-1] for s in scores]
    p = softmax32(jnp.concatenate([s.astype(jnp.float32) for s in scores], axis=-1))
    cuts = [int(v) for v in np.cumsum(sizes)[:-1]]
    return jnp.split(p, cuts, axis=-1)

def to_blocks(t):
    lead = t.shape[:-2]
    L, d = t.shape[-2], t.shape[-1]
    t = t.reshape(lead + (L // Q_BLOCK, Q_BLOCK, d))
    return jnp.moveaxis(t, -3, 0)

def from_blocks(t):
    t = jnp.moveaxis(t, 0, -3)
    lead = t.shape[:-3]
    nb, qb, d = t.shape[-3], t.shape[-2], t.shape[-1]
    return t.reshape(lead + (nb * qb, d))

def merge_heads(o):
    B, H, N, d = o.shape
    return o.transpose(0, 2, 1, 3).reshape(B, N, H * d)

def pv(eq, p, v):
    return jnp.einsum(eq, p.astype(v.dtype), v)

def mla_mixer(hx, hc, w_down, q_norm, kv_norm, w_uq, w_ukv, w_o, cos, sin, ctx_out):
    H = MLA_HEADS
    scale = (MLA_NOPE + MLA_ROPE) ** -0.5

    def project(h):
        B, N, _ = h.shape
        d = h @ w_down
        cq = rms_norm_2(d[..., :MLA_Q_RANK], q_norm)
        ckv = rms_norm_2(d[..., MLA_Q_RANK:MLA_Q_RANK + MLA_KV_RANK], kv_norm)
        k_rope = d[..., MLA_Q_RANK + MLA_KV_RANK:]
        q = (cq @ w_uq).reshape(B, N, H, MLA_NOPE + MLA_ROPE).transpose(0, 2, 1, 3)
        kv = (ckv @ w_ukv).reshape(B, N, H, MLA_NOPE + MLA_V).transpose(0, 2, 1, 3)
        return q[..., :MLA_NOPE], q[..., MLA_NOPE:], kv[..., :MLA_NOPE], k_rope, kv[..., MLA_NOPE:]

    qn_x, qr_x, kn_x, kr_x, v_x = project(hx)
    qn_c, qr_c, kn_c, kr_c, v_c = project(hc)
    qr_x_rot = apply_rope(qr_x, cos, sin)
    kr_x_rot = apply_rope(kr_x, cos, sin)

    def scores(qn, qr, kn, kr):
        s = jnp.einsum('bhqd,bhkd->bhqk', qn, kn) + jnp.einsum('bhqr,bkr->bhqk', qr, kr)
        return s.astype(jnp.float32) * scale

    def block(args):
        qn, qr_rot, qr_pl = args
        p_x, p_c = joint_softmax(scores(qn, qr_rot, kn_x, kr_x_rot), scores(qn, qr_pl, kn_c, kr_c))
        return pv('bhqk,bhkd->bhqd', p_x, v_x) + pv('bhqk,bhkd->bhqd', p_c, v_c)

    o_x = from_blocks(lax.map(block, (to_blocks(qn_x), to_blocks(qr_x_rot), to_blocks(qr_x))))
    out_x = merge_heads(o_x) @ w_o
    out_c = None
    if ctx_out:
        p = softmax32(scores(qn_c, qr_c, kn_c, kr_c))
        out_c = merge_heads(pv('bhqk,bhkd->bhqd', p, v_c)) @ w_o
    return out_x, out_c

def swa_mixer(hx, hc, w_qkv, sink, w_o, cos, sin, ctx_out):
    Hk, G, Dh = SWA_KV_HEADS, SWA_GROUP, SWA_HEAD_DIM
    scale = Dh ** -0.5

    def project(h):
        B, N, _ = h.shape
        p = h @ w_qkv
        q = p[..., :Hk * G * Dh].reshape(B, N, Hk, G, Dh).transpose(0, 2, 3, 1, 4)
        k = p[..., Hk * G * Dh:(Hk * G + Hk) * Dh].reshape(B, N, Hk, Dh).transpose(0, 2, 1, 3)
        v = p[..., (Hk * G + Hk) * Dh:].reshape(B, N, Hk, Dh).transpose(0, 2, 1, 3)
        return q, k, v

    B, L, _ = hx.shape
    C = hc.shape[1]
    q_x, k_x, v_x = project(hx)
    q_c, k_c, v_c = project(hc)
    q_x_rot = apply_rope(q_x, cos, sin)
    k_x_rot = apply_rope(k_x, cos, sin)
    pad = ((0, 0), (0, 0), (SWA_WINDOW, SWA_WINDOW), (0, 0))
    k_pad = jnp.pad(k_x_rot, pad)
    v_pad = jnp.pad(v_x, pad)
    span = Q_BLOCK + 2 * SWA_WINDOW
    qi = jnp.arange(Q_BLOCK)
    kj = jnp.arange(span)
    sink_b = sink.reshape(Hk, G)[None, :, :, None, None].astype(jnp.float32)

    def ctx_scores(q):
        return jnp.einsum('bkgqd,bkcd->bkgqc', q, k_c).astype(jnp.float32) * scale

    def block(args):
        n, q_rot, q_pl = args
        start = n * Q_BLOCK
        k_b = lax.dynamic_slice_in_dim(k_pad, start, span, axis=2)
        v_b = lax.dynamic_slice_in_dim(v_pad, start, span, axis=2)
        qpos = start + qi
        kpos = start - SWA_WINDOW + kj
        valid = ((jnp.abs(kpos[None, :] - qpos[:, None]) <= SWA_WINDOW)
                 & (kpos[None, :] >= 0) & (kpos[None, :] < L))
        s_w = jnp.einsum('bkgqd,bkjd->bkgqj', q_rot, k_b).astype(jnp.float32) * scale
        s_w = jnp.where(valid, s_w, NEG_INF)
        s_c = ctx_scores(q_pl)
        s_s = jnp.broadcast_to(sink_b, s_c.shape[:-1] + (1,))
        p_w, p_c, _ = joint_softmax(s_w, s_c, s_s)
        return pv('bkgqj,bkjd->bkgqd', p_w, v_b) + pv('bkgqc,bkcd->bkgqd', p_c, v_c)

    nb = L // Q_BLOCK
    o = from_blocks(lax.map(block, (jnp.arange(nb), to_blocks(q_x_rot), to_blocks(q_x))))
    out_x = o.transpose(0, 3, 1, 2, 4).reshape(B, L, Hk * G * Dh) @ w_o
    out_c = None
    if ctx_out:
        s_c = ctx_scores(q_c)
        s_s = jnp.broadcast_to(sink_b, s_c.shape[:-1] + (1,))
        p_c, _ = joint_softmax(s_c, s_s)
        o_c = pv('bkgqc,bkcd->bkgqd', p_c, v_c)
        out_c = o_c.transpose(0, 3, 1, 2, 4).reshape(B, C, Hk * G * Dh) @ w_o
    return out_x, out_c

def na_mixer(hx, hc, w_qkv, rpb, w_o, ctx_out):
    H, Dh = NA_HEADS, NA_HEAD_DIM
    scale = Dh ** -0.5

    def project(h):
        B, N, _ = h.shape
        p = (h @ w_qkv).reshape(B, N, 3, H, Dh).transpose(2, 0, 3, 1, 4)
        return p[0], p[1], p[2]

    B, L, _ = hx.shape
    rows = L // GRID_W
    kh = min(NA_KH, rows)
    kw = NA_KW
    q_x, k_x, v_x = project(hx)
    q_c, k_c, v_c = project(hc)
    col = jnp.arange(GRID_W)
    col_start = jnp.clip(col - kw // 2, 0, GRID_W - kw)
    key_cols = col_start[:, None] + jnp.arange(kw)[None, :]
    col_off = key_cols - col[:, None] + (NA_KW - 1)

    def block(args):
        r, q_row = args
        row_start = jnp.clip(r - kh // 2, 0, rows - kh)
        key_rows = row_start + jnp.arange(kh)
        idx = (key_rows[None, :, None] * GRID_W + key_cols[:, None, :]).reshape(-1)
        k_g = jnp.take(k_x, idx, axis=2).reshape(B, H, GRID_W, kh * kw, Dh)
        v_g = jnp.take(v_x, idx, axis=2).reshape(B, H, GRID_W, kh * kw, Dh)
        row_off = key_rows - r + (NA_KH - 1)
        bias = rpb[:, row_off[None, :, None], col_off[:, None, :]]
        bias = bias.reshape(H, GRID_W, kh * kw).astype(jnp.float32)
        s_n = jnp.einsum('bhqd,bhqkd->bhqk', q_row, k_g).astype(jnp.float32) * scale + bias[None]
        s_c = jnp.einsum('bhqd,bhcd->bhqc', q_row, k_c).astype(jnp.float32) * scale
        p_n, p_c = joint_softmax(s_n, s_c)
        return pv('bhqk,bhqkd->bhqd', p_n, v_g) + pv('bhqc,bhcd->bhqd', p_c, v_c)

    q_rows = q_x.reshape(B, H, rows, GRID_W, Dh).transpose(2, 0, 1, 3, 4)
    o = lax.map(block, (jnp.arange(rows), q_rows))
    out_x = o.transpose(1, 0, 3, 2, 4).reshape(B, L, H * Dh) @ w_o
    out_c = None
    if ctx_out:
        p = softmax32(jnp.einsum('bhqd,bhcd->bhqc', q_c, k_c).astype(jnp.float32) * scale)
        out_c = merge_heads(pv('bhqc,bhcd->bhqd', p, v_c)) @ w_o
    return out_x, out_c

def diff_mixer(hx, hc, w_qkv, lam_params, norm_g, w_o, cos, sin, lam_init, ctx_out):
    H, Dh = DIFF_HEADS, DIFF_HEAD_DIM
    scale = Dh ** -0.5

    def project(h):
        B, N, _ = h.shape
        p = h @ w_qkv
        q = p[..., :H * 2 * Dh].reshape(B, N, H, 2, Dh).transpose(0, 2, 3, 1, 4)
        k = p[..., H * 2 * Dh:H * 4 * Dh].reshape(B, N, H, 2, Dh).transpose(0, 2, 3, 1, 4)
        v = p[..., H * 4 * Dh:].reshape(B, N, H, 2 * Dh).transpose(0, 2, 1, 3)
        return q, k, v

    q_x, k_x, v_x = project(hx)
    q_c, k_c, v_c = project(hc)
    q_x_rot = apply_rope(q_x, cos, sin)
    k_x_rot = apply_rope(k_x, cos, sin)
    lp = lam_params.astype(jnp.float32)
    lam = jnp.exp(jnp.sum(lp[0] * lp[1])) - jnp.exp(jnp.sum(lp[2] * lp[3])) + lam_init

    def scores(q, k):
        return jnp.einsum('bhiqd,bhikd->bhiqk', q, k).astype(jnp.float32) * scale

    def block(args):
        q_rot, q_pl = args
        p_x, p_c = joint_softmax(scores(q_rot, k_x_rot), scores(q_pl, k_c))
        a_x = p_x[:, :, 0] - lam * p_x[:, :, 1]
        a_c = p_c[:, :, 0] - lam * p_c[:, :, 1]
        return pv('bhqk,bhkd->bhqd', a_x, v_x) + pv('bhqk,bhkd->bhqd', a_c, v_c)

    def finish(o):
        return merge_heads(rms_norm_2(o, norm_g) * (1.0 - lam_init)) @ w_o

    o_x = from_blocks(lax.map(block, (to_blocks(q_x_rot), to_blocks(q_x))))
    out_x = finish(o_x)
    out_c = None
    if ctx_out:
        p = softmax32(scores(q_c, k_c))
        out_c = finish(pv('bhqk,bhkd->bhqd', p[:, :, 0] - lam * p[:, :, 1], v_c))
    return out_x, out_c

def second_inputs(seed: int = 0) -> dict:
    key = jax.random.key(seed)
    keys = jax.random.split(key, 32)
    counter = [0]

    def normal(shape, std):
        k = keys[counter[0]]
        counter[0] += 1
        return jax.random.normal(k, shape, jnp.float32) * std

    def gain(shape):
        return 1.0 + normal(shape, 0.02)

    nA, nB, nC, nD = [len(range(m, DEPTH, N_MIXERS)) for m in range(N_MIXERS)]
    D = D_MODEL
    return {
        'x': normal((BATCH, SEQ, D), 1.0),
        'c': normal((BATCH, D), 1.0),
        'ctx': normal((BATCH, CTX_LEN, D), 1.0),
        'c_ctx': normal((D,), 1.0),
        'mod_w': normal((DEPTH, D, N_MOD * D), 0.5 * D ** -0.5),
        'mod_b': normal((DEPTH, N_MOD * D), 0.02),
        'norm_g': gain((DEPTH, 3, D)),
        'final_norm_g': gain((D,)),
        'ffn_w_in': normal((DEPTH, 2, D, 2 * D_FF), D ** -0.5),
        'ffn_w_out': normal((DEPTH, 2, D_FF, D), D_FF ** -0.5),
        'mla_w_down': normal((nA, D, MLA_Q_RANK + MLA_KV_RANK + MLA_ROPE), D ** -0.5),
        'mla_q_norm': gain((nA, MLA_Q_RANK)),
        'mla_kv_norm': gain((nA, MLA_KV_RANK)),
        'mla_w_uq': normal((nA, MLA_Q_RANK, MLA_HEADS * (MLA_NOPE + MLA_ROPE)), MLA_Q_RANK ** -0.5),
        'mla_w_ukv': normal((nA, MLA_KV_RANK, MLA_HEADS * (MLA_NOPE + MLA_V)), MLA_KV_RANK ** -0.5),
        'mla_w_o': normal((nA, MLA_HEADS * MLA_V, D), (MLA_HEADS * MLA_V) ** -0.5),
        'swa_w_qkv': normal((nB, D, (SWA_Q_HEADS + 2 * SWA_KV_HEADS) * SWA_HEAD_DIM), D ** -0.5),
        'swa_sink': normal((nB, SWA_Q_HEADS), 0.5),
        'swa_w_o': normal((nB, SWA_Q_HEADS * SWA_HEAD_DIM, D), (SWA_Q_HEADS * SWA_HEAD_DIM) ** -0.5),
        'na_w_qkv': normal((nC, D, 3 * NA_HEADS * NA_HEAD_DIM), D ** -0.5),
        'na_rpb': normal((nC, NA_HEADS, 2 * NA_KH - 1, 2 * NA_KW - 1), 0.2),
        'na_w_o': normal((nC, NA_HEADS * NA_HEAD_DIM, D), (NA_HEADS * NA_HEAD_DIM) ** -0.5),
        'diff_w_qkv': normal((nD, D, 6 * DIFF_HEADS * DIFF_HEAD_DIM), D ** -0.5),
        'diff_lambda': normal((nD, 4, DIFF_HEAD_DIM), 0.1),
        'diff_norm_g': gain((nD, 2 * DIFF_HEAD_DIM)),
        'diff_w_o': normal((nD, 2 * DIFF_HEADS * DIFF_HEAD_DIM, D), (2 * DIFF_HEADS * DIFF_HEAD_DIM) ** -0.5),
    }

def second_block(x, c, ctx, c_ctx, mod_w, mod_b, norm_g, final_norm_g, ffn_w_in, ffn_w_out,
              mla_w_down, mla_q_norm, mla_kv_norm, mla_w_uq, mla_w_ukv, mla_w_o,
              swa_w_qkv, swa_sink, swa_w_o, na_w_qkv, na_rpb, na_w_o,
              diff_w_qkv, diff_lambda, diff_norm_g, diff_w_o):
    L = x.shape[1]
    cos, sin = axial_rope_tables(L, ROPE_DIM)
    xc = ctx
    cond_x = jax.nn.silu(c)
    cond_c = jax.nn.silu(c_ctx)
    for layer in range(DEPTH):
        kind = layer % N_MIXERS
        j = layer // N_MIXERS
        last = layer == DEPTH - 1
        mx = jnp.split((cond_x @ mod_w[layer] + mod_b[layer])[:, None, :], N_MOD, axis=-1)
        mc = jnp.split(cond_c @ mod_w[layer] + mod_b[layer], N_MOD, axis=-1)

        x = x + 0.5 * mx[2] * swiglu_2(modulate(rms_norm_2(x, norm_g[layer, 0]), mx[0], mx[1]),
                                     ffn_w_in[layer, 0], ffn_w_out[layer, 0])
        xc = xc + 0.5 * mc[2] * swiglu_2(modulate(rms_norm_2(xc, norm_g[layer, 0]), mc[0], mc[1]),
                                       ffn_w_in[layer, 0], ffn_w_out[layer, 0])

        hx = modulate(rms_norm_2(x, norm_g[layer, 1]), mx[3], mx[4])
        hc = modulate(rms_norm_2(xc, norm_g[layer, 1]), mc[3], mc[4])
        if kind == 0:
            ox, oc = mla_mixer(hx, hc, mla_w_down[j], mla_q_norm[j], mla_kv_norm[j], mla_w_uq[j],
                               mla_w_ukv[j], mla_w_o[j], cos, sin, not last)
        elif kind == 1:
            ox, oc = swa_mixer(hx, hc, swa_w_qkv[j], swa_sink[j], swa_w_o[j], cos, sin, not last)
        elif kind == 2:
            ox, oc = na_mixer(hx, hc, na_w_qkv[j], na_rpb[j], na_w_o[j], not last)
        else:
            lam_init = 0.8 - 0.6 * math.exp(-0.3 * layer)
            ox, oc = diff_mixer(hx, hc, diff_w_qkv[j], diff_lambda[j], diff_norm_g[j], diff_w_o[j],
                                cos, sin, lam_init, not last)
        x = x + mx[5] * ox

        x = x + 0.5 * mx[8] * swiglu_2(modulate(rms_norm_2(x, norm_g[layer, 2]), mx[6], mx[7]),
                                     ffn_w_in[layer, 1], ffn_w_out[layer, 1])
        if not last:
            xc = xc + mc[5] * oc
            xc = xc + 0.5 * mc[8] * swiglu_2(modulate(rms_norm_2(xc, norm_g[layer, 2]), mc[6], mc[7]),
                                           ffn_w_in[layer, 1], ffn_w_out[layer, 1])
    return rms_norm_2(x, final_norm_g)


def setup_inputs(seed=0):
    out = dict(first_inputs(seed))
    for name, value in second_inputs(seed + 1).items():
        if name != "x":
            out[name + "_2"] = value
    return out


def reference(
    x, positions, ln1, ln2, w_in, fox_bf, fox_qn, fox_kn, gla_w2, gla_b, gla_norm, ret_norm,
    ssd_conv_w, ssd_conv_b, ssd_dt_bias, ssd_a_log, ssd_d, ssd_norm, w_up_a, w_up_b, w_up_c,
    w_up_d, w_out, w_ffn_in, w_ffn_out, c_2, ctx_2, c_ctx_2, mod_w_2, mod_b_2, norm_g_2,
    final_norm_g_2, ffn_w_in_2, ffn_w_out_2, mla_w_down_2, mla_q_norm_2, mla_kv_norm_2,
    mla_w_uq_2, mla_w_ukv_2, mla_w_o_2, swa_w_qkv_2, swa_sink_2, swa_w_o_2, na_w_qkv_2,
    na_rpb_2, na_w_o_2, diff_w_qkv_2, diff_lambda_2, diff_norm_g_2, diff_w_o_2,
):
    x = first_block(
        x, positions, ln1, ln2, w_in, fox_bf, fox_qn, fox_kn, gla_w2, gla_b, gla_norm, ret_norm,
        ssd_conv_w, ssd_conv_b, ssd_dt_bias, ssd_a_log, ssd_d, ssd_norm, w_up_a, w_up_b, w_up_c,
        w_up_d, w_out, w_ffn_in, w_ffn_out,
    )
    return second_block(
        x, c_2, ctx_2, c_ctx_2, mod_w_2, mod_b_2, norm_g_2, final_norm_g_2, ffn_w_in_2,
        ffn_w_out_2, mla_w_down_2, mla_q_norm_2, mla_kv_norm_2, mla_w_uq_2, mla_w_ukv_2,
        mla_w_o_2, swa_w_qkv_2, swa_sink_2, swa_w_o_2, na_w_qkv_2, na_rpb_2, na_w_o_2,
        diff_w_qkv_2, diff_lambda_2, diff_norm_g_2, diff_w_o_2,
    )


_drawn_inputs = setup_inputs


def setup_inputs(seed=0):
    import zlib

    import numpy as np

    out = dict(_drawn_inputs(seed))
    spreads = {}
    factors = {'ln2': 3.012,
     'fox_qn': 8.0,
     'fox_kn': 8.0,
     'gla_b': 2.96,
     'gla_norm': 5.442,
     'ret_norm': 6.031,
     'ssd_conv_b': 6.034,
     'ssd_norm': 3.913,
     'ctx_2': 3.469,
     'mod_b_2': 4.761,
     'norm_g_2': 8.0,
     'final_norm_g_2': 2.799,
     'mla_q_norm_2': 8.0,
     'mla_kv_norm_2': 8.0,
     'mla_w_uq_2': 3.53,
     'swa_sink_2': 8.0}
    for name, (base, spread) in spreads.items():
        noise = np.random.default_rng([zlib.crc32(name.encode()), seed]).standard_normal(out[name].shape)
        drawn = base * np.exp(spread * noise) if base else spread * noise
        out[name] = jnp.asarray(drawn.astype(out[name].dtype))
    for name, factor in factors.items():
        out[name] = (out[name] * factor).astype(out[name].dtype)
    return out
```

```python
from contextlib import ExitStack, contextmanager

import numpy as np

import concourse.bass as bass
from concourse import mybir

F32 = mybir.dt.float32
I32 = mybir.dt.int32
ALU = mybir.AluOpType
ACT = mybir.ActivationFunctionType
AX_X = mybir.AxisListType.X

P = 128
D = 1024
KT = D // P
SEQ = 256
TT = SEQ // P
CTX = 256
BOTH = SEQ + CTX
DEPTH = 2
HD = 64
CHUNK = 64
NCHUNK = SEQ // CHUNK
HEADS = 4
SSD_HEADS = 8
FF = 2816
FT = FF // P
CONV = 4
XBC_T = 6
N_MOD = 9
MOD_T = N_MOD * KT
MOD_N = 512
MOD_G = N_MOD * D // MOD_N
MOD_Q = 4
MOD_B = -(-MOD_G // MOD_Q)
LOWRANK = 16
GLA_TAU = 16.0
MLA_H = 8
MLA_SCALE = float((128 + 64) ** -0.5)
SWA_SCALE = 0.125
CAUSAL = SEQ + P
NEG = -1e30

SLOTS = 4
SLOT = FT * P
RING = 6

C = {}
_at = 0
for _name, _w in (("ident", P), ("ones", P), ("heads64", P), ("mask_low", P), ("mask_up", P), ("chunk_up", P),
                  ("reset", SEQ), ("decay", HEADS * CAUSAL), ("cos2", SEQ), ("sin2", SEQ),
                  ("inv", 1), ("eps", 1), ("one", 1), ("half", 2), ("half8", 2), ("quarter", 4)):
    C[_name] = (_at, _at + _w)
    _at += _w
N_CONST = _at

PAR = {}
_at = 0
for _l in range(DEPTH):
    for _name, _w in (("ln1", KT), ("ln2", KT), ("fox_qn", 1), ("fox_kn", 1), ("gla_b", 2), ("gla_norm", 1),
                      ("ret_norm", 1), ("conv_w", XBC_T * CONV), ("conv_b", XBC_T), ("ssd_d", 4),
                      ("ssd_norm", 4), ("fox_bf", 1), ("dt_bias", 1), ("a_log", 1), ("gla_w2", 256)):
        PAR[_name, _l] = (_at, _at + _w)
        _at += _w
for _l in range(DEPTH):
    for _name, _w in (("mod_b", MOD_T), ("norm_g", 3 * KT)):
        PAR[_name, _l] = (_at, _at + _w)
        _at += _w
for _name, _w in (("final_g", KT), ("q_norm", 4), ("kv_norm", 2), ("sink", 16), ("cond", 2 * KT)):
    PAR[_name, 0] = (_at, _at + _w)
    _at += _w
N_PAR = _at


PROJ_LOTS = [("t", ("x0", "x1")), ("t", ("x2", "x3")), ("t", ("x4", "x5")), ("t", ("fq0", "fq1")), ("t", ("fk0", "fk1")),
             ("misc", None), ("v", "fv"), ("t", ("gq0", "gq1")), ("t", ("gk0", "gk1")), ("v", "gv"),
             ("t", ("rqa", "rqb")), ("t", ("rka", "rkb")), ("v", "rv"), ("t", ("gr0", "gr1")), ("t", ("rg0", "rg1")),
             ("t", ("z0", "z1")), ("t", ("z2", "z3"))]
PROJ_ACT = [(f"x{i}", i) for i in range(6)] + [("gr0", 0), ("gr1", 1), ("rg0", 2), ("rg1", 3)] + [(f"z{i}", 4 + i) for i in range(4)]
PROJ_DVE = [("fq0", "pj", 0), ("fq1", "pj", 1), ("fk0", "pj", 2), ("fk1", "pj", 3), ("ff", "", 0), ("glr", "", 0), ("dt", "", 0),
            ("fv", "v", 0), ("gq0", "pj", 4), ("gq1", "pj", 5), ("gk0", "pj", 6), ("gk1", "pj", 7), ("gv", "v", 1),
            ("rqa", "pj", 8), ("rqb", "pj", 9), ("rka", "pj", 10), ("rkb", "pj", 11), ("rv", "v", 2)]


class Plan:

    def __init__(self, old=None):
        self.old = old
        self.count, self.event, self.delta, self.size, self.alias, self.banks = {}, {}, {}, {}, {}, {}
        self.taken = set()
        self.loops = []

    def made(self, sem, key, inc=1):
        self.count[sem] = self.count.get(sem, 0) + inc
        assert (sem, key) not in self.event, (sem, key)
        self.event[sem, key] = (self.count[sem], [name for name, _, _ in self.loops])

    @contextmanager
    def loop(self, eng, name, n):
        before = dict(self.count)
        self.size[name] = n
        with eng.Fori(0, n) as i:
            self.loops.append((name, n, i))
            yield i
            self.loops.pop()
        for sem, now in list(self.count.items()):
            d = now - before.get(sem, 0)
            if d:
                self.delta[sem, name] = d
                self.count[sem] = before.get(sem, 0) + n * d

    def here(self, sem, v):
        for name, _, i in self.loops:
            d = self.old.delta.get((sem, name), 0) if self.old else 0
            if d:
                v = i * d + v
        return v

    def value(self, sem, key, **at):
        if self.old is None:
            return 1
        v, loops = self.old.event[sem, key]
        mine = {name: i for name, _, i in self.loops}
        for name in loops:
            i = at.get(name, mine.get(name, self.old.size[name] - 1))
            v = i * self.old.delta[sem, name] + v
        return v


def build(nc, old, x_in, ctx_in, pos_in, const_in, par_in, w_proj, w_gate, w_up, w_out, ffn_in1, ffn_out1,
          mod_w, ffn_in2, ffn_out2, w_down, w_uq, w_ukv, w_mla_o, w_qkv, w_swa_o, out):
    plan = Plan(old)
    with ExitStack() as ctx:
        sems = {}

        def sem(name):
            if name not in sems:
                sems[name] = ctx.enter_context(nc.semaphore(name))
            return sems[name]

        def mark(name, key, inc=1):
            plan.made(name, key, inc)
            return sem(name), inc

        def done(name, key, **at):
            if old is not None and (name, key) in old.alias:
                name, key = "free", old.alias[name, key]
            if name == "free":
                name = f"bank{bank_index.get(key, 0)}_free"
            return sem(name), plan.value(name, key, **at)

        steps = {}

        def link(eng, name, ins):
            steps[name] = steps.get(name, 0) + 1
            ins.then_inc(*mark(name, steps[name]))
            eng.wait_ge(*done(name, steps[name]))

        ring = {"n": 0}
        bank_index = old.banks if old else {}

        def bank_free(key):
            b = ring["n"] % RING
            ring["n"] += 1
            plan.banks[key] = b
            name = f"bank{b}_free"
            before = plan.here(name, plan.count.get(name, 0))
            plan.made(name, key)
            return sem(name), before

        def bank_of(key):
            return psum[:, bank_index.get(key, 0), :]

        def freed(key, name=None, event=None):
            assert key not in plan.taken, key
            plan.taken.add(key)
            if name:
                plan.alias[name, event] = key
            return sem(f"bank{bank_index.get(key, 0)}_free"), 1

        def sb(name, shape, dt=F32):
            t = ctx.enter_context(nc.sbuf_tensor(name, shape, dt))
            return t[(slice(None),) * len(shape)]

        psum = ctx.enter_context(nc.psum_tensor("psum", [P, 8, 512], F32))[:, :, :]
        wring = sb("wring", [P, SLOTS, SLOT])
        X = sb("X", [P, KT, BOTH])
        H = sb("H", [P, KT, BOTH])
        R = sb("R", [P, BOTH])
        const = sb("const", [P, N_CONST])
        par = sb("par", [P, N_PAR])
        MODS = sb("MODS", [P, DEPTH, MOD_T, 2])
        NAS = sb("NAS", [P, DEPTH, 3 * KT, 2])
        ROW = sb("ROW", [P, 2, MOD_N])

        def mod_rows(b):
            return 32 * min(MOD_Q, MOD_G - b * MOD_Q)
        COND = sb("COND", [P, KT, 32])
        COS = sb("COS", [P, SEQ])
        SIN = sb("SIN", [P, SEQ])
        XP = sb("XP", [P, XBC_T, SEQ + CONV - 1])
        ARENA = 24100
        arena = sb("arena", [P, ARENA])

        def cst(name, rows=P):
            a, b = C[name]
            return const[0:rows, a:b]

        def prm(name, l, rows=P):
            a, b = PAR[name, l]
            return par[0:rows, a:b]

        def col(name, l, k, rows=P):
            a, _ = PAR[name, l]
            return par[0:rows, a + k:a + k + 1]

        def carve(parts, start=0):
            views, at = {}, start
            for name, *shape in parts:
                size = int(np.prod(shape))
                v = arena[:, at:at + size]
                if len(shape) == 2:
                    v = v.rearrange("p (a b) -> p a b", a=shape[0])
                elif len(shape) == 3:
                    v = v.rearrange("p (a b c) -> p a b c", a=shape[0], b=shape[1])
                views[name] = v
                at += size
            assert at <= ARENA, at
            views["end"] = at
            return views

        m1 = carve([("ybr", 10, SEQ), ("PJ", 12, SEQ), ("SG", 8, SEQ), ("V", TT, 768),
                    ("CV", XBC_T, SEQ), ("XC", XBC_T, SEQ)])
        gates = carve([("GT", KT, 4, SEQ)], m1["end"])["GT"]
        YBR, PJ, SG, V, CV, XC = (m1[k] for k in ("ybr", "PJ", "SG", "V", "CV", "XC"))
        FQ, GQ, RQ = 0, 4, 8
        t1 = carve([("A0", 4, SEQ), ("QZ", 4, SEQ), ("KF", 2, SEQ), ("RF", 4, SEQ),
                    ("E", 8, SEQ), ("PT", 4, TT * SEQ)], m1["end"])
        small = carve([("FX", 1, SEQ), ("FA", 1, SEQ), ("CC", 1, SEQ), ("NCC", 1, SEQ), ("NM", 1, 16), ("RS", 1, 16),
                       ("RC", 1, 16), ("DTT", TT, SSD_HEADS), ("GLR", 1, SEQ)], m1["end"] + 8192)
        g1 = carve([("GX", 2, SEQ), ("GA", 2, SEQ), ("B", 2, SEQ), ("ND", 2, SEQ), ("EB", 2, SEQ), ("EI", 2, SEQ),
                    ("EK", 2, SEQ), ("QDZ", 4, SEQ), ("KEZ", 2, TT * SEQ), ("AT", TT * HEADS, P),
                    ("S", NCHUNK * 2, HD), ("OB", 2, SEQ), ("OQ", 2, SEQ)], m1["end"])
        r1 = carve([("TC", 2, SEQ), ("TS", 2, SEQ), ("Q", 2, SEQ), ("K", 2, SEQ), ("QZ", HEADS * 2, SEQ),
                    ("RT", HEADS, CAUSAL), ("OB", 2, SEQ), ("OQ", 2, SEQ)], m1["end"])
        d1 = carve([("XDT", TT, 512), ("CZ", 2, SEQ), ("CB", 2, CAUSAL),
                    ("L", SSD_HEADS, CAUSAL), ("OD", 4, SEQ), ("OQ", 4, SEQ)], m1["end"])
        d2 = carve([("DX", 1, SEQ), ("DA", 1, SEQ), ("DL", 1, SEQ), ("CS", 1, SEQ), ("NCS", 1, SEQ), ("AE", 1, 1)],
                   small["end"])
        ff = carve([("hidden", FT, BOTH), ("silu", 4, BOTH), ("sq", KT, BOTH)])
        HID, SILU, SQ = ff["hidden"], ff["silu"], ff["sq"]
        mg = carve([("tmp", 4, 512)], m1["end"] + 8192)["tmp"]
        b2 = carve([("QN", MLA_H, BOTH), ("QR", 4, BOTH), ("QX", 4, SEQ), ("KN", MLA_H, BOTH), ("KZ", 8, BOTH),
                    ("VM", 4, 1024), ("CQ", 6, BOTH), ("PTX", 4, SEQ), ("PTC", 2, SEQ), ("NM", 1, 8), ("RS", 1, 8), ("RC", 1, 8)])
        n = MLA_H * BOTH + 4 * BOTH + 4 * SEQ
        b2.update({k: v for k, v in carve([("SQ2", 6, BOTH)], n).items() if k != "end"})
        n += MLA_H * BOTH + 8 * BOTH
        b2.update({k: v for k, v in carve([("RM", 2, BOTH)], n).items() if k != "end"})
        n += 4 * 1024
        b2.update({k: v for k, v in carve([("PR", 2, 1536)], n).items() if k != "end"})

        def mla_pr(h, qt):
            a = qt * BOTH if qt < 2 else 2 * BOTH + (qt - 2) * CTX
            return b2["PR"][:, h % 2, a:a + (BOTH if qt < 2 else CTX)]
        b3 = carve([("QS", 8, SEQ), ("QX", 8, SEQ), ("KAB", 2, BOTH), ("KR", 2, BOTH), ("TMP", 4, SEQ), ("KZ", 8, BOTH),
                    ("VS", 4, SEQ), ("PR", 8, BOTH), ("PTX", 8, SEQ), ("NM", 1, 8), ("RS", 1, 8), ("ES", 1, 8)])
        FF_OUT = {("n2", 0): "ffo0", ("n2", 1): "ffo1", ("b0", 0): "ffo200", ("b0", 1): "ffo210",
                  ("b2", 0): "ffo201", ("b2", 1): "ffo211"}

        def flat(v):
            return v.rearrange("p a b -> p (a b)") if len(v.shape) == 3 else v

        def x_after(tag, n_lots=None):
            def at(k):
                if n_lots:
                    return done("x_ready", (tag, k // 2, k % 2))
                kk, i = lot_key(KT, k)
                return done("x_ready", (tag, kk), **{FF_OUT[tag]: i})
            return at

        def slot_blocks(s, k, c):
            return wring[:, s, 0:k * c].rearrange("p (k c) -> p k c", k=k)

        wpos = {"load": 0, "use": 0}

        held = {}

        def slot_free(s, **at):
            if s not in held:
                return None
            before, where = held[s]
            return done("filled", ("lot",) + before, **{**where, **at})

        def stream(sp, tag, src, n, size, loop=True):
            turns = n // SLOTS
            if turns < 2 or not loop:
                turns = 0
            for k in range(n if not turns else SLOTS):
                load(sp, tag, src[k], size, k if turns else ("rest", k), turns)
            if not turns:
                return
            with sp.Fori(1, turns) as i:
                for k in range(SLOTS):
                    s = wpos["load"] % SLOTS
                    wpos["load"] += 1
                    sp.wait_ge(*slot_free(s, **{tag: i - 1}))
                    sp.dma_start(wring[:, s, 0:size], src[i * SLOTS + k]).then_inc(sem(f"slot{s}_loaded"), 16)
                    plan.count[f"slot{s}_loaded"] += 16 * (turns - 1)
            for k in range(turns * SLOTS, n):
                load(sp, tag, src[k], size, ("rest", k), 0)

        def load(sp, tag, src, size, k, turns):
            s = wpos["load"] % SLOTS
            wpos["load"] += 1
            if s in held:
                sp.wait_ge(*slot_free(s))
            sp.dma_start(wring[:, s, 0:size], src).then_inc(*mark(f"slot{s}_loaded", (tag, k), 16))
            if turns:
                plan.event[f"slot{s}_loaded", (tag, k)][1].append(tag)
                plan.delta[f"slot{s}_loaded", tag] = 16
            held[s] = ((tag, k), {tag: turns - 1} if turns else {})

        def use_lot(pe, key):
            s = wpos["use"] % SLOTS
            wpos["use"] += 1
            pe.wait_ge(*done(f"slot{s}_loaded", key))
            return s

        def used_lot(ins, s, key):
            plan.event["filled", ("lot",) + key] = (plan.count["filled"], [name for name, _, _ in plan.loops])

        def lots(eng, tag, n, body):
            turns = n // SLOTS
            if turns > 1:
                with plan.loop(eng, tag, turns) as i:
                    for k in range(SLOTS):
                        body(i * SLOTS + k, k)
            else:
                turns = 0
            for k in range(turns * SLOTS, n):
                body(k, ("rest", k))

        def lot_key(n, j):
            turns = n // SLOTS
            if turns > 1 and j < turns * SLOTS:
                return j % SLOTS, j // SLOTS
            return ("rest", j), 0

        block = ctx.enter_context(nc.Block())

        @block.sync
        def _(sp):
            sp.dma_start(X[:, :, 0:SEQ], x_in).then_inc(*mark("x_loaded", 0, 16))
            sp.dma_start(const[:, :], const_in).then_inc(*mark("const_loaded", 0, 16))
            sp.dma_start(par[:, :], par_in).then_inc(*mark("par_loaded", 0, 16))
            sp.dma_start(COS.bitcast(I32), pos_in.to_broadcast([P, SEQ])).then_inc(*mark("pos_loaded", 0, 16))
            sp.dma_start(X[:, :, SEQ:BOTH], ctx_in).then_inc(*mark("ctx_loaded", 0, 16))

            for l in range(DEPTH):
                stream(sp, f"proj{l}", w_proj[l], len(PROJ_LOTS), 16 * P, loop=False)
                stream(sp, f"mod{l}", mod_w[l], 2 * MOD_G, KT // 2 * MOD_N, loop=False)
                stream(sp, f"gate{l}", w_gate[l], 16, 16 * P)
                stream(sp, f"up{l}", w_up[l], 4, 20 * P)
                stream(sp, f"wo{l}", w_out[l], 4, 16 * P)
                stream(sp, f"ffi{l}", ffn_in1[l], FT, 16 * P)
                stream(sp, f"ffo{l}", ffn_out1[l], KT, FT * P)
            for l in range(DEPTH):
                stream(sp, f"ffi2{l}0", ffn_in2[l][0], FT, 16 * P)
                stream(sp, f"ffo2{l}0", ffn_out2[l][0], KT, FT * P)
                if l == 0:
                    stream(sp, "down", w_down, 4, 16 * P)
                    stream(sp, "uq", w_uq, 3, 16 * P)
                    stream(sp, "ukv", w_ukv, 2, 16 * P)
                    stream(sp, "mlao", w_mla_o, 4, 16 * P)
                else:
                    stream(sp, "qkv", w_qkv, 6, 16 * P)
                    stream(sp, "swao", w_swa_o, 4, 16 * P)
                stream(sp, f"ffi2{l}1", ffn_in2[l][1], FT, 16 * P)
                stream(sp, f"ffo2{l}1", ffn_out2[l][1], KT, FT * P)
            sp.wait_ge(*done("result", KT - 1))
            sp.dma_start(out, H[:, :, 0:SEQ]).then_inc(*mark("stored", 0, 16))
            sp.wait_ge(*done("stored", 0))

        @block.gpsimd
        def _(pool):
            pool.memset(XP[:, :, 0:CONV - 1], 0.0).then_inc(*mark("conv_pad", 0))
            pool.memset(COND, 0.0).then_inc(*mark("cond_pad", 0))

        @block.tensor
        def _(pe):
            ident, ones, heads64 = cst("ident"), cst("ones"), cst("heads64")
            mm = pe.matmul

            def head_row(heads, h, n):
                return cst("ident", heads)[:, h:h + 1].to_broadcast([heads, n])

            def norm_sum(tag, n, tiles=KT):
                pe.wait_ge(*bank_free(("ss", tag)))
                bank = bank_of(("ss", tag))
                for k in range(tiles):
                    pe.wait_ge(*done("squares", (tag, k)))
                    last = mm(bank[:, 0:n], ones, SQ[:, k, 0:n], start=(k == 0), stop=(k == tiles - 1))
                last.then_inc(*mark("filled", ("ss", tag)))

            def dense(tag, n_lots, n, act, kt, keys):
                per = 16 // kt

                def lot(j, k):
                    s = use_lot(pe, (tag, k))
                    w = slot_blocks(s, 16, P)
                    for t in range(per):
                        key = (keys, k, t)
                        pe.wait_ge(*bank_free(key))
                        bank = bank_of(key)
                        for c in range(kt):
                            last = mm(bank[:, 0:n], w[:, t * kt + c, :], act(c), start=(c == 0), stop=(c == kt - 1))
                        last.then_inc(*mark("filled", key))
                    used_lot(last, s, (tag, k))
                lots(pe, tag, n_lots, lot)

            def ffn(tag_in, tag_out, tag, n):
                pe.wait_ge(*done("h_ready" if tag[0] == "n2" else "h_shifted", tag))

                def lot(j, k):
                    s = use_lot(pe, (tag_in, k))
                    w = slot_blocks(s, 16, P)
                    for part, t in (("u", 1), ("g", 0)):
                        key = (tag, part, k)
                        pe.wait_ge(*bank_free(key))
                        bank = bank_of(key)
                        for c in range(KT):
                            last = mm(bank[:, 0:n], w[:, t * KT + c, :], H[:, c, 0:n], start=(c == 0), stop=(c == KT - 1))
                        last.then_inc(*mark("filled", key))
                    used_lot(last, s, (tag_in, k))
                lots(pe, tag_in, FT, lot)

                pe.wait_ge(*done("hidden", (tag, lot_key(FT, FT - 1)[0])))

                def lot2(j, k):
                    s = use_lot(pe, (tag_out, k))
                    w = slot_blocks(s, FT, P)
                    key = (tag, "o", k)
                    pe.wait_ge(*bank_free(key))
                    bank = bank_of(key)
                    for c in range(FT):
                        last = mm(bank[:, 0:n], w[:, c, :], HID[:, c, 0:n], start=(c == 0), stop=(c == FT - 1))
                    last.then_inc(*mark("filled", key))
                    used_lot(last, s, (tag_out, k))
                lots(pe, tag_out, KT, lot2)

            def project(l):
                pe.wait_ge(*done("h_ready", ("n1", l)))
                tag = f"proj{l}"

                def hk(c):
                    return H[:, c, 0:SEQ]
                items = PROJ_LOTS

                def lot(kind, names, s):
                    if kind == "v":
                        w = slot_blocks(s, KT, SEQ)
                        key = ("p", l, names)
                        pe.wait_ge(*bank_free(key))
                        bank = bank_of(key)
                        for tt in range(TT):
                            for c in range(KT):
                                last = mm(bank[:, tt * SEQ:(tt + 1) * SEQ], H[:, c, tt * P:(tt + 1) * P], w[:, c, :],
                                          start=(c == 0), stop=(c == KT - 1))
                        last.then_inc(*mark("filled", key))
                        return last
                    w = slot_blocks(s, 16, P)
                    if kind == "misc":
                        for name, a, m in (("ff", 0, HEADS), ("glr", 32, LOWRANK), ("dt", 64, SSD_HEADS)):
                            key = ("p", l, name)
                            pe.wait_ge(*bank_free(key))
                            bank = bank_of(key)
                            for c in range(KT):
                                last = mm(bank[0:m, 0:SEQ], w[:, c, a:a + m], hk(c), start=(c == 0), stop=(c == KT - 1))
                            last.then_inc(*mark("filled", key))
                        return last
                    for t, name in enumerate(names):
                        key = ("p", l, name)
                        pe.wait_ge(*bank_free(key))
                        bank = bank_of(key)
                        for c in range(KT):
                            last = mm(bank[:, 0:SEQ], w[:, t * KT + c, :], hk(c), start=(c == 0), stop=(c == KT - 1))
                        last.then_inc(*mark("filled", key))
                    return last
                for j, (kind, names) in enumerate(items):
                    s = wpos["use"] % SLOTS
                    wpos["use"] += 1
                    pe.wait_ge(*done(f"slot{s}_loaded", (tag, ("rest", j))))
                    used_lot(lot(kind, names, s), s, (tag, ("rest", j)))

            def head_sums(key, src, wait, n=512):
                pe.wait_ge(*done(*wait))
                pe.wait_ge(*bank_free(key))
                bank = bank_of(key)
                mm(bank[:, 0:n], heads64, flat(src), start=True, stop=True).then_inc(*mark("filled", key))

            def fox_pe(l):
                mods_pe(1)
                for i in range(2):
                    head_sums(("ssf", l, i), t1["A0"][:, 2 * i:2 * i + 2, :], ("fox_sq", l))
                cs, ncs = small["CC"][0:HEADS, 0, :], small["NCC"][0:HEADS, 0, :]
                mods_pe(2)
                pe.wait_ge(*done("values", (l, 0)))
                pe.wait_ge(*done("fox_qk", l))
                pe.wait_ge(*done("fox_c", l))
                for h in range(HEADS):
                    for qt in range(TT):
                        nk, q = P * (qt + 1), slice(qt * P, qt * P + P)
                        pe.wait_ge(*bank_free(("fs", l, h, qt)))
                        bank = bank_of(("fs", l, h, qt))
                        mm(bank[:, 0:nk], t1["QZ"][:, h, q], t1["KF"][:, h // 2, 0:nk], start=True, stop=False)
                        mm(bank[:, 0:nk], cs[:, q], head_row(HEADS, h, nk), start=False, stop=False)
                        mm(bank[:, 0:nk], head_row(HEADS, h, P), ncs[:, 0:nk], start=False, stop=False)
                        mm(bank[:, qt * P:nk], ident, cst("mask_low"), start=False, stop=True).then_inc(*mark("filled", ("fs", l, h, qt)))
                mods_pe(1)
                for h in range(HEADS):
                    for qt in range(TT):
                        pe.wait_ge(*done("fox_p", (l, h, qt)))
                        pe.wait_ge(*bank_free(("ft", l, h, qt)))
                        bank = bank_of(("ft", l, h, qt))
                        for kt in range(qt + 1):
                            last = pe.transpose(bank[:, kt * P:kt * P + P],
                                                t1["E"][:, 2 * h + qt, kt * P:kt * P + P], ident)
                        last.then_inc(*mark("filled", ("ft", l, h, qt)))
                PT = t1["PT"].rearrange("p h (k q) -> p h k q", k=TT)
                for t in range(2):
                    pe.wait_ge(*bank_free(("fo", l, t)))
                    bank = bank_of(("fo", l, t))
                    for p in range(2):
                        h = 2 * t + p
                        pe.wait_ge(*done("fox_pt", (l, h, 1)))
                        v = slice(h * HD, h * HD + HD)
                        o = bank[p * HD:p * HD + HD, :]
                        mm(o[:, 0:P], V[:, 0, v], PT[:, h, 0, 0:P], start=True, stop=True)
                        mm(o[:, P:SEQ], V[:, 0, v], PT[:, h, 0, P:SEQ], start=True, stop=False)
                        last = mm(o[:, P:SEQ], V[:, 1, v], PT[:, h, 1, P:SEQ], start=False, stop=True)
                    last.then_inc(*mark("filled", ("fo", l, t)))

            def gla_pe(l):
                mods_pe(1)
                pe.wait_ge(*done("glr", l))
                pe.wait_ge(*bank_free(("la", l)))
                bank = bank_of(("la", l))
                w2 = prm("gla_w2", l, LOWRANK)
                for t in range(2):
                    last = mm(bank[:, t * SEQ:t * SEQ + SEQ], w2[:, t * P:t * P + P], small["GLR"][0:LOWRANK, 0, :],
                              start=True, stop=True)
                last.then_inc(*mark("filled", ("la", l)))
                mods_pe(3)
                mod_columns(l, 0)
                pe.wait_ge(*done("gla_ke", l))
                pe.wait_ge(*bank_free(("gkt", l)))
                bank = bank_of(("gkt", l))
                for tt in range(TT):
                    for t in range(2):
                        last = pe.transpose(bank[:, (2 * tt + t) * P:(2 * tt + t + 1) * P],
                                            g1["EK"][:, t, tt * P:tt * P + P], ident)
                last.then_inc(*mark("filled", ("gkt", l)))
                pe.wait_ge(*done("gla_qdz", l))
                for tt in range(TT):
                    pe.wait_ge(*bank_free(("ga", l, tt)))
                    bank = bank_of(("ga", l, tt))
                    for h in range(HEADS):
                        last = mm(bank[:, h * P:h * P + P], g1["EI"][:, h // 2, tt * P:tt * P + P],
                                  g1["QDZ"][:, h, tt * P:tt * P + P], start=True, stop=True)
                    last.then_inc(*mark("filled", ("ga", l, tt)))
                pe.wait_ge(*done("values", (l, 1)))
                pe.wait_ge(*done("gla_kez", l))
                pe.wait_ge(*bank_free(("gkv", l)))
                bank = bank_of(("gkv", l))
                KEZ = g1["KEZ"].rearrange("p c (t f) -> p c t f", t=TT)
                for c in range(NCHUNK - 1):
                    for h in range(HEADS):
                        p = HD * (h % 2)
                        last = mm(bank[p:p + HD, (2 * c + h // 2) * HD:(2 * c + h // 2 + 1) * HD],
                                  KEZ[:, c % 2, c // 2, h * HD:h * HD + HD], V[:, c // 2, SEQ + h * HD:SEQ + h * HD + HD],
                                  start=True, stop=True)
                last.then_inc(*mark("filled", ("gkv", l)))
                mods_pe(1)
                pe.wait_ge(*done("gla_at", (l, 1)))
                pe.wait_ge(*done("gla_s", (l, NCHUNK - 1)))
                for t in range(2):
                    pe.wait_ge(*bank_free(("go", l, t)))
                    bank = bank_of(("go", l, t))
                    for pp in range(2):
                        h = 2 * t + pp
                        o = bank[pp * HD:pp * HD + HD, :]
                        for tt in range(TT):
                            last = mm(o[:, tt * P:tt * P + P], V[:, tt, SEQ + h * HD:SEQ + h * HD + HD],
                                      g1["AT"][:, tt * HEADS + h, :], start=True, stop=False)
                            for c in (2 * tt, 2 * tt + 1):
                                if c:
                                    last = mm(o[:, c * CHUNK:c * CHUNK + CHUNK], g1["S"][:, 2 * c + t, :],
                                              g1["QDZ"][:, h, c * CHUNK:c * CHUNK + CHUNK], start=False, stop=c % 2 == 1)
                    last.then_inc(*mark("filled", ("go", l, t)))
                head_sums(("gss", l), g1["OQ"], ("gla_oq", l))

            def causal_out(key, val, w):
                for t in range(val[1]):
                    pe.wait_ge(*bank_free(key + (t,)))
                    bank = bank_of(key + (t,))
                    for pp in range(2):
                        h = 2 * t + pp
                        o = bank[pp * HD:pp * HD + HD, :]
                        pe.wait_ge(*done(w[1], key[1:] + (h,)))
                        mm(o[:, 0:SEQ], val[0](0, h), w[0][:, h, 0:SEQ], start=True, stop=False)
                        last = mm(o[:, P:SEQ], val[0](1, h), w[0][:, h, SEQ:CAUSAL], start=False, stop=True)
                    last.then_inc(*mark("filled", key + (t,)))

            def ret_pe(l):
                mods_pe(2)
                mod_columns(l, 1)
                pe.wait_ge(*done("values", (l, 2)))
                pe.wait_ge(*done("ret_qk", l))
                K, QZ = r1["K"], r1["QZ"]
                for h in range(HEADS):
                    pe.wait_ge(*bank_free(("rs", l, h)))
                    bank = bank_of(("rs", l, h))
                    for st in range(TT):
                        a, b = (0, SEQ) if st == 0 else (SEQ, CAUSAL)
                        for ab in range(2):
                            last = mm(bank[:, a:b], K[:, ab, st * P:st * P + P], QZ[:, 2 * h + ab, st * P:SEQ],
                                      start=(ab == 0), stop=(ab == 1))
                    last.then_inc(*mark("filled", ("rs", l, h)))
                mods_pe(1)
                causal_out(("ro", l), (lambda tt, h: V[:, tt, 512 + h * HD:512 + h * HD + HD], 2), (r1["RT"], "ret_w"))
                head_sums(("rss", l), r1["OQ"], ("ret_oq", l))

            def ssd_pe(l):
                CS, NCS = d2["CS"][0:SSD_HEADS, 0, :], d2["NCS"][0:SSD_HEADS, 0, :]
                mods_pe(2)
                mod_columns(l, 2)
                pe.wait_ge(*done("ssd_dt", l))
                pe.wait_ge(*bank_free(("dtt", l)))
                bank = bank_of(("dtt", l))
                for tt in range(TT):
                    last = pe.transpose(bank[:, tt * SSD_HEADS:(tt + 1) * SSD_HEADS],
                                        d2["DX"][0:SSD_HEADS, 0, tt * P:tt * P + P], ident[0:SSD_HEADS, 0:SSD_HEADS])
                last.then_inc(*mark("filled", ("dtt", l)))
                pe.wait_ge(*done("ssd_xc", l))
                for tt in range(TT):
                    pe.wait_ge(*bank_free(("xt", l, tt)))
                    bank = bank_of(("xt", l, tt))
                    for t in range(4):
                        last = pe.transpose(bank[:, t * P:t * P + P], XC[:, t, tt * P:tt * P + P], ident)
                    last.then_inc(*mark("filled", ("xt", l, tt)))
                mods_pe(1)
                pe.wait_ge(*done("ssd_cz", l))
                for g in range(2):
                    pe.wait_ge(*bank_free(("cb", l, g)))
                    bank = bank_of(("cb", l, g))
                    mm(bank[:, 0:SEQ], XC[:, 4, 0:P], d1["CZ"][:, g, :], start=True, stop=True)
                    last = mm(bank[:, SEQ:CAUSAL], XC[:, 4, P:SEQ], d1["CZ"][:, g, P:SEQ], start=True, stop=True)
                    last.then_inc(*mark("filled", ("cb", l, g)))
                pe.wait_ge(*done("ssd_cs", l))
                for h in range(SSD_HEADS):
                    pe.wait_ge(*bank_free(("sg", l, h)))
                    bank = bank_of(("sg", l, h))
                    for st in range(TT):
                        a, n = st * SEQ, SEQ - st * P
                        mm(bank[:, a:a + n], head_row(SSD_HEADS, h, P), CS[:, st * P:SEQ], start=True, stop=False)
                        mm(bank[:, a:a + n], NCS[:, st * P:st * P + P], head_row(SSD_HEADS, h, n), start=False, stop=False)
                        last = mm(bank[:, a:a + P], ident, cst("mask_up"), start=False, stop=True)
                    last.then_inc(*mark("filled", ("sg", l, h)))
                mods_pe(1)
                pe.wait_ge(*done("ssd_xdt", (l, 1)))
                causal_out(("yo", l), (lambda tt, h: d1["XDT"][:, tt, h * HD:h * HD + HD], 4), (d1["L"], "ssd_w"))
                mods_pe(2)
                pe.wait_ge(*done("ssd_oq", l))
                pe.wait_ge(*bank_free(("yss", l)))
                bank = bank_of(("yss", l))
                for g in range(2):
                    for t in range(2):
                        last = mm(bank[:, g * SEQ:g * SEQ + SEQ], ones, d1["OQ"][:, 2 * g + t, :], start=(t == 0), stop=(t == 1))
                last.then_inc(*mark("filled", ("yss", l)))

            def merge_pe(l):
                dense(f"gate{l}", 16, SEQ, lambda c: H[:, c, 0:SEQ], KT, ("gate", l))
                mod_columns(l, 3)
                mod_columns(l, 4)
                pe.wait_ge(*done("fox_y", (l, 1)))
                pe.wait_ge(*done("branches", (l, 9)))
                for u in range(4):
                    s = use_lot(pe, (f"up{l}", ("rest", u)))
                    w = slot_blocks(s, 20, P)
                    for mi in range(2):
                        m = 2 * u + mi
                        for half, parts in enumerate((((0, 2), (2, 4)), ((4, 6), (6, 10)))):
                            key = ("up", l, m, half)
                            pe.wait_ge(*bank_free(key))
                            bank = bank_of(key)
                            for q, (a, b) in enumerate(parts):
                                for c in range(a, b):
                                    last = mm(bank[:, q * SEQ:q * SEQ + SEQ], w[:, 10 * mi + c, :], YBR[:, c, :],
                                              start=(c == a), stop=(c == b - 1))
                            last.then_inc(*mark("filled", key))
                    used_lot(last, s, (f"up{l}", ("rest", u)))
                pe.wait_ge(*done("merged", (l, KT - 1)))
                dense(f"wo{l}", 4, SEQ, lambda c: H[:, c, 0:SEQ], KT, ("wo", l))

            turn = {"l": 0, "g": 0}

            def mods_pe(n):
                l = turn["l"]
                for g in range(turn["g"], min(turn["g"] + n, MOD_G)):
                    if (l, g) == (0, 0):
                        pe.wait_ge(*done("cond", 0))
                    i, q = l * MOD_B + g // MOD_Q, g % MOD_Q
                    if q == 0 and i >= 2:
                        pe.wait_ge(*done("mod_row", i - 2))
                    for part in range(2):
                        s = use_lot(pe, (f"mod{l}", ("rest", 2 * g + part)))
                        w = slot_blocks(s, KT // 2, MOD_N)
                        for c in range(KT // 2):
                            k = part * KT // 2 + c
                            last = mm(psum[32 * q:32 * q + 32, RING + i % 2, :], COND[:, k, :], w[:, c, :],
                                      start=(k == 0), stop=(k == KT - 1))
                        last.then_inc(*mark("filled", ("mod_part", l, g) if part == 0 else ("mg", l, g)))
                        used_lot(last, s, (f"mod{l}", ("rest", 2 * g + part)))
                    turn["g"] = g + 1

            def mod_columns(l, b):
                i = l * MOD_B + b
                pe.wait_ge(*done("mod_row", i))
                pe.wait_ge(*bank_free(("mc", i)))
                bank, m = bank_of(("mc", i)), mod_rows(b)
                for t in range(MOD_N // P):
                    last = pe.transpose(bank[:, t * P:t * P + m], ROW[0:m, i % 2, t * P:(t + 1) * P], ident[0:m, 0:m])
                last.then_inc(*mark("filled", ("mc", i)))

            def mods_end():
                mods_pe(MOD_G)
                turn.update(l=turn["l"] + 1, g=0)

            def mla_pe():
                pe.wait_ge(*done("h_shifted", ("b1", 0)))
                dense("down", 4, BOTH, lambda c: H[:, c, :], KT, "down")
                pe.wait_ge(*done("mla_sq", 5))
                for part, (a, b) in enumerate(((0, 4), (4, 6))):
                    pe.wait_ge(*bank_free(("mss", part)))
                    bank = bank_of(("mss", part))
                    for k in range(a, b):
                        last = mm(bank, ones, b2["SQ2"][:, k, :], start=(k == a), stop=(k == b - 1))
                    last.then_inc(*mark("filled", ("mss", part)))
                pe.wait_ge(*done("mla_c", 5))
                dense("uq", 3, BOTH, lambda c: b2["CQ"][:, c, :], 4, "uq")
                s = use_lot(pe, ("ukv", ("rest", 0)))
                w = slot_blocks(s, 16, P)
                for h in range(MLA_H):
                    pe.wait_ge(*bank_free(("kn", h)))
                    bank = bank_of(("kn", h))
                    for c in range(2):
                        last = mm(bank, w[:, 2 * h + c, :], b2["CQ"][:, 4 + c, :], start=(c == 0), stop=(c == 1))
                    last.then_inc(*mark("filled", ("kn", h)))
                used_lot(last, s, ("ukv", ("rest", 0)))
                s = use_lot(pe, ("ukv", ("rest", 1)))
                w = slot_blocks(s, 2, 1024)
                for kt in range(4):
                    for half in range(2):
                        pe.wait_ge(*bank_free(("mv", kt, half)))
                        bank = bank_of(("mv", kt, half))
                        for c in range(2):
                            last = mm(bank, b2["CQ"][:, 4 + c, kt * P:kt * P + P], w[:, c, half * 512:half * 512 + 512],
                                      start=(c == 0), stop=(c == 1))
                        last.then_inc(*mark("filled", ("mv", kt, half)))
                used_lot(last, s, ("ukv", ("rest", 1)))
                pe.wait_ge(*done("mla_kz", 3))
                pe.wait_ge(*done("mla_qx", 1))
                pe.wait_ge(*done("mla_v", (3, 1)))
                pe.wait_ge(*done("mla_kn", 7))

                def scores(h):
                    for qt in range(2):
                        q = slice(qt * P, qt * P + P)
                        pe.wait_ge(*bank_free(("ms", h, qt)))
                        bank = bank_of(("ms", h, qt))
                        mm(bank, b2["QN"][:, h, q], b2["KN"][:, h, :], start=True, stop=False)
                        for ab in range(2):
                            kz = b2["KZ"][:, 2 * (h % 4) + ab, :]
                            mm(bank[:, 0:SEQ], b2["QX"][:, 2 * (h // 4) + ab, q], kz[:, 0:SEQ], start=False, stop=False)
                            last = mm(bank[:, SEQ:BOTH], b2["QR"][:, 2 * (h // 4) + ab, q], kz[:, SEQ:BOTH],
                                      start=False, stop=(ab == 1))
                        last.then_inc(*mark("filled", ("ms", h, qt)))
                    for qt in range(2):
                        q = slice(SEQ + qt * P, SEQ + qt * P + P)
                        pe.wait_ge(*bank_free(("ms", h, 2 + qt)))
                        bank = bank_of(("ms", h, 2 + qt))
                        mm(bank[:, 0:CTX], b2["QN"][:, h, q], b2["KN"][:, h, SEQ:BOTH], start=True, stop=False)
                        for ab in range(2):
                            last = mm(bank[:, 0:CTX], b2["QR"][:, 2 * (h // 4) + ab, q],
                                      b2["KZ"][:, 2 * (h % 4) + ab, SEQ:BOTH], start=False, stop=(ab == 1))
                        last.then_inc(*mark("filled", ("ms", h, 2 + qt)))

                def attend(h):
                    for qt in range(4):
                        nk = 4 if qt < 2 else 2
                        pe.wait_ge(*done("mla_p", (h, qt)))
                        pe.wait_ge(*bank_free(("mt", h, qt)))
                        bank = bank_of(("mt", h, qt))
                        for kt in range(nk):
                            last = pe.transpose(bank[:, kt * P:kt * P + P], mla_pr(h, qt)[:, kt * P:kt * P + P], ident)
                        last.then_inc(*mark("filled", ("mt", h, qt)))
                    pe.wait_ge(*done("mla_pt", (h, 3)))
                    pe.wait_ge(*bank_free(("mo", h)))
                    bank = bank_of(("mo", h))
                    for kt in range(4):
                        mm(bank[:, 0:SEQ], b2["VM"][:, kt, h * P:h * P + P], b2["PTX"][:, kt, :], start=(kt == 0), stop=(kt == 3))
                    for kt in range(2):
                        last = mm(bank[:, SEQ:BOTH], b2["VM"][:, 2 + kt, h * P:h * P + P], b2["PTC"][:, kt, :],
                                  start=(kt == 0), stop=(kt == 1))
                    last.then_inc(*mark("filled", ("mo", h)))
                scores(0)
                for h in range(MLA_H):
                    if h + 1 < MLA_H:
                        scores(h + 1)
                    attend(h)
                pe.wait_ge(*done("mla_o", MLA_H - 1))
                dense("mlao", 4, BOTH, lambda c: H[:, c, :], KT, "mlao")

            def swa_pe():
                pe.wait_ge(*done("h_shifted", ("b1", 1)))
                for j in range(6):
                    key = ("qkv", lot_key(6, j)[0])
                    s = use_lot(pe, key)
                    if j < 5:
                        w = slot_blocks(s, 16, P)
                        n = SEQ if j < 4 else BOTH
                        for t in range(2):
                            pe.wait_ge(*bank_free(("sq", j, t)))
                            bank = bank_of(("sq", j, t))
                            for c in range(KT):
                                last = mm(bank[:, 0:n], w[:, t * KT + c, :], H[:, c, 0:n], start=(c == 0), stop=(c == KT - 1))
                            last.then_inc(*mark("filled", ("sq", j, t)))
                    else:
                        w = slot_blocks(s, KT, 256)
                        for kt in range(4):
                            pe.wait_ge(*bank_free(("sv", kt)))
                            bank = bank_of(("sv", kt))
                            for c in range(KT):
                                last = mm(bank[:, 0:256], H[:, c, kt * P:kt * P + P], w[:, c, :], start=(c == 0), stop=(c == KT - 1))
                            last.then_inc(*mark("filled", ("sv", kt)))
                    used_lot(last, s, key)
                pe.wait_ge(*done("swa_kz", 3))
                pe.wait_ge(*done("swa_qx", 3))
                pe.wait_ge(*done("swa_v", 3))

                def scores(h):
                    j, g = h // 4, h % 4
                    for qt in range(2):
                        q = slice(qt * P, qt * P + P)
                        pe.wait_ge(*bank_free(("ws", h, qt)))
                        bank = bank_of(("ws", h, qt))
                        for ab in range(2):
                            mm(bank[:, 0:SEQ], b3["QX"][:, 2 * g + ab, q], b3["KZ"][:, 2 * j + ab, 0:SEQ],
                               start=(ab == 0), stop=False)
                        if qt == 0:
                            mm(bank[:, P:SEQ], ident, cst("mask_low"), start=False, stop=True)
                        else:
                            mm(bank[:, 0:P], ident, cst("mask_up"), start=False, stop=True)
                        for ab in range(2):
                            last = mm(bank[:, SEQ:BOTH], b3["QS"][:, 2 * g + ab, q], b3["KZ"][:, 2 * j + ab, SEQ:BOTH],
                                      start=(ab == 0), stop=(ab == 1))
                        last.then_inc(*mark("filled", ("ws", h, qt)))

                def attend(t):
                    for h in (2 * t, 2 * t + 1):
                        for qt in range(2):
                            pe.wait_ge(*done("swa_p", (h, qt)))
                            pe.wait_ge(*bank_free(("wt", h, qt)))
                            bank = bank_of(("wt", h, qt))
                            for kt in range(4):
                                last = pe.transpose(bank[:, kt * P:kt * P + P], b3["PR"][:, 2 * (h % 4) + qt, kt * P:kt * P + P], ident)
                            last.then_inc(*mark("filled", ("wt", h, qt)))
                    pe.wait_ge(*bank_free(("wo2", t)))
                    bank = bank_of(("wo2", t))
                    for h in (2 * t, 2 * t + 1):
                        pe.wait_ge(*done("swa_pt", (h, 1)))
                        o = bank[HD * (h % 2):HD * (h % 2) + HD, 0:SEQ]
                        v = slice((h // 4) * HD, (h // 4) * HD + HD)
                        for kt in range(4):
                            last = mm(o, b3["VS"][:, kt, v], b3["PTX"][:, 4 * (h % 2) + kt, :], start=(kt == 0), stop=(kt == 3))
                    last.then_inc(*mark("filled", ("wo2", t)))
                for t in range(8 + 1):
                    if t < 8:
                        scores(2 * t)
                        scores(2 * t + 1)
                    if t:
                        attend(t - 1)
                pe.wait_ge(*done("swa_o", 7))
                dense("swao", 4, SEQ, lambda c: H[:, c, 0:SEQ], KT, "swao")

            pe.wait_ge(*done("const_loaded", 0))
            pe.wait_ge(*done("par_loaded", 0))
            for l in range(DEPTH):
                norm_sum(("n1", l), SEQ)
                project(l)
                fox_pe(l)
                gla_pe(l)
                ret_pe(l)
                ssd_pe(l)
                mods_end()
                merge_pe(l)
                norm_sum(("n2", l), SEQ)
                ffn(f"ffi{l}", f"ffo{l}", ("n2", l), SEQ)
            for l in range(DEPTH):
                norm_sum(("b0", l), BOTH)
                ffn(f"ffi2{l}0", f"ffo2{l}0", ("b0", l), BOTH)
                norm_sum(("b1", l), BOTH)
                (mla_pe, swa_pe)[l]()
                n = BOTH if l == 0 else SEQ
                norm_sum(("b2", l), n)
                ffn(f"ffi2{l}1", f"ffo2{l}1", ("b2", l), n)
            norm_sum("final", SEQ)

        @block.scalar
        def _(act):
            A = act.activation
            one, eps = cst("one"), cst("eps")

            def squares(tag, n, wait):
                for k in range(KT):
                    act.wait_ge(*wait(k))
                    A(SQ[:, k, 0:n], X[:, k, 0:n], ACT.Square).then_inc(*mark("squares", (tag, k)))

            def rsqrt(out_, bank_key, n, count, name, key):
                act.wait_ge(*done("filled", bank_key))
                bank = bank_of(bank_key)
                out_ = flat(out_)
                A(out_, bank[:, 0:n], ACT.Ln, bias=eps, scale=1.0 / count).then_inc(*freed(bank_key))
                act.wait_ge(*done("free", bank_key))
                A(out_, out_, ACT.Exp, scale=-0.5).then_inc(*mark(name, key))

            def ffn(tag_in, tag, n):
                def lot(j, k):
                    act.wait_ge(*done("filled", (tag, "g", k)))
                    bank = bank_of((tag, "g", k))
                    slot = k if isinstance(k, int) else k[1] % 4
                    ins = A(SILU[:, slot, 0:n], bank[:, 0:n], ACT.Silu)
                    ins.then_inc(*freed((tag, "g", k), "silu", (tag, k)))
                lots(act, tag_in, FT, lot)

            def project(l):
                for name, dst in PROJ_ACT:
                    key = ("p", l, name)
                    act.wait_ge(*done("filled", key))
                    bank = bank_of(key)
                    if name[0] == "x":
                        if l == 0:
                            act.wait_ge(*done("conv_pad", 0))
                        A(XP[:, dst, CONV - 1:], bank[:, 0:SEQ], ACT.Copy).then_inc(*freed(key, "xbc", (l, dst)))
                    else:
                        A(SG[:, dst, :], bank[:, 0:SEQ], ACT.Silu).then_inc(*freed(key, "silu_gate", (l, dst)))
                act.wait_ge(*done("conv", (l, XBC_T - 1)))
                A(XC, CV, ACT.Silu).then_inc(*mark("ssd_xc", l))

            def softplus_parts(ax, src, name, key, wait):
                act.wait_ge(*done(*wait))
                link(act, "act_step", A(ax, src, ACT.Abs))
                link(act, "act_step", A(ax, ax, ACT.Exp, scale=-1.0))
                A(ax, ax, ACT.Ln, bias=cst("one", ax.shape[0]), scale=1.0).then_inc(*mark(name, key))

            def fox_act(l):
                act.wait_ge(*done("fox_pj", (l, 3)))
                A(t1["A0"], PJ[:, FQ:FQ + 4, :], ACT.Square).then_inc(*mark("fox_sq", l))
                for i in range(2):
                    rsqrt(t1["RF"][:, 2 * i:2 * i + 2, :], ("ssf", l, i), 512, HD, "fox_r", (l, i))
                softplus_parts(small["FA"][0:HEADS, 0, :], small["FX"][0:HEADS, 0, :], "fox_ln", l, ("fox_fx", l))
                for h in range(HEADS):
                    for qt in range(TT):
                        i, nk = 2 * h + qt, P * (qt + 1)
                        act.wait_ge(*done("fox_nm", (l, h, qt)))
                        act.wait_ge(*done("filled", ("fs", l, h, qt)))
                        bank = bank_of(("fs", l, h, qt))
                        ins = A(t1["E"][:, i, 0:nk], bank[:, 0:nk], ACT.Exp, bias=small["NM"][:, 0, i:i + 1], scale=1.0,
                                accum_out=small["RS"][:, 0, i:i + 1])
                        ins.then_inc(*freed(("fs", l, h, qt), "fox_e", (l, h, qt)))
                for h in range(HEADS):
                    for qt in range(TT):
                        key = ("ft", l, h, qt)
                        act.wait_ge(*done("filled", key))
                        bank = bank_of(key)
                        PT = t1["PT"].rearrange("p h (k q) -> p h k q", k=TT)
                        src = bank[:, 0:P * (qt + 1)].rearrange("p (k q) -> p k q", k=qt + 1)
                        A(PT[:, h, 0:qt + 1, qt * P:qt * P + P], src, ACT.Copy).then_inc(*freed(key, "fox_pt", (l, h, qt)))
                for t in range(2):
                    act.wait_ge(*done("filled", ("fo", l, t)))
                    bank = bank_of(("fo", l, t))
                    A(YBR[:, t, :], bank[:, 0:SEQ], ACT.Copy).then_inc(*freed(("fo", l, t), "fox_y", (l, t)))

            def gla_act(l):
                softplus_parts(g1["GA"], g1["GX"], "gla_ln", l, ("gla_gx", l))
                act.wait_ge(*done("gla_b", l))
                A(g1["EB"], g1["B"], ACT.Exp, scale=1.0 / GLA_TAU).then_inc(*mark("gla_e", (l, 0)))
                A(g1["EI"], g1["B"], ACT.Exp, scale=-1.0 / GLA_TAU).then_inc(*mark("gla_e", (l, 1)))
                act.wait_ge(*done("gla_nd", l))
                A(g1["EK"], g1["ND"], ACT.Exp, scale=1.0 / GLA_TAU).then_inc(*mark("gla_e", (l, 2)))
                head_norm_act(l, "go", "gss", g1, "gla")

            def head_norm_act(l, okey, skey, buf, name):
                for t in range(2):
                    act.wait_ge(*done("filled", (okey, l, t)))
                    bank = bank_of((okey, l, t))
                    A(buf["OB"][:, t, :], bank[:, 0:SEQ], ACT.Copy).then_inc(*freed((okey, l, t)))
                    act.wait_ge(*done("free", (okey, l, t)))
                A(buf["OQ"], buf["OB"], ACT.Square).then_inc(*mark(f"{name}_oq", l))
                rsqrt(buf["OQ"], (skey, l), 512, HD, f"{name}_r", l)

            def ssd_act(l):
                DL = d2["DL"][0:SSD_HEADS, 0, :]
                softplus_parts(DL, d2["DX"][0:SSD_HEADS, 0, :], "ssd_ln", l, ("ssd_dx", l))
                A(d2["AE"][0:SSD_HEADS, 0, :], col("a_log", l, 0, SSD_HEADS), ACT.Exp).then_inc(*mark("ssd_ae", l))
                for g in range(2):
                    act.wait_ge(*done("filled", ("cb", l, g)))
                    bank = bank_of(("cb", l, g))
                    A(d1["CB"][:, g, :], bank[:, 0:CAUSAL], ACT.Copy).then_inc(*freed(("cb", l, g), "ssd_cb", (l, g)))
                for h in range(SSD_HEADS):
                    act.wait_ge(*done("filled", ("sg", l, h)))
                    bank = bank_of(("sg", l, h))
                    A(d1["L"][:, h, :], bank[:, 0:CAUSAL], ACT.Exp).then_inc(*freed(("sg", l, h), "ssd_l", (l, h)))
                act.wait_ge(*done("ssd_od", (l, 3)))
                A(d1["OQ"], d1["OD"], ACT.Square).then_inc(*mark("ssd_oq", l))
                rsqrt(d1["OQ"][:, 0:2, :], ("yss", l), 512, 256, "ssd_r", l)

            def merge_act(l):
                act.wait_ge(*done("branches", (l, 9)))
                tag = f"gate{l}"

                def lot(j, k):
                    for t in range(2):
                        key = (("gate", l), k, t)
                        act.wait_ge(*done("filled", key))
                        bank = bank_of(key)
                        q = (2 * k + t) % 4
                        m = plan.loops[-1][2] * 2 + (2 * k + t) // 4
                        A(gates[:, m, q, :], bank[:, 0:SEQ], ACT.Sigmoid).then_inc(*freed(key, "gate", (l, k, t)))
                lots(act, tag, 16, lot)

            def mod_row_act(l, b):
                i, m = l * MOD_B + b, mod_rows(b)
                act.wait_ge(*done("filled", ("mg", l, b * MOD_Q + m // 32 - 1)))
                if i >= 2:
                    act.wait_ge(*done("filled", ("mc", i - 2)))
                A(ROW[0:m, i % 2, :], psum[0:m, RING + i % 2, :], ACT.Copy).then_inc(*mark("mod_row", i))

            def mla_act():
                for t in range(8):
                    key = ("down", ("rest", t // 2), t % 2)
                    act.wait_ge(*done("filled", key))
                    bank = bank_of(key)
                    dst = b2["CQ"][:, t, :] if t < 6 else b2["QX"][:, 2 * (t - 6):2 * (t - 6) + 2, :]
                    src = bank if t < 6 else bank.rearrange("p (a b) -> p a b", a=2)
                    A(dst, src, ACT.Copy).then_inc(*freed(key, "mla_down", t))
                    if t < 6:
                        act.wait_ge(*done("free", key))
                        A(b2["SQ2"][:, t, :], b2["CQ"][:, t, :], ACT.Square).then_inc(*mark("mla_sq", t))
                for part, count in ((0, 512), (1, 256)):
                    rsqrt(b2["RM"][:, part, :], ("mss", part), 512, count, "mla_r", part)
                for t in range(12):
                    key = ("uq", ("rest", t // 4), t % 4)
                    act.wait_ge(*done("filled", key))
                    bank = bank_of(key)
                    if t < 8:
                        A(b2["QN"][:, t, :], bank, ACT.Copy).then_inc(*freed(key, "mla_qn", t))
                    else:
                        A(b2["QR"][:, t - 8, :], bank, ACT.Copy).then_inc(*freed(key, "mla_qr", t - 8))
                for h in range(MLA_H):
                    act.wait_ge(*done("filled", ("kn", h)))
                    bank = bank_of(("kn", h))
                    A(b2["KN"][:, h, :], bank, ACT.Copy).then_inc(*freed(("kn", h), "mla_kn", h))
                for kt in range(4):
                    for half in range(2):
                        act.wait_ge(*done("filled", ("mv", kt, half)))
                        bank = bank_of(("mv", kt, half))
                        A(b2["VM"][:, kt, half * 512:half * 512 + 512], bank, ACT.Copy).then_inc(*freed(("mv", kt, half), "mla_v", (kt, half)))
                def exps(h):
                    for qt in range(4):
                        nk = BOTH if qt < 2 else CTX
                        act.wait_ge(*done("mla_nm", (h, qt)))
                        act.wait_ge(*done("filled", ("ms", h, qt)))
                        bank = bank_of(("ms", h, qt))
                        i = 4 * (h % 2) + qt
                        ins = A(mla_pr(h, qt), bank[:, 0:nk], ACT.Exp, bias=b2["NM"][:, 0, i:i + 1],
                                scale=MLA_SCALE, accum_out=b2["RS"][:, 0, i:i + 1])
                        ins.then_inc(*freed(("ms", h, qt), "mla_e", (h, qt)))
                exps(0)
                for h in range(MLA_H):
                    if h + 1 < MLA_H:
                        exps(h + 1)
                    for qt in range(4):
                        key = ("mt", h, qt)
                        act.wait_ge(*done("filled", key))
                        bank = bank_of(key)
                        nk = 4 if qt < 2 else 2
                        dst = b2["PTX" if qt < 2 else "PTC"][:, :, (qt % 2) * P:(qt % 2) * P + P]
                        A(dst, bank[:, 0:nk * P].rearrange("p (k q) -> p k q", k=nk), ACT.Copy).then_inc(*freed(key, "mla_pt", (h, qt)))
                    act.wait_ge(*done("filled", ("mo", h)))
                    bank = bank_of(("mo", h))
                    A(H[:, h, :], bank, ACT.Copy).then_inc(*freed(("mo", h), "mla_o", h))

            def swa_act():
                for t in range(8):
                    act.wait_ge(*done("filled", ("sq", t // 2, t % 2)))
                    bank = bank_of(("sq", t // 2, t % 2))
                    A(b3["QS"][:, t, :], bank[:, 0:SEQ], ACT.Copy).then_inc(*freed(("sq", t // 2, t % 2), "swa_qs", t))
                for t in range(2):
                    act.wait_ge(*done("filled", ("sq", 4, t)))
                    bank = bank_of(("sq", 4, t))
                    A(b3["KAB"][:, t, :], bank, ACT.Copy).then_inc(*freed(("sq", 4, t), "swa_kab", t))
                for kt in range(4):
                    act.wait_ge(*done("filled", ("sv", kt)))
                    bank = bank_of(("sv", kt))
                    A(b3["VS"][:, kt, :], bank[:, 0:256], ACT.Copy).then_inc(*freed(("sv", kt), "swa_v", kt))
                def exps(t):
                    for h in (2 * t, 2 * t + 1):
                        for qt in range(2):
                            i = 2 * (h % 4) + qt
                            act.wait_ge(*done("swa_nm", (h, qt)))
                            act.wait_ge(*done("filled", ("ws", h, qt)))
                            bank = bank_of(("ws", h, qt))
                            A(b3["PR"][:, i, :], bank, ACT.Exp, bias=b3["NM"][:, 0, i:i + 1],
                                        scale=SWA_SCALE, accum_out=b3["RS"][:, 0, i:i + 1]).then_inc(*freed(("ws", h, qt), "swa_e", (h, qt)))
                            A(b3["ES"][:, 0, i:i + 1], prm("sink", 0)[:, h:h + 1], ACT.Exp,
                                   bias=b3["NM"][:, 0, i:i + 1]).then_inc(*mark("swa_es", (h, qt)))
                exps(0)
                for t in range(8):
                    if t < 7:
                        exps(t + 1)
                    for h in (2 * t, 2 * t + 1):
                        for qt in range(2):
                            key = ("wt", h, qt)
                            act.wait_ge(*done("filled", key))
                            bank = bank_of(key)
                            q = 4 * (h % 2)
                            A(b3["PTX"][:, q:q + 4, qt * P:qt * P + P],
                                        bank.rearrange("p (k q) -> p k q", k=4), ACT.Copy).then_inc(*freed(key, "swa_pt", (h, qt)))
                    act.wait_ge(*done("filled", ("wo2", t)))
                    bank = bank_of(("wo2", t))
                    A(H[:, t, 0:SEQ], bank[:, 0:SEQ], ACT.Copy).then_inc(*freed(("wo2", t), "swa_o", t))

            def shift(tag, l, n3, n):
                for k in range(KT):
                    for s in range(n // SEQ):
                        act.wait_ge(*done("scaled", (tag, k, s)))
                        ins = A(H[:, k, s * SEQ:s * SEQ + SEQ], H[:, k, s * SEQ:s * SEQ + SEQ], ACT.Identity,
                                bias=MODS[:, l, 3 * n3 * KT + k, s:s + 1], scale=1.0)
                        if (k, s) == (KT - 1, n // SEQ - 1):
                            ins.then_inc(*mark("h_shifted", tag))

            def norm2(tag, l, n3, n, wait):
                squares(tag, n, wait)
                rsqrt(R[:, 0:n], ("ss", tag), n, D, "factor", tag)
                shift(tag, l, n3, n)

            act.wait_ge(*done("const_loaded", 0))
            act.wait_ge(*done("par_loaded", 0))
            for i, t in ((0, COS), (1, SIN)):
                act.wait_ge(*done("angle", i))
                A(t, t, ACT.Sin).then_inc(*mark("rotary", i))
            act.wait_ge(*done("cond_pad", 0))
            A(COND[:, :, 0:2], prm("cond", 0).rearrange("p (k s) -> p k s", k=KT), ACT.Silu).then_inc(*mark("cond", 0))
            for l in range(DEPTH):
                squares(("n1", l), SEQ, (lambda k: done("x_loaded", 0)) if l == 0 else x_after(("n2", l - 1)))
                rsqrt(R[:, 0:SEQ], ("ss", ("n1", l)), SEQ, D, "factor", ("n1", l))
                project(l)
                fox_act(l)
                mod_row_act(l, 0)
                gla_act(l)
                mod_row_act(l, 1)
                head_norm_act(l, "ro", "rss", r1, "ret")
                mod_row_act(l, 2)
                ssd_act(l)
                mod_row_act(l, 3)
                mod_row_act(l, 4)
                merge_act(l)
                squares(("n2", l), SEQ, x_after(("wo", l), 4))
                rsqrt(R[:, 0:SEQ], ("ss", ("n2", l)), SEQ, D, "factor", ("n2", l))
                ffn(f"ffi{l}", ("n2", l), SEQ)
            for l in range(DEPTH):
                if l == 0:
                    act.wait_ge(*done("ctx_loaded", 0))
                norm2(("b0", l), l, 0, BOTH, x_after(("n2", 1) if l == 0 else ("b2", 0)))
                ffn(f"ffi2{l}0", ("b0", l), BOTH)
                norm2(("b1", l), l, 1, BOTH, x_after(("b0", l)))
                (mla_act, swa_act)[l]()
                n = BOTH if l == 0 else SEQ
                norm2(("b2", l), l, 2, n, x_after(("mlao", "swao")[l], 4))
                ffn(f"ffi2{l}1", ("b2", l), n)
            squares("final", SEQ, x_after(("b2", 1)))
            rsqrt(R[:, 0:SEQ], ("ss", "final"), SEQ, D, "factor", "final")

        @block.vector
        def _(dve):
            v = dve
            TTN, TS, STT = dve.tensor_tensor, dve.tensor_scalar, dve.scalar_tensor_tensor
            half, half8, quarter = cst("half"), cst("half8"), cst("quarter")
            ln = lambda ins: link(dve, "dve_step", ins)

            def angles():
                v.wait_ge(*done("pos_loaded", 0))
                T = [PJ[:, i, :] for i in range(4)]
                ln(v.tensor_copy(T[0], COS.bitcast(I32)))
                ln(TS(T[1], T[0], cst("inv"), None, ALU.mult))
                big = 1.5 * 2.0 ** 23
                for i, (dst, turn, back) in enumerate(((COS, 0.25, float(np.pi / 2)), (SIN, 0.0, 0.0))):
                    ln(TS(T[2], T[1], float(1 / (2 * np.pi)), turn, ALU.mult, ALU.add))
                    ln(TS(T[2], T[2], big, -big, ALU.add, ALU.add))
                    ln(STT(T[3], T[2], -6.28125, T[1], ALU.mult, ALU.add))
                    c2 = float(np.float32(2 * np.pi - 6.28125))
                    c3 = float(2 * np.pi - 6.28125 - c2)
                    ln(STT(T[3], T[2], -c2, T[3], ALU.mult, ALU.add))
                    ln(STT(T[3], T[2], -c3, T[3], ALU.mult, ALU.add))
                    pi = 3.1415925
                    ln(TS(T[3], T[3], back, pi, ALU.add, ALU.min))
                    TS(dst, T[3], -pi, None, ALU.max).then_inc(*mark("angle", i))

            def norm1(tag, name, l, n=SEQ):
                v.wait_ge(*done("factor", tag))
                for k in range(KT):
                    ins = STT(H[:, k, 0:n], X[:, k, 0:n], col(name, l, k), R[:, 0:n], ALU.mult, ALU.mult)
                    if tag == "final":
                        ins.then_inc(*mark("result", k))
                if tag != "final":
                    ins.then_inc(*mark("h_ready", tag))

            def project(l):
                for name, kind, dst in PROJ_DVE:
                    key = ("p", l, name)
                    v.wait_ge(*done("filled", key))
                    bank = bank_of(key)
                    if kind == "pj":
                        v.tensor_copy(PJ[:, dst, :], bank[:, 0:SEQ]).then_inc(*freed(key, ("fox_pj", "gla_pj", "ret_pj")[dst // 4], (l, dst % 4)))
                    elif kind == "v":
                        v.tensor_copy(V[:, :, dst * SEQ:dst * SEQ + SEQ], bank.rearrange("p (t f) -> p t f", t=TT)).then_inc(*freed(key, "values", (l, dst)))
                    elif name == "ff":
                        TS(small["FX"][0:HEADS, 0, :], bank[0:HEADS, 0:SEQ], col("fox_bf", l, 0, HEADS), None, ALU.add).then_inc(*freed(key, "fox_fx", l))
                    elif name == "glr":
                        v.tensor_copy(small["GLR"][0:LOWRANK, 0, :], bank[0:LOWRANK, 0:SEQ]).then_inc(*freed(key, "glr", l))
                    elif name == "dt":
                        TS(d2["DX"][0:SSD_HEADS, 0, :], bank[0:SSD_HEADS, 0:SEQ], col("dt_bias", l, 0, SSD_HEADS), None,
                                     ALU.add).then_inc(*freed(key, "ssd_dx", l))
                for t in range(XBC_T):
                    v.wait_ge(*done("xbc", (l, t)))
                    w = lambda i: col("conv_w", l, t * CONV + i)
                    ln(TS(CV[:, t, :], XP[:, t, 0:SEQ], w(0), col("conv_b", l, t), ALU.mult, ALU.add))
                    for i in range(1, CONV):
                        ins = STT(CV[:, t, :], XP[:, t, i:i + SEQ], w(i), CV[:, t, :], ALU.mult, ALU.add)
                        if i < CONV - 1:
                            ln(ins)
                    ins.then_inc(*mark("conv", (l, t)))

            def fox_dve(l):
                v.wait_ge(*done("fox_ln", l))
                FX, FA = small["FX"][0:HEADS, 0, :], small["FA"][0:HEADS, 0, :]
                CC, NCC = small["CC"][0:HEADS, 0, :], small["NCC"][0:HEADS, 0, :]
                ln(TS(FX, FX, 0.0, None, ALU.min))
                ln(TTN(FX, FX, FA, ALU.subtract))
                ln(v.tensor_tensor_scan(CC, cst("ones", HEADS)[:, 0:1].to_broadcast([HEADS, SEQ]), FX, 0.0, ALU.mult, ALU.add))
                TS(NCC, CC, -1.0, None, ALU.mult).then_inc(*mark("fox_c", l))
                v.wait_ge(*done("fox_r", (l, 1)))
                for t in range(2):
                    STT(t1["KF"][:, t, :], PJ[:, FQ + 2 + t, :], col("fox_kn", l, 0), t1["RF"][:, 2 + t, :], ALU.mult, ALU.mult).then_inc(*mark("fox_kf", (l, t)))
                ln(STT(t1["A0"][:, 0:2, :], PJ[:, FQ:FQ + 2, :], col("fox_qn", l, 0), t1["RF"][:, 0:2, :], ALU.mult, ALU.mult))
                for h in range(HEADS):
                    ins = TS(t1["QZ"][:, h, :], t1["A0"][:, h // 2, :], half8[:, h % 2:h % 2 + 1], None, ALU.mult)
                ins.then_inc(*mark("fox_qk", l))
                for h in range(HEADS):
                    for qt in range(TT):
                        i, nk = 2 * h + qt, P * (qt + 1)
                        v.wait_ge(*done("filled", ("fs", l, h, qt)))
                        bank = bank_of(("fs", l, h, qt))
                        v.tensor_reduce(small["NM"][:, 0, i:i + 1], bank[:, 0:nk], AX_X, ALU.max, negate=True).then_inc(*mark("fox_nm", (l, h, qt)))
                for h in range(HEADS):
                    for qt in range(TT):
                        i, nk = 2 * h + qt, P * (qt + 1)
                        v.wait_ge(*done("fox_e", (l, h, qt)))
                        ln(v.reciprocal(small["RC"][:, 0, i:i + 1], small["RS"][:, 0, i:i + 1]))
                        TS(t1["E"][:, i, 0:nk], t1["E"][:, i, 0:nk], small["RC"][:, 0, i:i + 1], None, ALU.mult).then_inc(*mark("fox_p", (l, h, qt)))

            def gla_dve(l):
                v.wait_ge(*done("filled", ("la", l)))
                bank = bank_of(("la", l))
                GX, B = g1["GX"], g1["B"]
                TS(GX[:, 0, :], bank[:, 0:SEQ], col("gla_b", l, 0), None, ALU.add)
                TS(GX[:, 1, :], bank[:, SEQ:512], col("gla_b", l, 1), None, ALU.add).then_inc(*freed(("la", l), "gla_gx", l))
                v.wait_ge(*done("gla_ln", l))
                ln(TS(GX, GX, 0.0, None, ALU.min))
                ln(TTN(GX, GX, g1["GA"], ALU.subtract))
                for t in range(2):
                    ins = v.tensor_tensor_scan(B[:, t, :], cst("reset"), GX[:, t, :], 0.0, ALU.mult, ALU.add)
                ins.then_inc(*mark("gla_b", l))
                v.wait_ge(*done("gla_b", l))
                for t in range(2):
                    b4 = B[:, t, :].rearrange("p (c i) -> p c i", c=NCHUNK)
                    n4 = g1["ND"][:, t, :].rearrange("p (c i) -> p c i", c=NCHUNK)
                    ins = TTN(n4, b4[:, :, CHUNK - 1:CHUNK].to_broadcast([P, NCHUNK, CHUNK]), b4, ALU.subtract)
                ins.then_inc(*mark("gla_nd", l))
                v.wait_ge(*done("gla_e", (l, 0)))
                ln(STT(GX, PJ[:, GQ:GQ + 2, :], 0.125, g1["EB"], ALU.mult, ALU.mult))
                for h in range(HEADS):
                    ins = TS(g1["QDZ"][:, h, :], GX[:, h // 2, :], half[:, h % 2:h % 2 + 1], None, ALU.mult)
                v.wait_ge(*done("gla_e", (l, 1)))
                TTN(g1["EI"], g1["EI"], PJ[:, GQ + 2:GQ + 4, :], ALU.mult).then_inc(*mark("gla_qdz", l))
                v.wait_ge(*done("gla_e", (l, 2)))
                TTN(g1["EK"], g1["EK"], PJ[:, GQ + 2:GQ + 4, :], ALU.mult).then_inc(*mark("gla_ke", l))
                mod_columns(l, 0)
                v.wait_ge(*done("filled", ("gkt", l)))
                bank = bank_of(("gkt", l))
                for c in range(2):
                    ins = TS(g1["KEZ"][:, c, :], bank, half[:, c:c + 1], None, ALU.mult)
                ins.then_inc(*freed(("gkt", l), "gla_kez", l))
                for tt in range(TT):
                    v.wait_ge(*done("filled", ("ga", l, tt)))
                    bank = bank_of(("ga", l, tt))
                    mask = cst("chunk_up").unsqueeze(1).to_broadcast([P, HEADS, P])
                    TTN(g1["AT"][:, tt * HEADS:(tt + 1) * HEADS, :], bank.rearrange("p (h t) -> p h t", h=HEADS), mask,
                                  ALU.mult).then_inc(*freed(("ga", l, tt), "gla_at", (l, tt)))
                v.wait_ge(*done("filled", ("gkv", l)))
                bank = bank_of(("gkv", l))
                S = g1["S"]
                kv = bank.rearrange("p (c d) -> p c d", c=8)
                ln(v.tensor_copy(S[:, 2:4, :], kv[:, 0:2, :]))
                for c in range(1, NCHUNK - 1):
                    for t in range(2):
                        e = c * CHUNK + CHUNK - 1
                        ins = STT(S[:, 2 * (c + 1) + t, :], S[:, 2 * c + t, :], g1["EB"][:, t, e:e + 1], kv[:, 2 * c + t, :],
                                  ALU.mult, ALU.add)
                        if c < NCHUNK - 2:
                            ln(ins)
                ins.then_inc(*freed(("gkv", l), "gla_s", (l, NCHUNK - 1)))
                head_norm(l, g1, "gla", 2, 0)

            def head_norm(l, buf, name, y, sg):
                v.wait_ge(*done(f"{name}_r", l))
                ln(STT(buf["OB"], buf["OB"], col(f"{name}_norm", l, 0), buf["OQ"], ALU.mult, ALU.mult))
                v.wait_ge(*done("silu_gate", (l, 3)))
                ins = TTN(YBR[:, y:y + 2, :], buf["OB"], SG[:, sg:sg + 2, :], ALU.mult)
                ins.then_inc(*mark("branches", (l, y)))

            def rope(dst, src, cos, sin, tc, ts):
                bc = lambda t: t.unsqueeze(1).to_broadcast([P, 2, SEQ])
                TTN(tc, src, bc(cos), ALU.mult)
                ln(TTN(ts, src, bc(sin), ALU.mult))
                TTN(dst[:, 0, :], tc[:, 0, :], ts[:, 1, :], ALU.subtract)
                return TTN(dst[:, 1, :], ts[:, 0, :], tc[:, 1, :], ALU.add)

            def ret_dve(l):
                v.wait_ge(*done("rotary", 1))
                v.wait_ge(*done("gla_r", l))
                ln(rope(r1["K"], PJ[:, RQ + 2:RQ + 4, :], COS, SIN, r1["TC"], r1["TS"]))
                ln(rope(r1["Q"], PJ[:, RQ:RQ + 2, :], COS, SIN, r1["TC"], r1["TS"]))
                for h in range(HEADS):
                    ins = TS(r1["QZ"][:, 2 * h:2 * h + 2, :], r1["Q"], quarter[:, h:h + 1], None, ALU.mult)
                ins.then_inc(*mark("ret_qk", l))
                mod_columns(l, 1)
                dec = cst("decay").rearrange("p (h t) -> p h t", h=HEADS)
                for h in range(HEADS):
                    v.wait_ge(*done("filled", ("rs", l, h)))
                    bank = bank_of(("rs", l, h))
                    TTN(r1["RT"][:, h, :], bank[:, 0:CAUSAL], dec[:, h, :], ALU.mult).then_inc(*freed(("rs", l, h), "ret_w", (l, h)))
                head_norm(l, r1, "ret", 4, 2)

            def ssd_pre(l):
                v.wait_ge(*done("ssd_ln", l))
                DX, DA, DL = (d2[k][0:SSD_HEADS, 0, :] for k in ("DX", "DA", "DL"))
                CS, NCS, AE = (d2[k][0:SSD_HEADS, 0, :] for k in ("CS", "NCS", "AE"))
                ln(TS(DX, DX, 0.0, None, ALU.max))
                ins = TTN(DX, DX, DL, ALU.add)
                ins.then_inc(*mark("ssd_dt", l))
                v.wait_ge(*done("ssd_dt", l))
                v.wait_ge(*done("ssd_ae", l))
                ln(TS(DA, DX, AE, -1.0, ALU.mult, ALU.mult))
                ln(v.tensor_tensor_scan(CS, cst("ones", SSD_HEADS)[:, 0:1].to_broadcast([SSD_HEADS, SEQ]), DA, 0.0, ALU.mult, ALU.add))
                TS(NCS, CS, -1.0, None, ALU.mult).then_inc(*mark("ssd_cs", l))
                v.wait_ge(*done("ssd_xc", l))
                for g in range(2):
                    ins = TS(d1["CZ"][:, g, :], XC[:, 5, :], half[:, g:g + 1], None, ALU.mult)
                ins.then_inc(*mark("ssd_cz", l))
                mod_columns(l, 2)
                v.wait_ge(*done("filled", ("dtt", l)))
                bank = bank_of(("dtt", l))
                v.tensor_copy(small["DTT"], bank[:, 0:TT * SSD_HEADS].rearrange("p (t h) -> p t h", t=TT)).then_inc(*freed(("dtt", l)))
                dve.wait_ge(*done("free", ("dtt", l)))
                for tt in range(TT):
                    v.wait_ge(*done("filled", ("xt", l, tt)))
                    bank = bank_of(("xt", l, tt))
                    dt = small["DTT"][:, tt, :].unsqueeze(2).to_broadcast([P, SSD_HEADS, HD])
                    TTN(d1["XDT"][:, tt, :].rearrange("p (h d) -> p h d", h=SSD_HEADS),
                                  bank.rearrange("p (h d) -> p h d", h=SSD_HEADS), dt, ALU.mult).then_inc(*freed(("xt", l, tt), "ssd_xdt", (l, tt)))

            def ssd_dve(l):
                ssd_pre(l)
                for h in range(SSD_HEADS):
                    v.wait_ge(*done("ssd_cb", (l, h // 4)))
                    v.wait_ge(*done("ssd_l", (l, h)))
                    TTN(d1["L"][:, h, :], d1["L"][:, h, :], d1["CB"][:, h // 4, :], ALU.mult).then_inc(*mark("ssd_w", (l, h)))
                for t in range(4):
                    v.wait_ge(*done("filled", ("yo", l, t)))
                    bank = bank_of(("yo", l, t))
                    STT(d1["OD"][:, t, :], XC[:, t, :], col("ssd_d", l, t), bank[:, 0:SEQ], ALU.mult, ALU.add).then_inc(*freed(("yo", l, t)))
                    dve.wait_ge(*done("free", ("yo", l, t)))
                    v.wait_ge(*done("silu_gate", (l, 4 + t)))
                    TTN(d1["OD"][:, t, :], d1["OD"][:, t, :], SG[:, 4 + t, :], ALU.mult).then_inc(*mark("ssd_od", (l, t)))
                v.wait_ge(*done("ssd_r", l))
                for t in range(4):
                    ins = STT(YBR[:, 6 + t, :], d1["OD"][:, t, :], col("ssd_norm", l, t), d1["OQ"][:, t // 2, :], ALU.mult, ALU.mult)
                ins.then_inc(*mark("branches", (l, 9)))

            def merge_dve(l):
                mod_columns(l, 3)
                mod_columns(l, 4)
                for k in range(4):
                    v.wait_ge(*done("gate", (l, k, 1)))
                for m in range(KT):
                    for q in range(2):
                        v.wait_ge(*done("filled", ("up", l, m, q)))
                        bank = bank_of(("up", l, m, q))
                        TTN(mg[:, 2 * (m % 2) + q, :], bank, flat(gates[:, m, 2 * q:2 * q + 2, :]), ALU.mult).then_inc(*freed(("up", l, m, q)))
                        dve.wait_ge(*done("free", ("up", l, m, q)))
                    a, b = mg[:, 2 * (m % 2), :], mg[:, 2 * (m % 2) + 1, :]
                    ln(TTN(a, a, b, ALU.add))
                    TTN(H[:, m, 0:SEQ], a[:, 0:SEQ], a[:, SEQ:512], ALU.add).then_inc(*mark("merged", (l, m)))
                residual(("wo", l), 4, ("wo", l))

            def residual(tag, n_lots, key0, coef=None, n=SEQ, l=0):
                for j in range(n_lots):
                    for t in range(2):
                        m, key = 2 * j + t, (key0, ("rest", j), t)
                        v.wait_ge(*done("filled", key))
                        bank = bank_of(key)
                        add_tile(m, bank, key, coef, n, (tag, j, t), l)

            def add_tile(m, bank, key, coef, n, event, l=0):
                if coef is None:
                    TTN(X[:, m, 0:n], X[:, m, 0:n], bank[:, 0:n], ALU.add).then_inc(*freed(key, "x_ready", event))
                    return
                for s in range(n // SEQ):
                    w = slice(s * SEQ, s * SEQ + SEQ)
                    ins = STT(X[:, m, w], bank[:, w], MODS[:, l, coef * KT + m, s:s + 1], X[:, m, w], ALU.mult, ALU.add)
                ins.then_inc(*freed(key, "x_ready", event))

            def ffn(tag_in, tag_out, tag, n, coef=None, l=0):
                def lot(j, k):
                    slot = k if isinstance(k, int) else k[1] % 4
                    v.wait_ge(*done("filled", (tag, "u", k)))
                    bank = bank_of((tag, "u", k))
                    v.wait_ge(*done("silu", (tag, k)))
                    TTN(HID[:, j, 0:n], SILU[:, slot, 0:n], bank[:, 0:n], ALU.mult).then_inc(*freed((tag, "u", k), "hidden", (tag, k)))
                lots(v, tag_in, FT, lot)

                def lot2(j, k):
                    key = (tag, "o", k)
                    v.wait_ge(*done("filled", key))
                    bank = bank_of(key)
                    add_tile(j, bank, key, coef, n, (tag, k), l)
                lots(v, tag_out, KT, lot2)

            def mod_columns(l, b):
                key, q, n = ("mc", l * MOD_B + b), mod_rows(b) // 32, MOD_N // P
                v.wait_ge(*done("filled", key))
                src = bank_of(key).rearrange("p (t r) -> p t r", t=n)
                a = b * MOD_Q * n
                for g in range(q):
                    bias = prm("mod_b", l)[:, a + g * n:a + (g + 1) * n].unsqueeze(2).to_broadcast([P, n, 2])
                    ins = TTN(MODS[:, l, a + g * n:a + (g + 1) * n, :], src[:, :, 32 * g:32 * g + 2], bias, ALU.add)
                ins.then_inc(*freed(key, "mod", (l, b)))

            def mods(l):
                v.wait_ge(*done("mod", (l, MOD_B - 1)))
                MOD, NA = MODS[:, l], NAS[:, l].rearrange("p (n k) s -> p n k s", n=3)
                g = prm("norm_g", l).rearrange("p (n k) -> p n k", n=3)
                for n3 in range(3):
                    STT(NA[:, n3, :, :], MOD[:, (3 * n3 + 1) * KT:(3 * n3 + 2) * KT, :], 1.0,
                        g[:, n3, :].unsqueeze(2).to_broadcast([P, KT, 2]), ALU.add, ALU.mult)
                for c in (2, 8):
                    ins = TS(MOD[:, c * KT:(c + 1) * KT, :], MOD[:, c * KT:(c + 1) * KT, :], 0.5, None, ALU.mult)
                ln(ins)

            def norm2(tag, l, n3, n):
                v.wait_ge(*done("factor", tag))
                for k in range(KT):
                    for s in range(n // SEQ):
                        w = slice(s * SEQ, s * SEQ + SEQ)
                        STT(H[:, k, w], X[:, k, w], NAS[:, l, n3 * KT + k, s:s + 1], R[:, w], ALU.mult, ALU.mult).then_inc(*mark("scaled", (tag, k, s)))

            def rope_keys(src, kr, kz, tmp, name):
                ln(rope(kr[:, :, 0:SEQ], src[:, :, 0:SEQ], cst("cos2"), cst("sin2"), tmp[:, 0:2, 0:SEQ], tmp[:, 2:4, 0:SEQ]))
                ln(v.tensor_copy(kr[:, :, SEQ:BOTH], src[:, :, SEQ:BOTH]))
                for j in range(4):
                    TS(kz[:, 2 * j:2 * j + 2, :], kr, quarter[:, j:j + 1], None, ALU.mult).then_inc(*mark(name, j))

            def mla_dve():
                KAB = b2["QX"].rearrange("p a b -> p (a b)").rearrange("p (a b) -> p a b", a=2)
                v.wait_ge(*done("mla_down", 7))
                rope_keys(KAB, H[:, 0:2, :], b2["KZ"], H[:, 2:6, :], "mla_kz")
                for t in range(6):
                    v.wait_ge(*done("mla_r", t // 4))
                    g = col("q_norm", 0, t) if t < 4 else col("kv_norm", 0, t - 4)
                    STT(b2["CQ"][:, t, :], b2["CQ"][:, t, :], g, b2["RM"][:, t // 4, :], ALU.mult, ALU.mult).then_inc(*mark("mla_c", t))
                for j in range(2):
                    v.wait_ge(*done("mla_qr", 2 * j + 1))
                    ins = rope(b2["QX"][:, 2 * j:2 * j + 2, :], b2["QR"][:, 2 * j:2 * j + 2, 0:SEQ], cst("cos2"), cst("sin2"),
                               H[:, 2:4, 0:SEQ], H[:, 4:6, 0:SEQ])
                    ins.then_inc(*mark("mla_qx", j))
                    v.wait_ge(*done("mla_qx", j))
                def maxima(h):
                    for qt in range(4):
                        i, nk = 4 * (h % 2) + qt, BOTH if qt < 2 else CTX
                        v.wait_ge(*done("filled", ("ms", h, qt)))
                        bank = bank_of(("ms", h, qt))
                        ln(v.tensor_reduce(b2["NM"][:, 0, i:i + 1], bank[:, 0:nk], AX_X, ALU.max, negate=True))
                        TS(b2["NM"][:, 0, i:i + 1], b2["NM"][:, 0, i:i + 1], MLA_SCALE, None, ALU.mult).then_inc(*mark("mla_nm", (h, qt)))
                maxima(0)
                for h in range(MLA_H):
                    if h + 1 < MLA_H:
                        maxima(h + 1)
                    for qt in range(4):
                        i, nk = 4 * (h % 2) + qt, BOTH if qt < 2 else CTX
                        v.wait_ge(*done("mla_e", (h, qt)))
                        ln(v.reciprocal(b2["RC"][:, 0, i:i + 1], b2["RS"][:, 0, i:i + 1]))
                        TS(mla_pr(h, qt), mla_pr(h, qt), b2["RC"][:, 0, i:i + 1], None, ALU.mult).then_inc(*mark("mla_p", (h, qt)))
                residual("mlao", 4, "mlao", 5, BOTH, 0)

            def swa_dve():
                for g in range(4):
                    v.wait_ge(*done("swa_qs", 2 * g + 1))
                    ins = rope(b3["QX"][:, 2 * g:2 * g + 2, :], b3["QS"][:, 2 * g:2 * g + 2, :], cst("cos2"), cst("sin2"),
                               b3["TMP"][:, 0:2, 0:SEQ], b3["TMP"][:, 2:4, 0:SEQ])
                    ins.then_inc(*mark("swa_qx", g))
                    v.wait_ge(*done("swa_qx", g))
                v.wait_ge(*done("swa_kab", 1))
                rope_keys(b3["KAB"], b3["KR"], b3["KZ"], b3["TMP"], "swa_kz")
                def maxima(t):
                    for h in (2 * t, 2 * t + 1):
                        for qt in range(2):
                            i = 2 * (h % 4) + qt
                            v.wait_ge(*done("filled", ("ws", h, qt)))
                            bank = bank_of(("ws", h, qt))
                            nm = b3["NM"][:, 0, i:i + 1]
                            ln(v.tensor_reduce(nm, bank, AX_X, ALU.max))
                            ln(TS(nm, nm, SWA_SCALE, prm("sink", 0)[:, h:h + 1], ALU.mult, ALU.max))
                            TS(nm, nm, -1.0, None, ALU.mult).then_inc(*mark("swa_nm", (h, qt)))
                maxima(0)
                for t in range(8):
                    if t < 7:
                        maxima(t + 1)
                    for h in (2 * t, 2 * t + 1):
                        for qt in range(2):
                            i = 2 * (h % 4) + qt
                            rs = b3["RS"][:, 0, i:i + 1]
                            v.wait_ge(*done("swa_es", (h, qt)))
                            v.wait_ge(*done("swa_e", (h, qt)))
                            ln(TTN(rs, rs, b3["ES"][:, 0, i:i + 1], ALU.add))
                            ln(v.reciprocal(rs, rs))
                            TS(b3["PR"][:, i, :], b3["PR"][:, i, :], rs, None, ALU.mult).then_inc(*mark("swa_p", (h, qt)))
                residual("swao", 4, "swao", 5, SEQ, 1)

            v.wait_ge(*done("const_loaded", 0))
            v.wait_ge(*done("par_loaded", 0))
            angles()
            v.wait_ge(*done("x_loaded", 0))
            for l in range(DEPTH):
                norm1(("n1", l), "ln1", l)
                project(l)
                fox_dve(l)
                gla_dve(l)
                ret_dve(l)
                ssd_dve(l)
                merge_dve(l)
                norm1(("n2", l), "ln2", l)
                mods(l)
                ffn(f"ffi{l}", f"ffo{l}", ("n2", l), SEQ)
            v.wait_ge(*done("ctx_loaded", 0))
            for l in range(DEPTH):
                norm2(("b0", l), l, 0, BOTH)
                ffn(f"ffi2{l}0", f"ffo2{l}0", ("b0", l), BOTH, 2, l)
                norm2(("b1", l), l, 1, BOTH)
                (mla_dve, swa_dve)[l]()
                n = BOTH if l == 0 else SEQ
                norm2(("b2", l), l, 2, n)
                ffn(f"ffi2{l}1", f"ffo2{l}1", ("b2", l), n, 8, l)
            norm1("final", "final_g", 0)
    return plan


def constants():
    t = np.zeros((P, N_CONST), np.float32)

    def put(name, v):
        a, b = C[name]
        t[:v.shape[0], a:b] = v.reshape(v.shape[0], -1)
    r, c = np.arange(P)[:, None], np.arange(P)[None, :]
    put("ident", (r == c).astype(np.float32))
    put("ones", np.ones((P, P)))
    put("heads64", (r // HD == c // HD).astype(np.float32))
    put("mask_low", np.where(c <= r, 0.0, NEG))
    put("mask_up", np.where(r <= c, 0.0, NEG))
    put("chunk_up", ((r <= c) & (r // CHUNK == c // CHUNK)).astype(np.float32))
    put("reset", np.tile(np.arange(SEQ) % CHUNK != 0, (P, 1)).astype(np.float32))
    gamma = np.log(1.0 - 2.0 ** (-5.0 - np.arange(HEADS)))
    rel = np.concatenate([np.arange(SEQ)[None, :] - r, c - r], axis=1)
    put("decay", np.where(rel[:, None, :] >= 0, 0.125 * np.exp(np.maximum(rel, 0)[:, None, :] * gamma[None, :, None]), 0.0))
    i = np.arange(P) % 32
    tok = np.arange(SEQ)
    inv = np.exp(-np.log(10000.0) * (i % 16) / 16)
    ang = np.where(i < 16, 1, 0)[:, None] * (tok // 64)[None, :] * inv[:, None] \
        + np.where(i < 16, 0, 1)[:, None] * (tok % 64)[None, :] * inv[:, None]
    put("cos2", np.cos(ang))
    put("sin2", np.sin(ang))
    put("inv", (10000.0 ** (-i / 32.0))[:, None])
    put("eps", np.full((P, 1), 1e-6))
    put("one", np.ones((P, 1)))
    put("half", (r // HD == np.arange(2)).astype(np.float32))
    put("half8", 0.125 * (r // HD == np.arange(2)))
    put("quarter", (r // 32 == np.arange(4)).astype(np.float32))
    return t


def kernel(**inputs):
    import concourse.bacc as bacc
    from concourse.bass_utils import run_bass_kernel_spmd

    g = {k: np.asarray(v) for k, v in inputs.items()}
    asc = np.ascontiguousarray

    def lots_of(w, cols, per):
        kt = w.shape[0] // P
        t = w[:, cols].reshape(kt, P, -1, per, P)
        return asc(t.transpose(2, 1, 3, 0, 4)).reshape(t.shape[2], P, per * kt * P)

    def wide(w, cols):
        t = w[:, cols].reshape(w.shape[0] // P, P, -1)
        return asc(t.transpose(1, 0, 2)).reshape(1, P, -1)

    def mod_lots(w):
        t = w.reshape(2, KT // 2, P, MOD_G, MOD_N)
        return asc(t.transpose(3, 0, 2, 1, 4)).reshape(2 * MOD_G, P, KT // 2 * MOD_N)

    def cols_of(v):
        return v.reshape(-1, P).T

    halves = lambda base, heads, step, off: np.concatenate([base + h * step + off + np.arange(32) for h in heads])
    ar = np.arange
    start = {}
    at = 0
    for name, n in (("fq", 256), ("fk", 256), ("fv", 256), ("ff", 4), ("gq", 256), ("gk", 256), ("gv", 256), ("glr", 16),
                    ("gr", 256), ("rq", 256), ("rk", 256), ("rv", 256), ("rg", 256), ("z", 512), ("x", 768), ("dt", 8),
                    ("gates", 4096)):
        start[name] = at
        at += n

    def tile_cols(name):
        if name[:2] in ("rq", "rk"):
            return halves(start[name[:2]], range(4), 64, 32 if name[2] == "b" else 0)
        return start[name[:-1]] + int(name[-1]) * P + ar(P)

    proj, gate = [], []
    for l in range(DEPTH):
        w = g["w_in"][l]
        rows = []
        for kind, names in PROJ_LOTS:
            if kind == "t":
                rows.append(lots_of(w, np.concatenate([tile_cols(n) for n in names]), 2))
            elif kind == "v":
                rows.append(wide(w, start[names] + ar(256)))
            else:
                m = np.zeros((D, 2 * P), np.float32)
                for name, a, n in (("ff", 0, 4), ("glr", 32, 16), ("dt", 64, 8)):
                    m[:, a:a + n] = w[:, start[name]:start[name] + n]
                rows.append(lots_of(m, ar(2 * P), 2))
        proj.append(np.concatenate(rows))
        gate.append(lots_of(w, np.concatenate([start["gates"] + q * D + m * P + ar(P) for m in range(KT) for q in range(4)]), 2))
    up = np.stack([lots_of(np.concatenate([g[f"w_up_{b}"][l] for b in "abcd"]), ar(D), 2) for l in range(DEPTH)])
    pairs = np.concatenate([np.concatenate([j * P + ar(P), FF + j * P + ar(P)]) for j in range(FT)])
    uq_cols = np.concatenate([h * 192 + ar(P) for h in range(8)]
                             + [halves(128, range(4 * j, 4 * j + 4), 192, o) for j in range(2) for o in (0, 32)])
    ukv = g["mla_w_ukv_2"][0]
    q_cols = np.concatenate([halves(0, [j * 4 + gg for j in range(4)], 64, o) for gg in range(4) for o in (0, 32)]
                            + [halves(D, range(4), 64, o) for o in (0, 32)])
    down_cols = np.concatenate([ar(768), np.tile(768 + ar(32), 4), np.tile(800 + ar(32), 4)])
    par = np.zeros((P, N_PAR), np.float32)

    def put(name, l, v):
        a, b = PAR[name, l]
        par[:v.shape[0], a:b] = v.reshape(v.shape[0], -1)
    for l in range(DEPTH):
        put("ln1", l, cols_of(g["ln1"][l]))
        put("ln2", l, cols_of(g["ln2"][l]))
        for name in ("fox_qn", "fox_kn", "gla_norm", "ret_norm"):
            put(name, l, np.tile(g[name][l], 2)[:, None])
        put("gla_b", l, cols_of(g["gla_b"][l]))
        put("conv_w", l, g["ssd_conv_w"][l].reshape(CONV, XBC_T, P).transpose(2, 1, 0))
        put("conv_b", l, cols_of(g["ssd_conv_b"][l]))
        put("ssd_d", l, cols_of(np.repeat(g["ssd_d"][l], HD)))
        put("ssd_norm", l, cols_of(g["ssd_norm"][l]))
        put("fox_bf", l, g["fox_bf"][l][:, None])
        put("dt_bias", l, g["ssd_dt_bias"][l][:, None])
        put("a_log", l, g["ssd_a_log"][l][:, None])
        put("gla_w2", l, g["gla_w2"][l])
        put("mod_b", l, cols_of(g["mod_b_2"][l]))
        put("norm_g", l, cols_of(g["norm_g_2"][l]))
    put("final_g", 0, cols_of(g["final_norm_g_2"]))
    put("q_norm", 0, cols_of(g["mla_q_norm_2"][0]))
    put("kv_norm", 0, cols_of(g["mla_kv_norm_2"][0]))
    put("sink", 0, np.tile(g["swa_sink_2"][0], (P, 1)))
    put("cond", 0, np.stack([cols_of(g["c_2"][0]), cols_of(g["c_ctx_2"])], axis=2))

    ffo = lambda w: asc(w.reshape(FT, P, KT, P).transpose(2, 1, 0, 3)).reshape(KT, P, FT * P)
    seq = lambda x: asc(x[0].T.reshape(KT, P, SEQ).transpose(1, 0, 2))
    arrays = {
        "x_in": seq(g["x"]), "ctx_in": seq(g["ctx_2"]), "pos_in": asc(g["positions"]), "const_in": constants(), "par_in": par,
        "w_proj": np.stack(proj), "w_gate": np.stack(gate), "w_up": up,
        "w_out": np.stack([lots_of(g["w_out"][l], ar(D), 2) for l in range(DEPTH)]),
        "ffn_in1": np.stack([lots_of(g["w_ffn_in"][l], pairs, 2) for l in range(DEPTH)]),
        "ffn_out1": np.stack([ffo(g["w_ffn_out"][l]) for l in range(DEPTH)]),
        "mod_w": np.stack([mod_lots(g["mod_w_2"][l]) for l in range(DEPTH)]),
        "ffn_in2": np.stack([np.stack([lots_of(g["ffn_w_in_2"][l, i], pairs, 2) for i in range(2)]) for l in range(DEPTH)]),
        "ffn_out2": np.stack([np.stack([ffo(g["ffn_w_out_2"][l, i]) for i in range(2)]) for l in range(DEPTH)]),
        "w_down": lots_of(g["mla_w_down_2"][0], down_cols, 2),
        "w_uq": lots_of(g["mla_w_uq_2"][0], uq_cols, 4),
        "w_ukv": np.concatenate([lots_of(ukv, np.concatenate([h * 256 + ar(P) for h in range(8)]), 8),
                                 wide(ukv, np.concatenate([h * 256 + P + ar(P) for h in range(8)]))]),
        "w_mla_o": lots_of(g["mla_w_o_2"][0], ar(D), 2),
        "w_qkv": np.concatenate([lots_of(g["swa_w_qkv_2"][0], q_cols, 2), wide(g["swa_w_qkv_2"][0], D + 256 + ar(256))]),
        "w_swa_o": lots_of(g["swa_w_o_2"][0], ar(D), 2),
    }

    def program(old):
        nc = bacc.Bacc("TRN2", target_bir_lowering=False, num_devices=1)
        args = [nc.dram_tensor(name, a.shape, mybir.dt.from_np(a.dtype), kind="ExternalInput").ap() for name, a in arrays.items()]
        out = nc.dram_tensor("out", (P, KT, SEQ), F32, kind="ExternalOutput").ap()
        return nc, build(nc, old, *args_in_order(dict(zip(arrays, args))), out)

    plan = None
    for _ in range(3):
        nc, plan = program(plan)
    r = run_bass_kernel_spmd(nc, [arrays], core_ids=[0])
    return asc(np.asarray(r.results[0]["out"]).transpose(2, 1, 0)).reshape(1, SEQ, D)


def args_in_order(a):
    return [a[n] for n in ("x_in", "ctx_in", "pos_in", "const_in", "par_in", "w_proj", "w_gate", "w_up", "w_out", "ffn_in1",
                           "ffn_out1", "mod_w", "ffn_in2", "ffn_out2", "w_down", "w_uq", "w_ukv", "w_mla_o", "w_qkv", "w_swa_o")]
```

```python
from contextlib import ExitStack, contextmanager

import numpy as np

import concourse.bass as bass
from concourse import mybir

F32 = mybir.dt.float32
F32R = mybir.dt.float32r
I32 = mybir.dt.int32
ALU = mybir.AluOpType
ACT = mybir.ActivationFunctionType
AX_X = mybir.AxisListType.X

P = 128
D = 1024
KT = D // P
SEQ = 256
TT = SEQ // P
CTX = 256
BOTH = SEQ + CTX
DEPTH = 2
HD = 64
CHUNK = 64
NCHUNK = SEQ // CHUNK
HEADS = 4
SSD_HEADS = 8
FF = 2816
FT = FF // P
CONV = 4
XBC_T = 6
N_MOD = 9
MOD_T = N_MOD * KT
MOD_N = 512
MOD_G = N_MOD * D // MOD_N
MOD_Q = 4
MOD_B = -(-MOD_G // MOD_Q)
LOWRANK = 16
GLA_TAU = 16.0
MLA_H = 8
MLA_SCALE = float((128 + 64) ** -0.5)
SWA_SCALE = 0.125
CAUSAL = SEQ + P
NEG = -1e30

SLOTS = 4
SLOT = KT * P
FF_PARTS = ((0, 8), (8, 15), (15, FT))
RING = 6

C = {}
_at = 0
for _name, _w in (("ident", P), ("ones", P), ("heads64", P), ("mask_low", P), ("mask_up", P), ("chunk_up", P),
                  ("cos2", SEQ), ("sin2", SEQ),
                  ("inv", 1), ("eps", 1), ("one", 1), ("half", 2), ("half8", 2), ("quarter", 4)):
    C[_name] = (_at, _at + _w)
    _at += _w
N_CONST = _at
C1 = {"decay": (0, HEADS * CAUSAL), "reset": (HEADS * CAUSAL, HEADS * CAUSAL + SEQ)}
N_CONST1 = HEADS * CAUSAL + SEQ

PAR = {}
_at = 0
for _l in range(DEPTH):
    for _name, _w in (("ln1", KT), ("ln2", KT), ("fox_qn", 1), ("fox_kn", 1), ("gla_b", 2), ("gla_norm", 1),
                      ("ret_norm", 1), ("conv_w", XBC_T * CONV), ("conv_b", XBC_T), ("ssd_d", 4),
                      ("ssd_norm", 4), ("fox_bf", 1), ("dt_bias", 1), ("a_log", 1), ("gla_w2", 256)):
        PAR[_name, _l] = (_at, _at + _w)
        _at += _w
for _l in range(DEPTH):
    for _name, _w in (("mod_b", MOD_T), ("norm_g", 3 * KT)):
        PAR[_name, _l] = (_at, _at + _w)
        _at += _w
for _name, _w in (("final_g", KT), ("q_norm", 4), ("kv_norm", 2), ("sink", 16), ("cond", 2 * KT)):
    PAR[_name, 0] = (_at, _at + _w)
    _at += _w
N_PAR = _at


PROJ_LOTS = ["misc", "fq0", "fq1", "fk0", "fk1", "fv.0", "fv.1", "x0", "x1", "x2", "x3", "x4", "x5", "gq0", "gq1", "gk0", "gk1",
             "gv.0", "gv.1", "rqa", "rqb", "rka", "rkb", "rv.0", "rv.1", "gr0", "gr1", "rg0", "rg1", "z0", "z1", "z2", "z3"]
FOX_SQUARES, FOX_SUMS, FOX_FACTORS, FOX_QK = 5, 8, 8, 9
FOX_SCORES, FOX_TURNS, FOX_OUT = 13, 16, 21
CONV_LOT, CONV_OUT = 22, 28
PROJ_ACT = dict([(f"x{i}", i) for i in range(6)] + [("gr0", 0), ("gr1", 1), ("rg0", 2), ("rg1", 3)] + [(f"z{i}", 4 + i) for i in range(4)])
PROJ_DVE = {"fq0": 0, "fq1": 1, "fk0": 2, "fk1": 3, "gq0": 4, "gq1": 5, "gk0": 6, "gk1": 7, "rqa": 8, "rqb": 9, "rka": 10, "rkb": 11}
PROJ_V = {"fv": 0, "gv": 1, "rv": 2}


def stage_table():
    order = []
    for l in range(DEPTH):
        order += [(f"proj{l}", len(PROJ_LOTS), 99, 1, 0), (f"mod{l}", 4 * MOD_G, 99, 0, 0), (f"gate{l}", 4 * KT, 4, 1, 0),
                  (f"up{l}", 10, 99, 0, 0), (f"wo{l}", KT, 99, 1, 1), (f"ffi{l}", 2 * FT, 4, 1, 1), (f"ffo{l}", 3 * KT, 12, 1, 1)]
    for l in range(DEPTH):
        order += [(f"ffi2{l}0", 2 * FT, 4, 1, 1), (f"ffo2{l}0", 3 * KT, 12, 1, 1)]
        if l == 0:
            order += [("down", 8, 99, 1, 0), ("uq", 6, 99, 0, 0), ("ukv", 4, 99, 0, 0), ("mlao", 8, 99, 1, 1)]
        else:
            order += [("qkv", 12, 99, 1, 1), ("swao", 8, 99, 1, 1)]
        order += [(f"ffi2{l}1", 2 * FT, 4, 1, 1), (f"ffo2{l}1", 3 * KT, 12, 1, l == 0)]
    table, lot, split = {}, 0, 0
    for tag, n, per, is_split, chained in order:
        table[tag] = dict(n=n, per=per, lot0=lot, split0=split if is_split else None, chained=bool(chained))
        lot += n
        split += n if is_split else 0
    return table


STAGES = stage_table()


class Plan:

    def __init__(self, old=None):
        self.old = old
        self.count, self.event, self.delta, self.size, self.alias, self.banks = {}, {}, {}, {}, {}, {}
        self.taken = set()
        self.stage_start = {}
        self.loops = []

    def made(self, sem, key, inc=1):
        self.count[sem] = self.count.get(sem, 0) + inc
        assert (sem, key) not in self.event, (sem, key)
        self.event[sem, key] = (self.count[sem], [name for name, _, _ in self.loops])

    @contextmanager
    def loop(self, eng, name, n):
        before = dict(self.count)
        self.size[name] = n
        with eng.Fori(0, n) as i:
            self.loops.append((name, n, i))
            yield i
            self.loops.pop()
        for sem, now in list(self.count.items()):
            d = now - before.get(sem, 0)
            if d:
                self.delta[sem, name] = d
                self.count[sem] = before.get(sem, 0) + n * d

    def here(self, sem, v):
        for name, _, i in self.loops:
            d = self.old.delta.get((sem, name), 0) if self.old else 0
            if d:
                v = i * d + v
        return v

    def value(self, sem, key, **at):
        if self.old is None:
            return 1
        v, loops = self.old.event[sem, key]
        mine = {name: i for name, _, i in self.loops}
        for name in loops:
            i = at.get(name, mine.get(name, self.old.size[name] - 1))
            v = i * self.old.delta[sem, name] + v
        return v


def build(nc, old, x_in, ctx_in, pos_in, const_in, const1_in, par_in, w_proj, w_gate, w_up, w_out, ffn_in1, ffn_out1,
          mod_w, ffn_in2, ffn_out2, w_down, w_uq, w_ukv, w_mla_o, w_qkv, w_swa_o, out):
    plan = Plan(old)
    with ExitStack() as ctx:
        sems = {}

        def sem(name):
            if name not in sems:
                sems[name] = ctx.enter_context(nc.semaphore(name))
            return sems[name]

        def mark(name, key, inc=1):
            plan.made(name, key, inc)
            return sem(name), inc

        def done(name, key, **at):
            if old is not None and (name, key) in old.alias:
                name, key = "free", old.alias[name, key]
            if name == "free":
                name = f"bank{bank_index.get(key, 0)}_free"
            return sem(name), plan.value(name, key, **at)

        steps = {}

        def link(eng, name, ins):
            steps[name] = steps.get(name, 0) + 1
            ins.then_inc(*mark(name, steps[name]))
            eng.wait_ge(*done(name, steps[name]))

        ring = {"n": 0}
        bank_index = old.banks if old else {}

        def bank_free(key):
            b = ring["n"] % RING
            ring["n"] += 1
            plan.banks[key] = b
            name = f"bank{b}_free"
            before = plan.here(name, plan.count.get(name, 0))
            plan.made(name, key)
            return sem(name), before

        def bank_of(key):
            return psum[:, bank_index.get(key, 0), :]

        def freed(key, name=None, event=None):
            assert key not in plan.taken, key
            plan.taken.add(key)
            if name:
                plan.alias[name, event] = key
            return sem(f"bank{bank_index.get(key, 0)}_free"), 1

        place = {"at": 16512 // 4}

        def sb(name, shape, dt=F32, at=None):
            size = int(np.prod(shape[1:]))
            if at is None:
                at, place["at"] = place["at"], place["at"] + -(-size // 8) * 8
            t = nc.alloc_sbuf_tensor_at(name, shape, dt, offset=4 * at)
            return t[(slice(None),) * len(shape)]

        psum = ctx.enter_context(nc.psum_tensor("psum", [P, 8, 512], F32))[:, :, :]
        wring = sb("wring", [P, SLOTS, SLOT])
        whi = sb("whi", [P, SLOTS, SLOT], F32R)
        wlo = sb("wlo", [P, SLOTS, SLOT], F32R)
        X = sb("X", [P, KT, BOTH])
        h_at = place["at"]
        HHI = sb("HHI", [P, KT, BOTH], F32R)
        b1_at = place["at"]
        HLO = sb("HLO", [P, KT, BOTH], F32R)
        HF = sb("HF", [P, KT, BOTH], at=h_at)
        SQ = sb("SQ", [P, KT, BOTH], at=b1_at)
        HHI1 = sb("HHI1", [P, KT, SEQ], F32R, at=h_at)
        HLO1 = sb("HLO1", [P, KT, SEQ], F32R, at=h_at + KT * SEQ)
        COS = sb("COS", [P, SEQ], at=b1_at)
        SIN = sb("SIN", [P, SEQ], at=b1_at + SEQ)
        const1 = sb("const1", [P, N_CONST1], at=b1_at + 2 * SEQ)
        b1_at += 2 * SEQ + N_CONST1
        XP = sb("XP", [P, XBC_T, SEQ + CONV - 1], at=b1_at)
        assert b1_at + XBC_T * (SEQ + CONV - 1) <= h_at + 2 * KT * BOTH
        SPARE = sb("SPARE", [P, 8])
        R = sb("R", [P, BOTH])
        const = sb("const", [P, N_CONST])
        par = sb("par", [P, N_PAR])
        MODS = sb("MODS", [P, DEPTH, MOD_T, 2])
        NAS = sb("NAS", [P, DEPTH, 3 * KT, 2])
        COND = sb("COND", [P, KT, 32])
        ROW = sb("ROW", [P, 2, MOD_N])
        ARENA = 24100
        arena_at = place["at"]
        arena = sb("arena", [P, ARENA])
        assert place["at"] * 4 <= 229368, place["at"]

        def cst(name, rows=P):
            if name in C1:
                a, b = C1[name]
                return const1[0:rows, a:b]
            a, b = C[name]
            return const[0:rows, a:b]

        def prm(name, l, rows=P):
            a, b = PAR[name, l]
            return par[0:rows, a:b]

        def col(name, l, k, rows=P):
            a, _ = PAR[name, l]
            return par[0:rows, a + k:a + k + 1]

        def carve(parts, start=0):
            views, at = {}, start
            for name, *shape in parts:
                size = int(np.prod(shape))
                v = arena[:, at:at + size]
                if len(shape) == 2:
                    v = v.rearrange("p (a b) -> p a b", a=shape[0])
                elif len(shape) == 3:
                    v = v.rearrange("p (a b c) -> p a b c", a=shape[0], b=shape[1])
                views[name] = v
                at += size
            assert at <= ARENA, at
            views["end"] = at
            return views

        def mod_rows(b):
            return 32 * min(MOD_Q, MOD_G - b * MOD_Q)

        m1 = carve([("ybr", 10, SEQ), ("PJ", 12, SEQ), ("SG", 8, SEQ), ("V", TT, 768),
                    ("CV", XBC_T, SEQ), ("XC", XBC_T, SEQ)])
        gates = carve([("GT", KT, 4, SEQ)], m1["end"])["GT"]
        YBR, PJ, SG, V, CV, XC = (m1[k] for k in ("ybr", "PJ", "SG", "V", "CV", "XC"))
        FQ, GQ, RQ = 0, 4, 8
        t1 = carve([("A0", 4, SEQ), ("QZ", 4, SEQ), ("KF", 2, SEQ), ("RF", 4, SEQ),
                    ("E", 8, SEQ), ("PT", 4, TT * SEQ)], m1["end"])
        small = carve([("FX", 1, SEQ), ("FA", 1, SEQ), ("CC", 1, SEQ), ("NCC", 1, SEQ), ("NM", 1, 16), ("RS", 1, 16),
                       ("RC", 1, 16), ("DTT", TT, SSD_HEADS), ("GLR", 1, SEQ)], m1["end"] + 8192)
        g1 = carve([("GX", 2, SEQ), ("GA", 2, SEQ), ("B", 2, SEQ), ("ND", 2, SEQ), ("EB", 2, SEQ), ("EI", 2, SEQ),
                    ("EK", 2, SEQ), ("QDZ", 4, SEQ), ("KEZ", 2, TT * SEQ), ("AT", TT * HEADS, P),
                    ("S", NCHUNK * 2, HD), ("OB", 2, SEQ), ("OQ", 2, SEQ)], m1["end"])
        r1 = carve([("TC", 2, SEQ), ("TS", 2, SEQ), ("Q", 2, SEQ), ("K", 2, SEQ), ("QZ", HEADS * 2, SEQ),
                    ("RT", HEADS, CAUSAL), ("OB", 2, SEQ), ("OQ", 2, SEQ)], m1["end"])
        d1 = carve([("XDT", TT, 512), ("CZ", 2, SEQ), ("CB", 2, CAUSAL),
                    ("L", SSD_HEADS, CAUSAL), ("OD", 4, SEQ), ("OQ", 4, SEQ)], m1["end"])
        d2 = carve([("DX", 1, SEQ), ("DA", 1, SEQ), ("DL", 1, SEQ), ("CS", 1, SEQ), ("NCS", 1, SEQ), ("AE", 1, 1)],
                   small["end"])
        HIDHI = sb("HIDHI", [P, FT, BOTH], F32R, at=arena_at)
        HIDLO = sb("HIDLO", [P, FT, BOTH], F32R, at=arena_at + FT * BOTH)
        S = carve([("S", 2, BOTH)], 2 * FT * BOTH)["S"]
        HIDHI1 = sb("HIDHI1", [P, FT, SEQ], F32R, at=arena_at)
        HIDLO1 = sb("HIDLO1", [P, FT, SEQ], F32R, at=arena_at + FT * SEQ)
        S1 = carve([("S", 2, SEQ)], 2 * FT * SEQ)["S"]
        T1, SQ1 = (carve([("b", KT, SEQ)], at)["b"] for at in (m1["end"], m1["end"] + 6144))
        T2, SQA = (carve([("b", KT, BOTH)], at)["b"] for at in (0, KT * BOTH))
        mg = carve([("tmp", 4, 512)], m1["end"] + 8192)["tmp"]

        def first(tag):
            return tag[0] in ("n1", "n2")

        def h_of(tag):
            return (HHI1, HLO1, T1) if first(tag) else (HHI, HLO, T2)

        def sq_of(tag):
            return SQ1 if first(tag) else SQA if tag[0] == "b2" else SQ

        def hid_of(tag):
            return (HIDHI1, HIDLO1, S1) if first(tag) else (HIDHI, HIDLO, S)
        b2 = carve([("QN", MLA_H, BOTH), ("QR", 4, BOTH), ("QX", 4, SEQ), ("KN", MLA_H, BOTH), ("KZ", 8, BOTH),
                    ("VM", 4, 1024), ("CQ", 6, BOTH), ("PTX", 4, SEQ), ("PTC", 2, SEQ), ("NM", 1, 8), ("RS", 1, 8), ("RC", 1, 8)])
        n = MLA_H * BOTH + 4 * BOTH + 4 * SEQ
        b2.update({k: v for k, v in carve([("SQ2", 6, BOTH)], n).items() if k != "end"})
        n += MLA_H * BOTH + 8 * BOTH
        b2.update({k: v for k, v in carve([("RM", 2, BOTH)], n).items() if k != "end"})
        n += 4 * 1024
        b2.update({k: v for k, v in carve([("PR", 2, 1536)], n).items() if k != "end"})

        def mla_pr(h, qt):
            a = qt * BOTH if qt < 2 else 2 * BOTH + (qt - 2) * CTX
            return b2["PR"][:, h % 2, a:a + (BOTH if qt < 2 else CTX)]
        b3 = carve([("QS", 8, SEQ), ("QX", 8, SEQ), ("KAB", 2, BOTH), ("KR", 2, BOTH), ("TMP", 4, SEQ), ("KZ", 8, BOTH),
                    ("VS", 4, SEQ), ("PR", 8, BOTH), ("PTX", 8, SEQ), ("NM", 1, 8), ("RS", 1, 8), ("ES", 1, 8)])

        def flat(v):
            return v.rearrange("p a b -> p (a b)") if len(v.shape) == 3 else v

        def turns_of(tag):
            st = STAGES[tag]
            whole = st["n"] if st["chained"] else st["n"] - SLOTS
            return whole // st["per"] if whole // st["per"] > 1 else 0

        def lots(eng, tag, body):
            st, turns = STAGES[tag], turns_of(tag)
            if turns:
                with plan.loop(eng, tag, turns) as i:
                    for k in range(st["per"]):
                        body(i, k, k, True)
            for j in range(turns * st["per"], st["n"]):
                body(0, j, ("rest", j), st["chained"] or j < st["n"] - SLOTS)

        def lot_no(tag, i, k):
            return i * STAGES[tag]["per"] + k

        def raw_slot(tag, k):
            return (STAGES[tag]["lot0"] + k) % SLOTS

        def split_slot(tag, k):
            return (STAGES[tag]["split0"] + k) % SLOTS

        def counted(tag, i, k, first):
            return i * STAGES[tag]["per"] + (first + k + 1)

        def loaded(tag, i, k):
            st = STAGES[tag]
            g = st["lot0"] + k
            return sem(f"slot{g % SLOTS}_loaded"), i * (st["per"] * 16 // SLOTS) + 16 * (g // SLOTS + 1)

        def hi_ready(tag, i, k):
            return sem("weights_hi"), counted(tag, i, k, STAGES[tag]["split0"])

        def lo_ready(tag, i, k):
            return sem("weights_lo"), counted(tag, i, k, STAGES[tag]["split0"])

        def lot_done(tag, i, k):
            if tag[:4] == "proj":
                return done("filled", ("lot", tag, ("rest", k)))
            return sem("filled"), counted(tag, i, k, old.stage_start[tag] if old else 0)

        def lot_event(ins, tag, key):
            ins.then_inc(*mark("filled", ("lot", tag, key)))

        def slot_free(tag, j):
            g = STAGES[tag]["lot0"] + j - SLOTS
            for t, st in STAGES.items():
                if st["lot0"] <= g < st["lot0"] + st["n"]:
                    j = g - st["lot0"]
                    return lo_ready(t, 0, j) if st["split0"] is not None else done("filled", ("lot", t, ("rest", j)))

        def raw_blocks(tag, j, k, c):
            return wring[:, raw_slot(tag, j), 0:k * c].rearrange("p (k c) -> p k c", k=k)

        def split_blocks(tag, j, k, c):
            s = split_slot(tag, j)
            return tuple(w[:, s, 0:k * c].rearrange("p (k c) -> p k c", k=k) for w in (whi, wlo))

        def stream(sp, tag, src, size=None):
            st = STAGES[tag]
            size = size or (lambda k: SLOT)
            turns = st["n"] // st["per"]

            def load(i, k):
                s = raw_slot(tag, k)
                sp.dma_start(wring[:, s, 0:size(k)], src(i, k)).then_inc(sem(f"slot{s}_loaded"), 16)
            straight = st["per"] if turns > 1 else st["n"]
            for j in range(straight):
                if st["lot0"] + j >= SLOTS:
                    sp.wait_ge(*slot_free(tag, j))
                load(0, j)
            if turns > 1:
                with sp.Fori(1, turns) as i:
                    for k in range(st["per"]):
                        sp.wait_ge(*lo_ready(tag, i, k - SLOTS))
                        load(i, k)

        def tile_key(tag, k):
            return (k % 4, k // 4) if turns_of(tag) else (("rest", k), 0)

        BEFORE = {("n1", 1): "ffo0", ("n2", 0): "wo0", ("n2", 1): "wo1", ("b0", 0): "ffo1", ("b1", 0): "ffo200", ("b2", 0): "mlao",
                  ("b0", 1): "ffo201", ("b1", 1): "ffo210", ("b2", 1): "swao", "final": "ffo211"}

        def at_tile(name, tag, k):
            before = BEFORE.get(tag)
            if before and before[:3] == "ffo":
                key, i = tile_key(before, k)
                return done(name, (tag, key), **{before: i})
            return done(name, (tag, k))

        def x_at(tag, k):
            if tag[:3] == "ffo":
                key, i = tile_key(tag, k)
                return done("x_ready", (tag, key), **{tag: i})
            return done("x_ready", (tag, k))

        block = ctx.enter_context(nc.Block())

        @block.sync
        def _(sp):
            sp.dma_start(X[:, 0:KT // 2, 0:SEQ], x_in[:, 0:KT // 2, :]).then_inc(*mark("x_loaded", 0, 16))
            sp.dma_start(const[:, :], const_in).then_inc(*mark("const_loaded", 0, 16))
            sp.dma_start(X[:, KT // 2:KT, 0:SEQ], x_in[:, KT // 2:KT, :]).then_inc(*mark("x_rest_loaded", 0, 16))
            sp.dma_start(par[:, :], par_in).then_inc(*mark("par_loaded", 0, 16))
            sp.dma_start(COS.bitcast(I32), pos_in.to_broadcast([P, SEQ])).then_inc(*mark("pos_loaded", 0, 16))

            def tiles(w):
                return lambda i, k: w[i * 4 + k]

            def ffo(tag, w):
                stream(sp, tag, lambda i, k: w[i * 4 + k // 3][:, FF_PARTS[k % 3][0] * P:FF_PARTS[k % 3][1] * P],
                       lambda k: (FF_PARTS[k % 3][1] - FF_PARTS[k % 3][0]) * P)
            for l in range(DEPTH):
                stream(sp, f"proj{l}", tiles(w_proj[l]))
                if l == 0:
                    sp.dma_start(const1[:, :], const1_in).then_inc(*mark("const1_loaded", 0, 16))
                    sp.dma_start(X[:, :, SEQ:BOTH], ctx_in).then_inc(*mark("ctx_loaded", 0, 16))
                stream(sp, f"mod{l}", tiles(mod_w[l]))
                stream(sp, f"gate{l}", tiles(w_gate[l]))
                stream(sp, f"up{l}", tiles(w_up[l]))
                stream(sp, f"wo{l}", tiles(w_out[l]))
                stream(sp, f"ffi{l}", tiles(ffn_in1[l]))
                ffo(f"ffo{l}", ffn_out1[l])
            for l in range(DEPTH):
                stream(sp, f"ffi2{l}0", tiles(ffn_in2[l][0]))
                ffo(f"ffo2{l}0", ffn_out2[l][0])
                if l == 0:
                    stream(sp, "down", tiles(w_down))
                    stream(sp, "uq", tiles(w_uq))
                    stream(sp, "ukv", tiles(w_ukv))
                    stream(sp, "mlao", tiles(w_mla_o))
                else:
                    stream(sp, "qkv", tiles(w_qkv))
                    stream(sp, "swao", tiles(w_swa_o))
                stream(sp, f"ffi2{l}1", tiles(ffn_in2[l][1]))
                ffo(f"ffo2{l}1", ffn_out2[l][1])
            sp.wait_ge(*done("normed", ("final", KT - 1)))
            sp.dma_start(out, T2[:, :, 0:SEQ]).then_inc(*mark("stored", 0, 16))
            sp.wait_ge(*done("stored", 0))

        @block.gpsimd
        def _(pool):
            pool.memset(XP[:, :, 0:CONV - 1], 0.0).then_inc(*mark("conv_pad", 0))
            pool.memset(COND, 0.0).then_inc(*mark("cond_pad", 0))

        @block.tensor
        def _(pe):
            ident, ones, heads64 = cst("ident"), cst("ones"), cst("heads64")
            mm = pe.matmul

            def head_row(heads, h, n):
                return cst("ident", heads)[:, h:h + 1].to_broadcast([heads, n])

            def norm_sum(tag, n):
                pe.wait_ge(*bank_free(("ss", tag)))
                pe.wait_ge(*at_tile("sq_sum", tag, KT - 1))
                mm(bank_of(("ss", tag))[:, 0:n], ones, R[:, 0:n], start=True, stop=True).then_inc(*mark("filled", ("ss", tag)))

            def mm3(out_, w, a, start, stop):
                mm(out_, w[0], a[0], start=start, stop=False)
                mm(out_, w[0], a[1], start=False, stop=False)
                return mm(out_, w[1], a[0], start=False, stop=stop)

            def tile3(bank, w, h, n, before=None):
                for c in range(KT):
                    if before:
                        pe.wait_ge(*before(c))
                    last = mm3(bank[:, 0:n], (w[0][:, c, :], w[1][:, c, :]), (h[0][:, c, 0:n], h[1][:, c, 0:n]), c == 0, c == KT - 1)
                return last

            def dense(tag, n, h, ready=None):
                plan.stage_start[tag] = plan.count.get("filled", 0)

                def lot(i, k, key, _):
                    pe.wait_ge(*lo_ready(tag, i, k))
                    w = split_blocks(tag, k, KT, P)
                    pe.wait_ge(*bank_free((tag, key)))
                    lot_event(tile3(bank_of((tag, key)), w, h, n, ready if k == 0 else None), tag, key)
                lots(pe, tag, lot)

            def ffn(tag_in, tag_out, tag, n):
                dense(tag_in, n, h_of(tag), lambda c: done("h_ready", (tag, c)))
                plan.stage_start[tag_out] = plan.count["filled"]
                hi, lo, _ = hid_of(tag)

                def lot(i, k, key, _):
                    pe.wait_ge(*lo_ready(tag_out, i, k))
                    if k in (0, 2):
                        pe.wait_ge(*done("hidden", (tag, k)))
                    a, b = FF_PARTS[k % 3]
                    w = split_blocks(tag_out, k, b - a, P)
                    tkey = (tag, "o", key[1] // 3 if isinstance(key, tuple) else key // 3, isinstance(key, tuple))
                    if k % 3 == 0:
                        pe.wait_ge(*bank_free(tkey))
                    bank = bank_of(tkey)
                    for c in range(a, b):
                        last = mm3(bank[:, 0:n], (w[0][:, c - a, :], w[1][:, c - a, :]), (hi[:, c, 0:n], lo[:, c, 0:n]),
                                   c == 0, c == FT - 1)
                    lot_event(last, tag_out, key)
                lots(pe, tag_out, lot)

            def values3(keys, tag, j, part, tiles_, h):
                w = split_blocks(tag, j, KT // 2, 256)
                for tt in range(tiles_):
                    if part == 0:
                        pe.wait_ge(*bank_free(keys + (tt,)))
                    bank = bank_of(keys + (tt,))
                    for c in range(KT // 2):
                        k = part * KT // 2 + c
                        t = slice(tt * P, tt * P + P)
                        last = mm3(bank[:, 0:256], (h[0][:, k, t], h[1][:, k, t]), (w[0][:, c, :], w[1][:, c, :]), k == 0, k == KT - 1)
                return last

            def project(l):
                tag, h = f"proj{l}", h_of(("n1", l))
                plan.stage_start[tag] = plan.count["filled"]
                for j, name in enumerate(PROJ_LOTS):
                    fox_pe(l, j)
                    pe.wait_ge(*lo_ready(tag, 0, j))
                    if "." in name:
                        last = values3(("p", l, name[:2]), tag, j, int(name[3]), TT, h)
                    else:
                        key = ("p", l, name)
                        pe.wait_ge(*bank_free(key))
                        last = tile3(bank_of(key), split_blocks(tag, j, KT, P), h, SEQ,
                                     (lambda c: done("h_ready", (("n1", l), c))) if j == 0 else None)
                    lot_event(last, tag, ("rest", j))

            def head_sums(key, src, wait, n=512):
                pe.wait_ge(*done(*wait))
                pe.wait_ge(*bank_free(key))
                bank = bank_of(key)
                mm(bank[:, 0:n], heads64, flat(src), start=True, stop=True).then_inc(*mark("filled", key))

            def fox_pe(l, j):
                if j == FOX_SUMS:
                    for i in range(2):
                        head_sums(("ssf", l, i), t1["A0"][:, 2 * i:2 * i + 2, :], ("fox_sq", l))
                cs, ncs = small["CC"][0:HEADS, 0, :], small["NCC"][0:HEADS, 0, :]
                if FOX_SCORES <= j < FOX_SCORES + HEADS:
                    h = j - FOX_SCORES
                    if h == 0:
                        pe.wait_ge(*done("fox_qk", l))
                        pe.wait_ge(*done("fox_c", l))
                    for qt in range(TT):
                        nk, q = P * (qt + 1), slice(qt * P, qt * P + P)
                        pe.wait_ge(*bank_free(("fs", l, h, qt)))
                        bank = bank_of(("fs", l, h, qt))
                        mm(bank[:, 0:nk], t1["QZ"][:, h, q], t1["KF"][:, h // 2, 0:nk], start=True, stop=False)
                        mm(bank[:, 0:nk], cs[:, q], head_row(HEADS, h, nk), start=False, stop=False)
                        mm(bank[:, 0:nk], head_row(HEADS, h, P), ncs[:, 0:nk], start=False, stop=False)
                        mm(bank[:, qt * P:nk], ident, cst("mask_low"), start=False, stop=True).then_inc(*mark("filled", ("fs", l, h, qt)))
                if FOX_TURNS <= j < FOX_TURNS + HEADS:
                    h = j - FOX_TURNS
                    for qt in range(TT):
                        pe.wait_ge(*done("fox_p", (l, h, qt)))
                        pe.wait_ge(*bank_free(("ft", l, h, qt)))
                        bank = bank_of(("ft", l, h, qt))
                        for kt in range(qt + 1):
                            last = pe.transpose(bank[:, kt * P:kt * P + P],
                                                t1["E"][:, 2 * h + qt, kt * P:kt * P + P], ident)
                        last.then_inc(*mark("filled", ("ft", l, h, qt)))
                if j == FOX_OUT:
                    pe.wait_ge(*done("values", (l, 0, 1)))
                    PT = t1["PT"].rearrange("p h (k q) -> p h k q", k=TT)
                    for t in range(2):
                        pe.wait_ge(*bank_free(("fo", l, t)))
                        bank = bank_of(("fo", l, t))
                        for p in range(2):
                            h = 2 * t + p
                            pe.wait_ge(*done("fox_pt", (l, h, 1)))
                            v = slice(h * HD, h * HD + HD)
                            o = bank[p * HD:p * HD + HD, :]
                            mm(o[:, 0:P], V[:, 0, v], PT[:, h, 0, 0:P], start=True, stop=True)
                            mm(o[:, P:SEQ], V[:, 0, v], PT[:, h, 0, P:SEQ], start=True, stop=False)
                            last = mm(o[:, P:SEQ], V[:, 1, v], PT[:, h, 1, P:SEQ], start=False, stop=True)
                        last.then_inc(*mark("filled", ("fo", l, t)))

            def gla_pe(l):
                mods_pe(4)
                pe.wait_ge(*done("glr", l))
                pe.wait_ge(*bank_free(("la", l)))
                bank = bank_of(("la", l))
                w2 = prm("gla_w2", l, LOWRANK)
                for t in range(2):
                    last = mm(bank[:, t * SEQ:t * SEQ + SEQ], w2[:, t * P:t * P + P], small["GLR"][0:LOWRANK, 0, :],
                              start=True, stop=True)
                last.then_inc(*mark("filled", ("la", l)))
                mods_pe(8)
                pe.wait_ge(*done("gla_ke", l))
                pe.wait_ge(*bank_free(("gkt", l)))
                bank = bank_of(("gkt", l))
                for tt in range(TT):
                    for t in range(2):
                        last = pe.transpose(bank[:, (2 * tt + t) * P:(2 * tt + t + 1) * P],
                                            g1["EK"][:, t, tt * P:tt * P + P], ident)
                last.then_inc(*mark("filled", ("gkt", l)))
                mods_pe(3)
                pe.wait_ge(*done("gla_qdz", l))
                for tt in range(TT):
                    pe.wait_ge(*bank_free(("ga", l, tt)))
                    bank = bank_of(("ga", l, tt))
                    for h in range(HEADS):
                        last = mm(bank[:, h * P:h * P + P], g1["EI"][:, h // 2, tt * P:tt * P + P],
                                  g1["QDZ"][:, h, tt * P:tt * P + P], start=True, stop=True)
                    last.then_inc(*mark("filled", ("ga", l, tt)))
                mods_pe(3)
                pe.wait_ge(*done("values", (l, 1, 1)))
                pe.wait_ge(*done("gla_kez", l))
                pe.wait_ge(*bank_free(("gkv", l)))
                bank = bank_of(("gkv", l))
                KEZ = g1["KEZ"].rearrange("p c (t f) -> p c t f", t=TT)
                for c in range(NCHUNK - 1):
                    for h in range(HEADS):
                        p = HD * (h % 2)
                        last = mm(bank[p:p + HD, (2 * c + h // 2) * HD:(2 * c + h // 2 + 1) * HD],
                                  KEZ[:, c % 2, c // 2, h * HD:h * HD + HD], V[:, c // 2, SEQ + h * HD:SEQ + h * HD + HD],
                                  start=True, stop=True)
                last.then_inc(*mark("filled", ("gkv", l)))
                mods_pe(6)
                pe.wait_ge(*done("gla_at", (l, 1)))
                pe.wait_ge(*done("gla_s", (l, NCHUNK - 1)))
                for t in range(2):
                    pe.wait_ge(*bank_free(("go", l, t)))
                    bank = bank_of(("go", l, t))
                    for pp in range(2):
                        h = 2 * t + pp
                        o = bank[pp * HD:pp * HD + HD, :]
                        for tt in range(TT):
                            last = mm(o[:, tt * P:tt * P + P], V[:, tt, SEQ + h * HD:SEQ + h * HD + HD],
                                      g1["AT"][:, tt * HEADS + h, :], start=True, stop=False)
                            for c in (2 * tt, 2 * tt + 1):
                                if c:
                                    last = mm(o[:, c * CHUNK:c * CHUNK + CHUNK], g1["S"][:, 2 * c + t, :],
                                              g1["QDZ"][:, h, c * CHUNK:c * CHUNK + CHUNK], start=False, stop=c % 2 == 1)
                    last.then_inc(*mark("filled", ("go", l, t)))
                mod_columns(l, 0)
                mods_pe(3)
                head_sums(("gss", l), g1["OQ"], ("gla_oq", l))

            def causal_out(key, val, w):
                for t in range(val[1]):
                    pe.wait_ge(*bank_free(key + (t,)))
                    bank = bank_of(key + (t,))
                    for pp in range(2):
                        h = 2 * t + pp
                        o = bank[pp * HD:pp * HD + HD, :]
                        pe.wait_ge(*done(w[1], key[1:] + (h,)))
                        mm(o[:, 0:SEQ], val[0](0, h), w[0][:, h, 0:SEQ], start=True, stop=False)
                        last = mm(o[:, P:SEQ], val[0](1, h), w[0][:, h, SEQ:CAUSAL], start=False, stop=True)
                    last.then_inc(*mark("filled", key + (t,)))

            def ret_pe(l):
                mods_pe(7)
                mod_columns(l, 1)
                pe.wait_ge(*done("values", (l, 2, 1)))
                pe.wait_ge(*done("ret_qk", l))
                K, QZ = r1["K"], r1["QZ"]
                for h in range(HEADS):
                    pe.wait_ge(*bank_free(("rs", l, h)))
                    bank = bank_of(("rs", l, h))
                    for st in range(TT):
                        a, b = (0, SEQ) if st == 0 else (SEQ, CAUSAL)
                        for ab in range(2):
                            last = mm(bank[:, a:b], K[:, ab, st * P:st * P + P], QZ[:, 2 * h + ab, st * P:SEQ],
                                      start=(ab == 0), stop=(ab == 1))
                    last.then_inc(*mark("filled", ("rs", l, h)))
                mods_pe(2)
                causal_out(("ro", l), (lambda tt, h: V[:, tt, 512 + h * HD:512 + h * HD + HD], 2), (r1["RT"], "ret_w"))
                mods_pe(3)
                head_sums(("rss", l), r1["OQ"], ("ret_oq", l))

            def ssd_pe(l):
                CS, NCS = d2["CS"][0:SSD_HEADS, 0, :], d2["NCS"][0:SSD_HEADS, 0, :]
                mods_pe(9)
                mod_columns(l, 2)
                pe.wait_ge(*done("ssd_dt", l))
                pe.wait_ge(*bank_free(("dtt", l)))
                bank = bank_of(("dtt", l))
                for tt in range(TT):
                    last = pe.transpose(bank[:, tt * SSD_HEADS:(tt + 1) * SSD_HEADS],
                                        d2["DX"][0:SSD_HEADS, 0, tt * P:tt * P + P], ident[0:SSD_HEADS, 0:SSD_HEADS])
                last.then_inc(*mark("filled", ("dtt", l)))
                pe.wait_ge(*done("ssd_xc", l))
                for tt in range(TT):
                    pe.wait_ge(*bank_free(("xt", l, tt)))
                    bank = bank_of(("xt", l, tt))
                    for t in range(4):
                        last = pe.transpose(bank[:, t * P:t * P + P], XC[:, t, tt * P:tt * P + P], ident)
                    last.then_inc(*mark("filled", ("xt", l, tt)))
                mods_pe(3)
                pe.wait_ge(*done("ssd_cz", l))
                for g in range(2):
                    pe.wait_ge(*bank_free(("cb", l, g)))
                    bank = bank_of(("cb", l, g))
                    mm(bank[:, 0:SEQ], XC[:, 4, 0:P], d1["CZ"][:, g, :], start=True, stop=True)
                    last = mm(bank[:, SEQ:CAUSAL], XC[:, 4, P:SEQ], d1["CZ"][:, g, P:SEQ], start=True, stop=True)
                    last.then_inc(*mark("filled", ("cb", l, g)))
                pe.wait_ge(*done("ssd_cs", l))
                mods_pe(2)
                for h in range(SSD_HEADS):
                    mods_pe(1)
                    pe.wait_ge(*bank_free(("sg", l, h)))
                    bank = bank_of(("sg", l, h))
                    for st in range(TT):
                        a, n = st * SEQ, SEQ - st * P
                        mm(bank[:, a:a + n], head_row(SSD_HEADS, h, P), CS[:, st * P:SEQ], start=True, stop=False)
                        mm(bank[:, a:a + n], NCS[:, st * P:st * P + P], head_row(SSD_HEADS, h, n), start=False, stop=False)
                        last = mm(bank[:, a:a + P], ident, cst("mask_up"), start=False, stop=True)
                    last.then_inc(*mark("filled", ("sg", l, h)))
                mods_pe(4)
                pe.wait_ge(*done("ssd_xdt", (l, 1)))
                causal_out(("yo", l), (lambda tt, h: d1["XDT"][:, tt, h * HD:h * HD + HD], 4), (d1["L"], "ssd_w"))
                mods_pe(8)
                pe.wait_ge(*done("ssd_oq", l))
                pe.wait_ge(*bank_free(("yss", l)))
                bank = bank_of(("yss", l))
                for g in range(2):
                    for t in range(2):
                        last = mm(bank[:, g * SEQ:g * SEQ + SEQ], ones, d1["OQ"][:, 2 * g + t, :], start=(t == 0), stop=(t == 1))
                last.then_inc(*mark("filled", ("yss", l)))

            def merge_pe(l):
                dense(f"gate{l}", SEQ, h_of(("n1", l)))
                mod_columns(l, 3)
                mod_columns(l, 4)
                pe.wait_ge(*done("fox_y", (l, 1)))
                pe.wait_ge(*done("branches", (l, 9)))
                tag, bank_at = f"up{l}", None
                for b in range(10 * KT):
                    m, c, j = b // 10, b % 10, b // 8
                    if b % 8 == 0:
                        pe.wait_ge(*loaded(tag, 0, j))
                        w = raw_blocks(tag, j, 8, P)
                    half = int(c >= 4)
                    key = ("up", l, m, half)
                    if c in (0, 4):
                        pe.wait_ge(*bank_free(key))
                    q = (c // 2 if c < 4 else int(c >= 6)) % 2
                    last = mm(bank_of(key)[:, q * SEQ:q * SEQ + SEQ], w[:, b % 8, :], YBR[:, c, :],
                              start=c in (0, 2, 4, 6), stop=c in (1, 3, 5, 9))
                    if c in (3, 9):
                        last.then_inc(*mark("filled", key))
                        if b % 8 == 7:
                            plan.event["filled", ("lot", tag, ("rest", j))] = plan.event["filled", key]
                    elif b % 8 == 7:
                        lot_event(last, tag, ("rest", j))
                dense(f"wo{l}", SEQ, h_of(("n1", l)), lambda c: done("merged", (l, c)))

            turn = {"l": 0, "lot": 0}

            def mods_pe(n):
                l, tag = turn["l"], f"mod{turn['l']}"
                for j in range(turn["lot"], min(turn["lot"] + n, 4 * MOD_G)):
                    g, part = j // 4, j % 4
                    if (l, j) == (0, 0):
                        pe.wait_ge(*done("cond", 0))
                    i, q = l * MOD_B + g // MOD_Q, g % MOD_Q
                    if part == 0 and q == 0 and i >= 2:
                        pe.wait_ge(*done("mod_row", i - 2))
                    pe.wait_ge(*loaded(tag, 0, j))
                    w = raw_blocks(tag, j, 2, MOD_N)
                    for c in range(2):
                        k = 2 * part + c
                        last = mm(psum[32 * q:32 * q + 32, RING + i % 2, :], COND[:, k, :], w[:, c, :],
                                  start=(k == 0), stop=(k == KT - 1))
                    lot_event(last, tag, ("rest", j))
                    turn["lot"] = j + 1

            def mod_columns(l, b):
                i = l * MOD_B + b
                pe.wait_ge(*done("mod_row", i))
                pe.wait_ge(*bank_free(("mc", i)))
                bank, m = bank_of(("mc", i)), mod_rows(b)
                for t in range(MOD_N // P):
                    last = pe.transpose(bank[:, t * P:t * P + m], ROW[0:m, i % 2, t * P:(t + 1) * P], ident[0:m, 0:m])
                last.then_inc(*mark("filled", ("mc", i)))

            def mods_end():
                mods_pe(4 * MOD_G)
                turn.update(l=turn["l"] + 1, lot=0)

            def mla_pe():
                dense("down", BOTH, (HHI, HLO), lambda c: done("h_ready", (("b1", 0), c)))
                pe.wait_ge(*done("mla_sq", 5))
                for part, (a, b) in enumerate(((0, 4), (4, 6))):
                    pe.wait_ge(*bank_free(("mss", part)))
                    bank = bank_of(("mss", part))
                    for k in range(a, b):
                        last = mm(bank, ones, b2["SQ2"][:, k, :], start=(k == a), stop=(k == b - 1))
                    last.then_inc(*mark("filled", ("mss", part)))
                pe.wait_ge(*done("mla_c", 3))
                for j in range(6):
                    pe.wait_ge(*loaded("uq", 0, j))
                    w = raw_blocks("uq", j, 8, P)
                    for t in range(2):
                        key = ("uq", 2 * j + t)
                        pe.wait_ge(*bank_free(key))
                        for c in range(4):
                            last = mm(bank_of(key), w[:, 4 * t + c, :], b2["CQ"][:, c, :], start=(c == 0), stop=(c == 3))
                        last.then_inc(*mark("filled", key))
                    plan.event["filled", ("lot", "uq", ("rest", j))] = plan.event["filled", key]
                pe.wait_ge(*done("mla_c", 5))
                for j in range(2):
                    pe.wait_ge(*loaded("ukv", 0, j))
                    w = raw_blocks("ukv", j, 8, P)
                    for t in range(4):
                        key = ("kn", 4 * j + t)
                        pe.wait_ge(*bank_free(key))
                        for c in range(2):
                            last = mm(bank_of(key), w[:, 2 * t + c, :], b2["CQ"][:, 4 + c, :], start=(c == 0), stop=(c == 1))
                        last.then_inc(*mark("filled", key))
                    plan.event["filled", ("lot", "ukv", ("rest", j))] = plan.event["filled", key]
                for half in range(2):
                    pe.wait_ge(*loaded("ukv", 0, 2 + half))
                    w = raw_blocks("ukv", 2 + half, 2, 512)
                    for kt in range(4):
                        key = ("mv", kt, half)
                        pe.wait_ge(*bank_free(key))
                        for c in range(2):
                            last = mm(bank_of(key), b2["CQ"][:, 4 + c, kt * P:kt * P + P], w[:, c, :], start=(c == 0), stop=(c == 1))
                        last.then_inc(*mark("filled", key))
                    plan.event["filled", ("lot", "ukv", ("rest", 2 + half))] = plan.event["filled", key]
                pe.wait_ge(*done("mla_kz", 3))
                pe.wait_ge(*done("mla_qx", 1))
                pe.wait_ge(*done("mla_v", (3, 1)))
                pe.wait_ge(*done("mla_kn", 7))

                def scores(h):
                    for qt in range(2):
                        q = slice(qt * P, qt * P + P)
                        pe.wait_ge(*bank_free(("ms", h, qt)))
                        bank = bank_of(("ms", h, qt))
                        mm(bank, b2["QN"][:, h, q], b2["KN"][:, h, :], start=True, stop=False)
                        for ab in range(2):
                            kz = b2["KZ"][:, 2 * (h % 4) + ab, :]
                            mm(bank[:, 0:SEQ], b2["QX"][:, 2 * (h // 4) + ab, q], kz[:, 0:SEQ], start=False, stop=False)
                            last = mm(bank[:, SEQ:BOTH], b2["QR"][:, 2 * (h // 4) + ab, q], kz[:, SEQ:BOTH],
                                      start=False, stop=(ab == 1))
                        last.then_inc(*mark("filled", ("ms", h, qt)))
                    for qt in range(2):
                        q = slice(SEQ + qt * P, SEQ + qt * P + P)
                        pe.wait_ge(*bank_free(("ms", h, 2 + qt)))
                        bank = bank_of(("ms", h, 2 + qt))
                        mm(bank[:, 0:CTX], b2["QN"][:, h, q], b2["KN"][:, h, SEQ:BOTH], start=True, stop=False)
                        for ab in range(2):
                            last = mm(bank[:, 0:CTX], b2["QR"][:, 2 * (h // 4) + ab, q],
                                      b2["KZ"][:, 2 * (h % 4) + ab, SEQ:BOTH], start=False, stop=(ab == 1))
                        last.then_inc(*mark("filled", ("ms", h, 2 + qt)))

                def transposes(h):
                    for qt in range(4):
                        nk = 4 if qt < 2 else 2
                        pe.wait_ge(*done("mla_p", (h, qt)))
                        pe.wait_ge(*bank_free(("mt", h, qt)))
                        bank = bank_of(("mt", h, qt))
                        for kt in range(nk):
                            last = pe.transpose(bank[:, kt * P:kt * P + P], mla_pr(h, qt)[:, kt * P:kt * P + P], ident)
                        last.then_inc(*mark("filled", ("mt", h, qt)))

                def attend(h):
                    pe.wait_ge(*done("mla_pt", (h, 3)))
                    pe.wait_ge(*bank_free(("mo", h)))
                    bank = bank_of(("mo", h))
                    for kt in range(4):
                        mm(bank[:, 0:SEQ], b2["VM"][:, kt, h * P:h * P + P], b2["PTX"][:, kt, :], start=(kt == 0), stop=(kt == 3))
                    for kt in range(2):
                        last = mm(bank[:, SEQ:BOTH], b2["VM"][:, 2 + kt, h * P:h * P + P], b2["PTC"][:, kt, :],
                                  start=(kt == 0), stop=(kt == 1))
                    last.then_inc(*mark("filled", ("mo", h)))
                scores(0)
                for h in range(MLA_H):
                    transposes(h)
                    if h + 1 < MLA_H:
                        scores(h + 1)
                    attend(h)
                dense("mlao", BOTH, (HHI, HLO), lambda c: done("mla_o", c))

            def swa_pe():
                plan.stage_start["qkv"] = plan.count["filled"]
                for j in range(12):
                    pe.wait_ge(*lo_ready("qkv", 0, j))
                    if j < 10:
                        pe.wait_ge(*bank_free(("sq", j)))
                        last = tile3(bank_of(("sq", j)), split_blocks("qkv", j, KT, P), (HHI, HLO), BOTH if j < 2 else SEQ,
                                     (lambda c: done("h_ready", (("b1", 1), c))) if j == 0 else None)
                    else:
                        last = values3(("sv",), "qkv", j, j - 10, 4, (HHI, HLO))
                    lot_event(last, "qkv", ("rest", j))
                pe.wait_ge(*done("swa_kz", 3))
                pe.wait_ge(*done("swa_qx", 3))
                pe.wait_ge(*done("swa_v", 3))

                def scores(h):
                    j, g = h // 4, h % 4
                    for qt in range(2):
                        q = slice(qt * P, qt * P + P)
                        pe.wait_ge(*bank_free(("ws", h, qt)))
                        bank = bank_of(("ws", h, qt))
                        for ab in range(2):
                            mm(bank[:, 0:SEQ], b3["QX"][:, 2 * g + ab, q], b3["KZ"][:, 2 * j + ab, 0:SEQ],
                               start=(ab == 0), stop=False)
                        if qt == 0:
                            mm(bank[:, P:SEQ], ident, cst("mask_low"), start=False, stop=True)
                        else:
                            mm(bank[:, 0:P], ident, cst("mask_up"), start=False, stop=True)
                        for ab in range(2):
                            last = mm(bank[:, SEQ:BOTH], b3["QS"][:, 2 * g + ab, q], b3["KZ"][:, 2 * j + ab, SEQ:BOTH],
                                      start=(ab == 0), stop=(ab == 1))
                        last.then_inc(*mark("filled", ("ws", h, qt)))

                def transposes(t):
                    for h in (2 * t, 2 * t + 1):
                        for qt in range(2):
                            pe.wait_ge(*done("swa_p", (h, qt)))
                            pe.wait_ge(*bank_free(("wt", h, qt)))
                            bank = bank_of(("wt", h, qt))
                            for kt in range(4):
                                last = pe.transpose(bank[:, kt * P:kt * P + P], b3["PR"][:, 2 * (h % 4) + qt, kt * P:kt * P + P], ident)
                            last.then_inc(*mark("filled", ("wt", h, qt)))

                def attend(t):
                    pe.wait_ge(*bank_free(("wo2", t)))
                    bank = bank_of(("wo2", t))
                    for h in (2 * t, 2 * t + 1):
                        pe.wait_ge(*done("swa_pt", (h, 1)))
                        o = bank[HD * (h % 2):HD * (h % 2) + HD, 0:SEQ]
                        v = slice((h // 4) * HD, (h // 4) * HD + HD)
                        for kt in range(4):
                            last = mm(o, b3["VS"][:, kt, v], b3["PTX"][:, 4 * (h % 2) + kt, :], start=(kt == 0), stop=(kt == 3))
                    last.then_inc(*mark("filled", ("wo2", t)))
                scores(0)
                scores(1)
                for t in range(8):
                    transposes(t)
                    if t < 7:
                        scores(2 * t + 2)
                        scores(2 * t + 3)
                    attend(t)
                dense("swao", SEQ, (HHI, HLO), lambda c: done("swa_o", c))

            pe.wait_ge(*done("const_loaded", 0))
            pe.wait_ge(*done("par_loaded", 0))
            for l in range(DEPTH):
                norm_sum(("n1", l), SEQ)
                project(l)
                gla_pe(l)
                ret_pe(l)
                ssd_pe(l)
                mods_end()
                merge_pe(l)
                norm_sum(("n2", l), SEQ)
                ffn(f"ffi{l}", f"ffo{l}", ("n2", l), SEQ)
            for l in range(DEPTH):
                norm_sum(("b0", l), BOTH)
                ffn(f"ffi2{l}0", f"ffo2{l}0", ("b0", l), BOTH)
                norm_sum(("b1", l), BOTH)
                (mla_pe, swa_pe)[l]()
                n = BOTH if l == 0 else SEQ
                norm_sum(("b2", l), n)
                ffn(f"ffi2{l}1", f"ffo2{l}1", ("b2", l), n)
            norm_sum("final", SEQ)

        @block.scalar
        def _(act):
            A = act.activation
            one, eps = cst("one"), cst("eps")

            def square(tag, n, t, key):
                A(sq_of(tag)[:, t, 0:n], X[:, t, 0:n], ACT.Square).then_inc(*mark("squares", (tag, key)))

            def split(tag, i, k):
                if k >= SLOTS:
                    act.wait_ge(*lot_done(tag, i, k - SLOTS))
                act.wait_ge(*loaded(tag, i, k))
                A(whi[:, split_slot(tag, k), :], wring[:, raw_slot(tag, k), :], ACT.Copy).then_inc(sem("weights_hi"), 1)

            def split_first(tag, before=None):
                if before:
                    act.wait_ge(*lot_done(before, 0, STAGES[before]["n"] - 1))
                for k in range(SLOTS):
                    split(tag, 0, k)

            def logarithm_table():
                A(SPARE[:, 0:1], one, ACT.Ln)

            def residual(tag, norm, n):
                logarithm_table()

                def lot(i, k, key, splits):
                    if splits:
                        split(tag, i, k + SLOTS)
                    act.wait_ge(*x_at(tag, k))
                    square(norm, n, k, k)
                lots(act, tag, lot)

            def rsqrt(out_, bank_key, n, count, name, key):
                act.wait_ge(*done("filled", bank_key))
                bank = bank_of(bank_key)
                out_ = flat(out_)
                A(out_, bank[:, 0:n], ACT.Ln, bias=eps, scale=1.0 / count).then_inc(*freed(bank_key))
                act.wait_ge(*done("free", bank_key))
                A(out_, out_, ACT.Exp, scale=-0.5).then_inc(*mark(name, key))

            def ffn(tag_in, tag_out, tag, n, norm, norm_n):
                hi, _, S_ = hid_of(tag)

                def lot(i, k, key, splits):
                    if k % 2:
                        slot = k // 2 % 2
                        act.wait_ge(*lot_done(tag_in, i, k))
                        A(S_[:, slot, 0:n], bank_of((tag_in, key))[:, 0:n], ACT.Silu).then_inc(*freed((tag_in, key), "silu", (tag, k)))
                        for d in (-1, 0):
                            split(tag_in, i, k + d + SLOTS)
                        act.wait_ge(*done("hid_t", (tag, k)))
                        j = i * (STAGES[tag_in]["per"] // 2) + k // 2
                        A(hi[:, j, 0:n], S_[:, slot, 0:n], ACT.Copy).then_inc(*mark("hid_hi", (tag, k)))
                lots(act, tag_in, lot)
                logarithm_table()

                def lot2(i, k, key, splits):
                    if splits:
                        split(tag_out, i, k + SLOTS)
                    if k % 3 == 2:
                        tkey = ("rest", k // 3) if isinstance(key, tuple) else k // 3
                        act.wait_ge(*done("x_ready", (tag_out, tkey)))
                        square(norm, norm_n, i * 4 + k // 3, tkey)
                lots(act, tag_out, lot2)

            def project(l):
                tag = f"proj{l}"
                for j, name in enumerate(PROJ_LOTS):
                    if name in PROJ_ACT:
                        dst, key = PROJ_ACT[name], ("p", l, name)
                        act.wait_ge(*lot_done(tag, 0, j))
                        bank = bank_of(key)
                        if name[0] == "x":
                            if (l, dst) == (0, 0):
                                act.wait_ge(*done("conv_pad", 0))
                            A(XP[:, dst, CONV - 1:], bank[:, 0:SEQ], ACT.Copy).then_inc(*freed(key, "xbc", (l, dst)))
                        else:
                            A(SG[:, dst, :], bank[:, 0:SEQ], ACT.Silu).then_inc(*freed(key, "silu_gate", (l, dst)))
                    fox_act(l, j)
                    if j == CONV_OUT:
                        act.wait_ge(*done("conv", (l, XBC_T - 1)))
                        A(XC, CV, ACT.Silu).then_inc(*mark("ssd_xc", l))
                    if j + SLOTS < len(PROJ_LOTS):
                        split(tag, 0, j + SLOTS)

            def softplus_parts(ax, src, name, key, wait):
                act.wait_ge(*done(*wait))
                link(act, "act_step", A(ax, src, ACT.Abs))
                link(act, "act_step", A(ax, ax, ACT.Exp, scale=-1.0))
                A(ax, ax, ACT.Ln, bias=cst("one", ax.shape[0]), scale=1.0).then_inc(*mark(name, key))

            def fox_act(l, j):
                if j == FOX_SQUARES:
                    act.wait_ge(*done("fox_pj", (l, 3)))
                    A(t1["A0"], PJ[:, FQ:FQ + 4, :], ACT.Square).then_inc(*mark("fox_sq", l))
                    softplus_parts(small["FA"][0:HEADS, 0, :], small["FX"][0:HEADS, 0, :], "fox_ln", l, ("fox_fx", l))
                if j == FOX_FACTORS:
                    for i in range(2):
                        rsqrt(t1["RF"][:, 2 * i:2 * i + 2, :], ("ssf", l, i), 512, HD, "fox_r", (l, i))
                if FOX_SCORES <= j < FOX_SCORES + HEADS:
                    h = j - FOX_SCORES
                    for qt in range(TT):
                        i, nk = 2 * h + qt, P * (qt + 1)
                        act.wait_ge(*done("fox_nm", (l, h, qt)))
                        act.wait_ge(*done("filled", ("fs", l, h, qt)))
                        bank = bank_of(("fs", l, h, qt))
                        ins = A(t1["E"][:, i, 0:nk], bank[:, 0:nk], ACT.Exp, bias=small["NM"][:, 0, i:i + 1], scale=1.0,
                                accum_out=small["RS"][:, 0, i:i + 1])
                        ins.then_inc(*freed(("fs", l, h, qt), "fox_e", (l, h, qt)))
                if FOX_TURNS <= j < FOX_TURNS + HEADS:
                    h = j - FOX_TURNS
                    for qt in range(TT):
                        key = ("ft", l, h, qt)
                        act.wait_ge(*done("filled", key))
                        bank = bank_of(key)
                        PT = t1["PT"].rearrange("p h (k q) -> p h k q", k=TT)
                        src = bank[:, 0:P * (qt + 1)].rearrange("p (k q) -> p k q", k=qt + 1)
                        A(PT[:, h, 0:qt + 1, qt * P:qt * P + P], src, ACT.Copy).then_inc(*freed(key, "fox_pt", (l, h, qt)))
                if j == FOX_OUT:
                    for t in range(2):
                        act.wait_ge(*done("filled", ("fo", l, t)))
                        bank = bank_of(("fo", l, t))
                        A(YBR[:, t, :], bank[:, 0:SEQ], ACT.Copy).then_inc(*freed(("fo", l, t), "fox_y", (l, t)))

            def gla_act(l):
                softplus_parts(g1["GA"], g1["GX"], "gla_ln", l, ("gla_gx", l))
                act.wait_ge(*done("gla_b", l))
                A(g1["EB"], g1["B"], ACT.Exp, scale=1.0 / GLA_TAU).then_inc(*mark("gla_e", (l, 0)))
                A(g1["EI"], g1["B"], ACT.Exp, scale=-1.0 / GLA_TAU).then_inc(*mark("gla_e", (l, 1)))
                act.wait_ge(*done("gla_nd", l))
                A(g1["EK"], g1["ND"], ACT.Exp, scale=1.0 / GLA_TAU).then_inc(*mark("gla_e", (l, 2)))
                mod_row_act(l, 0)
                head_norm_act(l, "go", "gss", g1, "gla")

            def head_norm_act(l, okey, skey, buf, name):
                for t in range(2):
                    act.wait_ge(*done("filled", (okey, l, t)))
                    bank = bank_of((okey, l, t))
                    A(buf["OB"][:, t, :], bank[:, 0:SEQ], ACT.Copy).then_inc(*freed((okey, l, t)))
                    act.wait_ge(*done("free", (okey, l, t)))
                A(buf["OQ"], buf["OB"], ACT.Square).then_inc(*mark(f"{name}_oq", l))
                rsqrt(buf["OQ"], (skey, l), 512, HD, f"{name}_r", l)

            def ssd_act(l):
                DL = d2["DL"][0:SSD_HEADS, 0, :]
                softplus_parts(DL, d2["DX"][0:SSD_HEADS, 0, :], "ssd_ln", l, ("ssd_dx", l))
                A(d2["AE"][0:SSD_HEADS, 0, :], col("a_log", l, 0, SSD_HEADS), ACT.Exp).then_inc(*mark("ssd_ae", l))
                mod_row_act(l, 2)
                for g in range(2):
                    act.wait_ge(*done("filled", ("cb", l, g)))
                    bank = bank_of(("cb", l, g))
                    A(d1["CB"][:, g, :], bank[:, 0:CAUSAL], ACT.Copy).then_inc(*freed(("cb", l, g), "ssd_cb", (l, g)))
                for h in range(SSD_HEADS):
                    act.wait_ge(*done("filled", ("sg", l, h)))
                    bank = bank_of(("sg", l, h))
                    A(d1["L"][:, h, :], bank[:, 0:CAUSAL], ACT.Exp).then_inc(*freed(("sg", l, h), "ssd_l", (l, h)))
                act.wait_ge(*done("ssd_od", (l, 3)))
                A(d1["OQ"], d1["OD"], ACT.Square).then_inc(*mark("ssd_oq", l))
                mod_row_act(l, 3)
                split_first(f"gate{l}", f"proj{l}")
                rsqrt(d1["OQ"][:, 0:2, :], ("yss", l), 512, 256, "ssd_r", l)

            def merge_act(l):
                tag = f"gate{l}"
                act.wait_ge(*done("branches", (l, 9)))

                def lot(i, k, key, splits):
                    act.wait_ge(*lot_done(tag, i, k))
                    m = i if isinstance(key, int) else k // 4
                    A(gates[:, m, k % 4, :], bank_of((tag, key))[:, 0:SEQ], ACT.Sigmoid).then_inc(*freed((tag, key), "gate", (l, key)))
                    if splits:
                        split(tag, i, k + SLOTS)
                lots(act, tag, lot)
                act.wait_ge(*lot_done(tag, 0, 4 * KT - 1))
                for m in range(KT):
                    if m >= KT - 2:
                        split(f"wo{l}", 0, m - KT + 2)
                    act.wait_ge(*done("merged_t", (l, m)))
                    A(HHI1[:, m, :], mg[:, 2 * (m % 2), 0:SEQ], ACT.Copy).then_inc(*mark("merged_hi", (l, m)))
                for k in range(2, SLOTS):
                    split(f"wo{l}", 0, k)

            def mod_row_act(l, b):
                i, m = l * MOD_B + b, mod_rows(b)
                act.wait_ge(*done("filled", ("lot", f"mod{l}", ("rest", 4 * (b * MOD_Q + m // 32) - 1))))
                if i >= 2:
                    act.wait_ge(*done("filled", ("mc", i - 2)))
                A(ROW[0:m, i % 2, :], psum[0:m, RING + i % 2, :], ACT.Copy).then_inc(*mark("mod_row", i))

            def mla_act():
                for t in range(8):
                    key = ("down", ("rest", t))
                    act.wait_ge(*lot_done("down", 0, t))
                    bank = bank_of(key)
                    dst = b2["CQ"][:, t, :] if t < 6 else b2["QX"][:, 2 * (t - 6):2 * (t - 6) + 2, :]
                    src = bank if t < 6 else bank.rearrange("p (a b) -> p a b", a=2)
                    A(dst, src, ACT.Copy).then_inc(*freed(key, "mla_down", t))
                    if t + SLOTS < 8:
                        split("down", 0, t + SLOTS)
                    if t < 6:
                        act.wait_ge(*done("free", key))
                        A(b2["SQ2"][:, t, :], b2["CQ"][:, t, :], ACT.Square).then_inc(*mark("mla_sq", t))
                for part, count in ((0, 512), (1, 256)):
                    rsqrt(b2["RM"][:, part, :], ("mss", part), 512, count, "mla_r", part)
                for t in range(12):
                    key = ("uq", t)
                    act.wait_ge(*done("filled", key))
                    bank = bank_of(key)
                    if t < 8:
                        A(b2["QN"][:, t, :], bank, ACT.Copy).then_inc(*freed(key, "mla_qn", t))
                    else:
                        A(b2["QR"][:, t - 8, :], bank, ACT.Copy).then_inc(*freed(key, "mla_qr", t - 8))
                for h in range(MLA_H):
                    act.wait_ge(*done("filled", ("kn", h)))
                    bank = bank_of(("kn", h))
                    A(b2["KN"][:, h, :], bank, ACT.Copy).then_inc(*freed(("kn", h), "mla_kn", h))
                for kt in range(4):
                    for half in range(2):
                        act.wait_ge(*done("filled", ("mv", kt, half)))
                        bank = bank_of(("mv", kt, half))
                        A(b2["VM"][:, kt, half * 512:half * 512 + 512], bank, ACT.Copy).then_inc(*freed(("mv", kt, half), "mla_v", (kt, half)))
                def exps(h):
                    for qt in range(4):
                        nk = BOTH if qt < 2 else CTX
                        act.wait_ge(*done("mla_nm", (h, qt)))
                        act.wait_ge(*done("filled", ("ms", h, qt)))
                        bank = bank_of(("ms", h, qt))
                        i = 4 * (h % 2) + qt
                        ins = A(mla_pr(h, qt), bank[:, 0:nk], ACT.Exp, bias=b2["NM"][:, 0, i:i + 1],
                                scale=MLA_SCALE, accum_out=b2["RS"][:, 0, i:i + 1])
                        ins.then_inc(*freed(("ms", h, qt), "mla_e", (h, qt)))
                exps(0)
                for h in range(MLA_H):
                    for qt in range(4):
                        key = ("mt", h, qt)
                        act.wait_ge(*done("filled", key))
                        bank = bank_of(key)
                        nk = 4 if qt < 2 else 2
                        dst = b2["PTX" if qt < 2 else "PTC"][:, :, (qt % 2) * P:(qt % 2) * P + P]
                        A(dst, bank[:, 0:nk * P].rearrange("p (k q) -> p k q", k=nk), ACT.Copy).then_inc(*freed(key, "mla_pt", (h, qt)))
                    if h + 1 < MLA_H:
                        exps(h + 1)
                    act.wait_ge(*done("filled", ("mo", h)))
                    bank = bank_of(("mo", h))
                    A(HHI[:, h, :], bank, ACT.Copy).then_inc(*mark("mla_ohi", h))
                    if h == MLA_H // 2:
                        split_first("mlao", "down")

            def swa_act():
                for j in range(12):
                    act.wait_ge(*lot_done("qkv", 0, j))
                    if j < 2:
                        A(b3["KAB"][:, j, :], bank_of(("sq", j)), ACT.Copy).then_inc(*freed(("sq", j), "swa_kab", j))
                    elif j < 10:
                        A(b3["QS"][:, j - 2, :], bank_of(("sq", j))[:, 0:SEQ], ACT.Copy).then_inc(*freed(("sq", j), "swa_qs", j - 2))
                    elif j == 11:
                        for kt in range(4):
                            A(b3["VS"][:, kt, :], bank_of(("sv", kt))[:, 0:256], ACT.Copy).then_inc(*freed(("sv", kt), "swa_v", kt))
                    split("qkv", 0, j + SLOTS)
                def exps(t):
                    for h in (2 * t, 2 * t + 1):
                        for qt in range(2):
                            i = 2 * (h % 4) + qt
                            act.wait_ge(*done("swa_nm", (h, qt)))
                            act.wait_ge(*done("filled", ("ws", h, qt)))
                            bank = bank_of(("ws", h, qt))
                            A(b3["PR"][:, i, :], bank, ACT.Exp, bias=b3["NM"][:, 0, i:i + 1],
                                        scale=SWA_SCALE, accum_out=b3["RS"][:, 0, i:i + 1]).then_inc(*freed(("ws", h, qt), "swa_e", (h, qt)))
                            A(b3["ES"][:, 0, i:i + 1], prm("sink", 0)[:, h:h + 1], ACT.Exp,
                                   bias=b3["NM"][:, 0, i:i + 1]).then_inc(*mark("swa_es", (h, qt)))
                exps(0)
                for t in range(8):
                    for h in (2 * t, 2 * t + 1):
                        for qt in range(2):
                            key = ("wt", h, qt)
                            act.wait_ge(*done("filled", key))
                            bank = bank_of(key)
                            q = 4 * (h % 2)
                            A(b3["PTX"][:, q:q + 4, qt * P:qt * P + P],
                                        bank.rearrange("p (k q) -> p k q", k=4), ACT.Copy).then_inc(*freed(key, "swa_pt", (h, qt)))
                    if t < 7:
                        exps(t + 1)
                    act.wait_ge(*done("filled", ("wo2", t)))
                    bank = bank_of(("wo2", t))
                    A(HHI[:, t, 0:SEQ], bank[:, 0:SEQ], ACT.Copy).then_inc(*mark("swa_ohi", t))

            def norm_hi(tag, n, l=None, n3=None):
                hi, _, T = h_of(tag)
                for k in range(KT):
                    act.wait_ge(*done("normed", (tag, k)))
                    if l is None:
                        ins = A(hi[:, k, 0:n], T[:, k, 0:n], ACT.Copy)
                    else:
                        for s in range(n // SEQ):
                            w = slice(s * SEQ, s * SEQ + SEQ)
                            ins = A(hi[:, k, w], T[:, k, w], ACT.Identity, bias=MODS[:, l, 3 * n3 * KT + k, s:s + 1], scale=1.0)
                    ins.then_inc(*mark("h_hi", (tag, k)))

            act.wait_ge(*done("x_loaded", 0))
            for k in range(KT // 2):
                square(("n1", 0), SEQ, k, k)
            act.wait_ge(*done("x_rest_loaded", 0))
            for k in range(KT // 2, KT):
                square(("n1", 0), SEQ, k, k)
            act.wait_ge(*done("const_loaded", 0))
            act.wait_ge(*done("par_loaded", 0))
            logarithm_table()
            split_first("proj0")
            for l in range(DEPTH):
                rsqrt(R[:, 0:SEQ], ("ss", ("n1", l)), SEQ, D, "factor", ("n1", l))
                norm_hi(("n1", l), SEQ)
                if l == 0:
                    act.wait_ge(*done("cond_pad", 0))
                    A(COND[:, :, 0:2], prm("cond", 0).rearrange("p (k s) -> p k s", k=KT), ACT.Silu).then_inc(*mark("cond", 0))
                    for i, t in ((0, COS), (1, SIN)):
                        act.wait_ge(*done("angle", i))
                        A(t, t, ACT.Sin).then_inc(*mark("rotary", i))
                project(l)
                gla_act(l)
                mod_row_act(l, 1)
                head_norm_act(l, "ro", "rss", r1, "ret")
                ssd_act(l)
                mod_row_act(l, 4)
                merge_act(l)
                residual(f"wo{l}", ("n2", l), SEQ)
                rsqrt(R[:, 0:SEQ], ("ss", ("n2", l)), SEQ, D, "factor", ("n2", l))
                norm_hi(("n2", l), SEQ)
                if l:
                    act.wait_ge(*done("ctx_loaded", 0))
                    act.wait_ge(*done("h_ready", (("n2", l), KT - 1)))
                ffn(f"ffi{l}", f"ffo{l}", ("n2", l), SEQ, *((("b0", 0), BOTH) if l else (("n1", 1), SEQ)))
            for l in range(DEPTH):
                rsqrt(R[:, 0:BOTH], ("ss", ("b0", l)), BOTH, D, "factor", ("b0", l))
                norm_hi(("b0", l), BOTH, l, 0)
                ffn(f"ffi2{l}0", f"ffo2{l}0", ("b0", l), BOTH, ("b1", l), BOTH)
                rsqrt(R[:, 0:BOTH], ("ss", ("b1", l)), BOTH, D, "factor", ("b1", l))
                norm_hi(("b1", l), BOTH, l, 1)
                (mla_act, swa_act)[l]()
                n = BOTH if l == 0 else SEQ
                residual(("mlao", "swao")[l], ("b2", l), n)
                rsqrt(R[:, 0:n], ("ss", ("b2", l)), n, D, "factor", ("b2", l))
                norm_hi(("b2", l), n, l, 2)
                ffn(f"ffi2{l}1", f"ffo2{l}1", ("b2", l), n, *((("b0", 1), BOTH) if l == 0 else ("final", SEQ)))
            rsqrt(R[:, 0:SEQ], ("ss", "final"), SEQ, D, "factor", "final")

        @block.vector
        def _(dve):
            v = dve
            TTN, TS, STT = dve.tensor_tensor, dve.tensor_scalar, dve.scalar_tensor_tensor
            half, half8, quarter = cst("half"), cst("half8"), cst("quarter")
            ln = lambda ins: link(dve, "dve_step", ins)

            def angles():
                v.wait_ge(*done("pos_loaded", 0))
                T = [PJ[:, i, :] for i in range(4)]
                ln(v.tensor_copy(T[0], COS.bitcast(I32)))
                ln(TS(T[1], T[0], cst("inv"), None, ALU.mult))
                big = 1.5 * 2.0 ** 23
                for i, (dst, turn, back) in enumerate(((COS, 0.25, float(np.pi / 2)), (SIN, 0.0, 0.0))):
                    ln(TS(T[2], T[1], float(1 / (2 * np.pi)), turn, ALU.mult, ALU.add))
                    ln(TS(T[2], T[2], big, -big, ALU.add, ALU.add))
                    ln(STT(T[3], T[2], -6.28125, T[1], ALU.mult, ALU.add))
                    c2 = float(np.float32(2 * np.pi - 6.28125))
                    c3 = float(2 * np.pi - 6.28125 - c2)
                    ln(STT(T[3], T[2], -c2, T[3], ALU.mult, ALU.add))
                    ln(STT(T[3], T[2], -c3, T[3], ALU.mult, ALU.add))
                    pi = 3.1415925
                    ln(TS(T[3], T[3], back, pi, ALU.add, ALU.min))
                    TS(dst, T[3], -pi, None, ALU.max).then_inc(*mark("angle", i))

            def split(tag, i, k):
                v.wait_ge(*hi_ready(tag, i, k))
                s = split_slot(tag, k)
                TTN(wlo[:, s, :], wring[:, raw_slot(tag, k), :], whi[:, s, :].bitcast(F32), ALU.subtract).then_inc(sem("weights_lo"), 1)

            def split_first(tag):
                for k in range(SLOTS):
                    split(tag, 0, k)

            def add_square(tag, n, t, key):
                v.wait_ge(*done("squares", (tag, key)))
                TTN(R[:, 0:n], R[:, 0:n], sq_of(tag)[:, t, 0:n], ALU.add).then_inc(*mark("sq_sum", (tag, key)))
                v.wait_ge(*done("sq_sum", (tag, key)))

            def norm(tag, n, name, l, n3=None):
                hi, lo, T = h_of(tag)

                def scaled(k):
                    if n3 is None:
                        ins = STT(T[:, k, 0:n], X[:, k, 0:n], col(name, l, k), R[:, 0:n], ALU.mult, ALU.mult)
                    else:
                        for s in range(n // SEQ):
                            w = slice(s * SEQ, s * SEQ + SEQ)
                            ins = STT(T[:, k, w], X[:, k, w], NAS[:, l, n3 * KT + k, s:s + 1], R[:, w], ALU.mult, ALU.mult)
                    ins.then_inc(*mark("normed", (tag, k)))

                def rest(k):
                    v.wait_ge(*done("h_hi", (tag, k)))
                    if n3 is None:
                        ins = TTN(lo[:, k, 0:n], T[:, k, 0:n], hi[:, k, 0:n].bitcast(F32), ALU.subtract)
                    else:
                        for s in range(n // SEQ):
                            w = slice(s * SEQ, s * SEQ + SEQ)
                            ins = STT(lo[:, k, w], T[:, k, w], MODS[:, l, 3 * n3 * KT + k, s:s + 1], hi[:, k, w].bitcast(F32),
                                      ALU.add, ALU.subtract)
                    ins.then_inc(*mark("h_ready", (tag, k)))
                v.wait_ge(*done("factor", tag))
                for k in range(KT + 1):
                    if k < KT:
                        scaled(k)
                    if k >= 1 and tag != "final":
                        rest(k - 1)

            def project(l):
                tag = f"proj{l}"
                for j, name in enumerate(PROJ_LOTS):
                    key = ("p", l, name)
                    if name in PROJ_DVE:
                        dst = PROJ_DVE[name]
                        v.wait_ge(*lot_done(tag, 0, j))
                        v.tensor_copy(PJ[:, dst, :], bank_of(key)[:, 0:SEQ]).then_inc(*freed(key, ("fox_pj", "gla_pj", "ret_pj")[dst // 4], (l, dst % 4)))
                    elif name == "misc":
                        v.wait_ge(*lot_done(tag, 0, j))
                        bank = bank_of(key)
                        TS(small["FX"][0:HEADS, 0, :], bank[0:HEADS, 0:SEQ], col("fox_bf", l, 0, HEADS), None, ALU.add).then_inc(*mark("fox_fx", l))
                        v.tensor_copy(small["GLR"][0:LOWRANK, 0, :], bank[32:32 + LOWRANK, 0:SEQ]).then_inc(*mark("glr", l))
                        TS(d2["DX"][0:SSD_HEADS, 0, :], bank[64:64 + SSD_HEADS, 0:SEQ], col("dt_bias", l, 0, SSD_HEADS), None,
                           ALU.add).then_inc(*freed(key, "ssd_dx", l))
                    elif name[3:] == "1":
                        b = PROJ_V[name[:2]]
                        v.wait_ge(*lot_done(tag, 0, j))
                        for tt in range(TT):
                            key = ("p", l, name[:2], tt)
                            v.tensor_copy(V[:, tt, b * SEQ:b * SEQ + SEQ], bank_of(key)[:, 0:256]).then_inc(*freed(key, "values", (l, b, tt)))
                    fox_dve(l, j)
                    if CONV_LOT <= j < CONV_LOT + XBC_T:
                        convolution(l, j - CONV_LOT)
                    if j + SLOTS < len(PROJ_LOTS):
                        split(tag, 0, j + SLOTS)

            def convolution(l, t):
                v.wait_ge(*done("xbc", (l, t)))
                w = lambda i: col("conv_w", l, t * CONV + i)
                ln(TS(CV[:, t, :], XP[:, t, 0:SEQ], w(0), col("conv_b", l, t), ALU.mult, ALU.add))
                for i in range(1, CONV):
                    ins = STT(CV[:, t, :], XP[:, t, i:i + SEQ], w(i), CV[:, t, :], ALU.mult, ALU.add)
                    if i < CONV - 1:
                        ln(ins)
                ins.then_inc(*mark("conv", (l, t)))

            def fox_dve(l, j):
                if j == FOX_SQUARES + 1:
                    v.wait_ge(*done("fox_ln", l))
                    FX, FA = small["FX"][0:HEADS, 0, :], small["FA"][0:HEADS, 0, :]
                    CC, NCC = small["CC"][0:HEADS, 0, :], small["NCC"][0:HEADS, 0, :]
                    ln(TS(FX, FX, 0.0, None, ALU.min))
                    ln(TTN(FX, FX, FA, ALU.subtract))
                    ln(v.tensor_tensor_scan(CC, cst("ones", HEADS)[:, 0:1].to_broadcast([HEADS, SEQ]), FX, 0.0, ALU.mult, ALU.add))
                    TS(NCC, CC, -1.0, None, ALU.mult).then_inc(*mark("fox_c", l))
                if j == FOX_QK:
                    v.wait_ge(*done("fox_r", (l, 1)))
                    for t in range(2):
                        STT(t1["KF"][:, t, :], PJ[:, FQ + 2 + t, :], col("fox_kn", l, 0), t1["RF"][:, 2 + t, :], ALU.mult, ALU.mult).then_inc(*mark("fox_kf", (l, t)))
                    ln(STT(t1["A0"][:, 0:2, :], PJ[:, FQ:FQ + 2, :], col("fox_qn", l, 0), t1["RF"][:, 0:2, :], ALU.mult, ALU.mult))
                    for h in range(HEADS):
                        ins = TS(t1["QZ"][:, h, :], t1["A0"][:, h // 2, :], half8[:, h % 2:h % 2 + 1], None, ALU.mult)
                    ins.then_inc(*mark("fox_qk", l))
                if FOX_SCORES <= j < FOX_SCORES + HEADS:
                    h = j - FOX_SCORES
                    for qt in range(TT):
                        i, nk = 2 * h + qt, P * (qt + 1)
                        v.wait_ge(*done("filled", ("fs", l, h, qt)))
                        bank = bank_of(("fs", l, h, qt))
                        v.tensor_reduce(small["NM"][:, 0, i:i + 1], bank[:, 0:nk], AX_X, ALU.max, negate=True).then_inc(*mark("fox_nm", (l, h, qt)))
                if FOX_SCORES < j <= FOX_SCORES + HEADS:
                    h = j - FOX_SCORES - 1
                    for qt in range(TT):
                        i, nk = 2 * h + qt, P * (qt + 1)
                        v.wait_ge(*done("fox_e", (l, h, qt)))
                        ln(v.reciprocal(small["RC"][:, 0, i:i + 1], small["RS"][:, 0, i:i + 1]))
                        TS(t1["E"][:, i, 0:nk], t1["E"][:, i, 0:nk], small["RC"][:, 0, i:i + 1], None, ALU.mult).then_inc(*mark("fox_p", (l, h, qt)))

            def gla_dve(l):
                v.wait_ge(*done("filled", ("la", l)))
                bank = bank_of(("la", l))
                GX, B = g1["GX"], g1["B"]
                TS(GX[:, 0, :], bank[:, 0:SEQ], col("gla_b", l, 0), None, ALU.add)
                TS(GX[:, 1, :], bank[:, SEQ:512], col("gla_b", l, 1), None, ALU.add).then_inc(*freed(("la", l), "gla_gx", l))
                v.wait_ge(*done("gla_ln", l))
                v.wait_ge(*done("const1_loaded", 0))
                ln(TS(GX, GX, 0.0, None, ALU.min))
                ln(TTN(GX, GX, g1["GA"], ALU.subtract))
                for t in range(2):
                    ins = v.tensor_tensor_scan(B[:, t, :], cst("reset"), GX[:, t, :], 0.0, ALU.mult, ALU.add)
                ins.then_inc(*mark("gla_b", l))
                v.wait_ge(*done("gla_b", l))
                for t in range(2):
                    b4 = B[:, t, :].rearrange("p (c i) -> p c i", c=NCHUNK)
                    n4 = g1["ND"][:, t, :].rearrange("p (c i) -> p c i", c=NCHUNK)
                    ins = TTN(n4, b4[:, :, CHUNK - 1:CHUNK].to_broadcast([P, NCHUNK, CHUNK]), b4, ALU.subtract)
                ins.then_inc(*mark("gla_nd", l))
                v.wait_ge(*done("gla_e", (l, 0)))
                ln(STT(GX, PJ[:, GQ:GQ + 2, :], 0.125, g1["EB"], ALU.mult, ALU.mult))
                for h in range(HEADS):
                    ins = TS(g1["QDZ"][:, h, :], GX[:, h // 2, :], half[:, h % 2:h % 2 + 1], None, ALU.mult)
                v.wait_ge(*done("gla_e", (l, 1)))
                TTN(g1["EI"], g1["EI"], PJ[:, GQ + 2:GQ + 4, :], ALU.mult).then_inc(*mark("gla_qdz", l))
                v.wait_ge(*done("gla_e", (l, 2)))
                TTN(g1["EK"], g1["EK"], PJ[:, GQ + 2:GQ + 4, :], ALU.mult).then_inc(*mark("gla_ke", l))
                v.wait_ge(*done("filled", ("gkt", l)))
                bank = bank_of(("gkt", l))
                for c in range(2):
                    ins = TS(g1["KEZ"][:, c, :], bank, half[:, c:c + 1], None, ALU.mult)
                ins.then_inc(*freed(("gkt", l), "gla_kez", l))
                for tt in range(TT):
                    v.wait_ge(*done("filled", ("ga", l, tt)))
                    bank = bank_of(("ga", l, tt))
                    mask = cst("chunk_up").unsqueeze(1).to_broadcast([P, HEADS, P])
                    TTN(g1["AT"][:, tt * HEADS:(tt + 1) * HEADS, :], bank.rearrange("p (h t) -> p h t", h=HEADS), mask,
                                  ALU.mult).then_inc(*freed(("ga", l, tt), "gla_at", (l, tt)))
                v.wait_ge(*done("filled", ("gkv", l)))
                bank = bank_of(("gkv", l))
                S = g1["S"]
                kv = bank.rearrange("p (c d) -> p c d", c=8)
                ln(v.tensor_copy(S[:, 2:4, :], kv[:, 0:2, :]))
                for c in range(1, NCHUNK - 1):
                    for t in range(2):
                        e = c * CHUNK + CHUNK - 1
                        ins = STT(S[:, 2 * (c + 1) + t, :], S[:, 2 * c + t, :], g1["EB"][:, t, e:e + 1], kv[:, 2 * c + t, :],
                                  ALU.mult, ALU.add)
                        if c < NCHUNK - 2:
                            ln(ins)
                ins.then_inc(*freed(("gkv", l), "gla_s", (l, NCHUNK - 1)))
                mod_columns(l, 0)
                head_norm(l, g1, "gla", 2, 0)

            def head_norm(l, buf, name, y, sg):
                v.wait_ge(*done(f"{name}_r", l))
                ln(STT(buf["OB"], buf["OB"], col(f"{name}_norm", l, 0), buf["OQ"], ALU.mult, ALU.mult))
                v.wait_ge(*done("silu_gate", (l, 3)))
                ins = TTN(YBR[:, y:y + 2, :], buf["OB"], SG[:, sg:sg + 2, :], ALU.mult)
                ins.then_inc(*mark("branches", (l, y)))

            def rope(dst, src, cos, sin, tc, ts):
                bc = lambda t: t.unsqueeze(1).to_broadcast([P, 2, SEQ])
                TTN(tc, src, bc(cos), ALU.mult)
                ln(TTN(ts, src, bc(sin), ALU.mult))
                TTN(dst[:, 0, :], tc[:, 0, :], ts[:, 1, :], ALU.subtract)
                return TTN(dst[:, 1, :], ts[:, 0, :], tc[:, 1, :], ALU.add)

            def ret_dve(l):
                v.wait_ge(*done("rotary", 1))
                v.wait_ge(*done("gla_r", l))
                ln(rope(r1["K"], PJ[:, RQ + 2:RQ + 4, :], COS, SIN, r1["TC"], r1["TS"]))
                ln(rope(r1["Q"], PJ[:, RQ:RQ + 2, :], COS, SIN, r1["TC"], r1["TS"]))
                for h in range(HEADS):
                    ins = TS(r1["QZ"][:, 2 * h:2 * h + 2, :], r1["Q"], quarter[:, h:h + 1], None, ALU.mult)
                ins.then_inc(*mark("ret_qk", l))
                mod_columns(l, 1)
                dec = cst("decay").rearrange("p (h t) -> p h t", h=HEADS)
                for h in range(HEADS):
                    v.wait_ge(*done("filled", ("rs", l, h)))
                    bank = bank_of(("rs", l, h))
                    TTN(r1["RT"][:, h, :], bank[:, 0:CAUSAL], dec[:, h, :], ALU.mult).then_inc(*freed(("rs", l, h), "ret_w", (l, h)))
                head_norm(l, r1, "ret", 4, 2)

            def ssd_pre(l):
                v.wait_ge(*done("ssd_ln", l))
                DX, DA, DL = (d2[k][0:SSD_HEADS, 0, :] for k in ("DX", "DA", "DL"))
                CS, NCS, AE = (d2[k][0:SSD_HEADS, 0, :] for k in ("CS", "NCS", "AE"))
                ln(TS(DX, DX, 0.0, None, ALU.max))
                ins = TTN(DX, DX, DL, ALU.add)
                ins.then_inc(*mark("ssd_dt", l))
                v.wait_ge(*done("ssd_dt", l))
                v.wait_ge(*done("ssd_ae", l))
                ln(TS(DA, DX, AE, -1.0, ALU.mult, ALU.mult))
                ln(v.tensor_tensor_scan(CS, cst("ones", SSD_HEADS)[:, 0:1].to_broadcast([SSD_HEADS, SEQ]), DA, 0.0, ALU.mult, ALU.add))
                TS(NCS, CS, -1.0, None, ALU.mult).then_inc(*mark("ssd_cs", l))
                v.wait_ge(*done("ssd_xc", l))
                for g in range(2):
                    ins = TS(d1["CZ"][:, g, :], XC[:, 5, :], half[:, g:g + 1], None, ALU.mult)
                ins.then_inc(*mark("ssd_cz", l))
                mod_columns(l, 2)
                v.wait_ge(*done("filled", ("dtt", l)))
                bank = bank_of(("dtt", l))
                v.tensor_copy(small["DTT"], bank[:, 0:TT * SSD_HEADS].rearrange("p (t h) -> p t h", t=TT)).then_inc(*freed(("dtt", l)))
                dve.wait_ge(*done("free", ("dtt", l)))
                for tt in range(TT):
                    v.wait_ge(*done("filled", ("xt", l, tt)))
                    bank = bank_of(("xt", l, tt))
                    dt = small["DTT"][:, tt, :].unsqueeze(2).to_broadcast([P, SSD_HEADS, HD])
                    TTN(d1["XDT"][:, tt, :].rearrange("p (h d) -> p h d", h=SSD_HEADS),
                                  bank.rearrange("p (h d) -> p h d", h=SSD_HEADS), dt, ALU.mult).then_inc(*freed(("xt", l, tt), "ssd_xdt", (l, tt)))

            def ssd_dve(l):
                ssd_pre(l)
                for h in range(SSD_HEADS):
                    v.wait_ge(*done("ssd_cb", (l, h // 4)))
                    v.wait_ge(*done("ssd_l", (l, h)))
                    TTN(d1["L"][:, h, :], d1["L"][:, h, :], d1["CB"][:, h // 4, :], ALU.mult).then_inc(*mark("ssd_w", (l, h)))
                for t in range(4):
                    v.wait_ge(*done("filled", ("yo", l, t)))
                    bank = bank_of(("yo", l, t))
                    STT(d1["OD"][:, t, :], XC[:, t, :], col("ssd_d", l, t), bank[:, 0:SEQ], ALU.mult, ALU.add).then_inc(*freed(("yo", l, t)))
                    dve.wait_ge(*done("free", ("yo", l, t)))
                    v.wait_ge(*done("silu_gate", (l, 4 + t)))
                    TTN(d1["OD"][:, t, :], d1["OD"][:, t, :], SG[:, 4 + t, :], ALU.mult).then_inc(*mark("ssd_od", (l, t)))
                split_first(f"gate{l}")
                v.wait_ge(*done("ssd_r", l))
                for t in range(4):
                    ins = STT(YBR[:, 6 + t, :], d1["OD"][:, t, :], col("ssd_norm", l, t), d1["OQ"][:, t // 2, :], ALU.mult, ALU.mult)
                ins.then_inc(*mark("branches", (l, 9)))

            def merge_dve(l):
                def lot(i, k, key, splits):
                    if splits:
                        split(f"gate{l}", i, k + SLOTS)
                lots(v, f"gate{l}", lot)
                mod_columns(l, 3)
                mod_columns(l, 4)
                v.wait_ge(*done("gate", (l, ("rest", 4 * KT - 1))))
                for m in range(KT):
                    if m >= 2:
                        v.wait_ge(*done("merged", (l, m - 2)))
                    for q in range(2):
                        v.wait_ge(*done("filled", ("up", l, m, q)))
                        bank = bank_of(("up", l, m, q))
                        TTN(mg[:, 2 * (m % 2) + q, :], bank, flat(gates[:, m, 2 * q:2 * q + 2, :]), ALU.mult).then_inc(*freed(("up", l, m, q)))
                        dve.wait_ge(*done("free", ("up", l, m, q)))
                    a, b = mg[:, 2 * (m % 2), :], mg[:, 2 * (m % 2) + 1, :]
                    ln(TTN(a, a, b, ALU.add))
                    TTN(a[:, 0:SEQ], a[:, 0:SEQ], a[:, SEQ:512], ALU.add).then_inc(*mark("merged_t", (l, m)))
                    if m:
                        merged_lo(l, m - 1)
                    if m >= KT - 2:
                        split(f"wo{l}", 0, m - KT + 2)
                merged_lo(l, KT - 1)
                for k in range(2, SLOTS):
                    split(f"wo{l}", 0, k)
                residual(f"wo{l}", ("n2", l))

            def merged_lo(l, m):
                v.wait_ge(*done("merged_hi", (l, m)))
                TTN(HLO1[:, m, :], mg[:, 2 * (m % 2), 0:SEQ], HHI1[:, m, :].bitcast(F32), ALU.subtract).then_inc(*mark("merged", (l, m)))

            def residual(tag, norm, coef=None, n=SEQ, l=0):
                ln(v.memset(R[:, 0:n], 0.0))

                def lot(i, k, key, splits):
                    v.wait_ge(*lot_done(tag, i, k))
                    add_tile(k, bank_of((tag, key)), (tag, key), coef, n, (tag, k), l)
                    if splits:
                        split(tag, i, k + SLOTS)
                    add_square(norm, n, k, k)
                lots(v, tag, lot)

            def add_tile(m, bank, key, coef, n, event, l=0):
                if coef is None:
                    TTN(X[:, m, 0:n], X[:, m, 0:n], bank[:, 0:n], ALU.add).then_inc(*freed(key, "x_ready", event))
                    return
                for s in range(n // SEQ):
                    w = slice(s * SEQ, s * SEQ + SEQ)
                    ins = STT(X[:, m, w], bank[:, w], MODS[:, l, coef * KT + m, s:s + 1], X[:, m, w], ALU.mult, ALU.add)
                ins.then_inc(*freed(key, "x_ready", event))

            def ffn(tag_in, tag_out, tag, n, norm, norm_n, coef=None, l=0):
                hi, lo, S_ = hid_of(tag)

                def lot(i, k, key, splits):
                    if k % 2:
                        slot, up = k // 2 % 2, (tag_in, k - 1)
                        v.wait_ge(*done("silu", (tag, k)))
                        TTN(S_[:, slot, 0:n], S_[:, slot, 0:n], bank_of(up)[:, 0:n], ALU.mult).then_inc(*freed(up, "hid_t", (tag, k)))
                        for d in (-1, 0):
                            split(tag_in, i, k + d + SLOTS)
                        v.wait_ge(*done("hid_hi", (tag, k)))
                        j = i * (STAGES[tag_in]["per"] // 2) + k // 2
                        TTN(lo[:, j, 0:n], S_[:, slot, 0:n], hi[:, j, 0:n].bitcast(F32), ALU.subtract).then_inc(*mark("hidden", (tag, k - 1)))
                lots(v, tag_in, lot)
                ln(v.memset(R[:, 0:norm_n], 0.0))

                def lot2(i, k, key, splits):
                    rest = isinstance(key, tuple)
                    if k % 3 == 2:
                        bkey = (tag, "o", k // 3, rest)
                        v.wait_ge(*lot_done(tag_out, i, k))
                        add_tile(i * 4 + k // 3, bank_of(bkey), bkey, coef, n, (tag_out, ("rest", k // 3) if rest else k // 3), l)
                    if splits:
                        split(tag_out, i, k + SLOTS)
                    if k % 3 == 2:
                        add_square(norm, norm_n, i * 4 + k // 3, ("rest", k // 3) if rest else k // 3)
                lots(v, tag_out, lot2)

            def mod_columns(l, b):
                key, q, n = ("mc", l * MOD_B + b), mod_rows(b) // 32, MOD_N // P
                v.wait_ge(*done("filled", key))
                src = bank_of(key).rearrange("p (t r) -> p t r", t=n)
                a = b * MOD_Q * n
                for g in range(q):
                    bias = prm("mod_b", l)[:, a + g * n:a + (g + 1) * n].unsqueeze(2).to_broadcast([P, n, 2])
                    ins = TTN(MODS[:, l, a + g * n:a + (g + 1) * n, :], src[:, :, 32 * g:32 * g + 2], bias, ALU.add)
                ins.then_inc(*freed(key, "mod", (l, b)))

            def mods(l):
                v.wait_ge(*done("mod", (l, MOD_B - 1)))
                MOD, NA = MODS[:, l], NAS[:, l].rearrange("p (n k) s -> p n k s", n=3)
                g = prm("norm_g", l).rearrange("p (n k) -> p n k", n=3)
                for n3 in range(3):
                    STT(NA[:, n3, :, :], MOD[:, (3 * n3 + 1) * KT:(3 * n3 + 2) * KT, :], 1.0,
                        g[:, n3, :].unsqueeze(2).to_broadcast([P, KT, 2]), ALU.add, ALU.mult)
                for c in (2, 8):
                    ins = TS(MOD[:, c * KT:(c + 1) * KT, :], MOD[:, c * KT:(c + 1) * KT, :], 0.5, None, ALU.mult)
                ln(ins)

            def rope_keys(src, kr, kz, tmp, name):
                ln(rope(kr[:, :, 0:SEQ], src[:, :, 0:SEQ], cst("cos2"), cst("sin2"), tmp[:, 0:2, 0:SEQ], tmp[:, 2:4, 0:SEQ]))
                ln(v.tensor_copy(kr[:, :, SEQ:BOTH], src[:, :, SEQ:BOTH]))
                for j in range(4):
                    TS(kz[:, 2 * j:2 * j + 2, :], kr, quarter[:, j:j + 1], None, ALU.mult).then_inc(*mark(name, j))

            def mla_dve():
                KAB = b2["QX"].rearrange("p a b -> p (a b)").rearrange("p (a b) -> p a b", a=2)
                for k in range(SLOTS, 2 * SLOTS):
                    split("down", 0, k)
                v.wait_ge(*done("mla_down", 7))
                rope_keys(KAB, HF[:, 0:2, :], b2["KZ"], HF[:, 2:6, :], "mla_kz")
                for t in range(6):
                    v.wait_ge(*done("mla_r", t // 4))
                    g = col("q_norm", 0, t) if t < 4 else col("kv_norm", 0, t - 4)
                    STT(b2["CQ"][:, t, :], b2["CQ"][:, t, :], g, b2["RM"][:, t // 4, :], ALU.mult, ALU.mult).then_inc(*mark("mla_c", t))
                for j in range(2):
                    v.wait_ge(*done("mla_qr", 2 * j + 1))
                    ins = rope(b2["QX"][:, 2 * j:2 * j + 2, :], b2["QR"][:, 2 * j:2 * j + 2, 0:SEQ], cst("cos2"), cst("sin2"),
                               HF[:, 2:4, 0:SEQ], HF[:, 4:6, 0:SEQ])
                    ins.then_inc(*mark("mla_qx", j))
                    v.wait_ge(*done("mla_qx", j))
                def maxima(h):
                    for qt in range(4):
                        i, nk = 4 * (h % 2) + qt, BOTH if qt < 2 else CTX
                        v.wait_ge(*done("filled", ("ms", h, qt)))
                        bank = bank_of(("ms", h, qt))
                        ln(v.tensor_reduce(b2["NM"][:, 0, i:i + 1], bank[:, 0:nk], AX_X, ALU.max, negate=True))
                        TS(b2["NM"][:, 0, i:i + 1], b2["NM"][:, 0, i:i + 1], MLA_SCALE, None, ALU.mult).then_inc(*mark("mla_nm", (h, qt)))

                def weights(h):
                    for qt in range(4):
                        i, nk = 4 * (h % 2) + qt, BOTH if qt < 2 else CTX
                        v.wait_ge(*done("mla_e", (h, qt)))
                        ln(v.reciprocal(b2["RC"][:, 0, i:i + 1], b2["RS"][:, 0, i:i + 1]))
                        TS(mla_pr(h, qt), mla_pr(h, qt), b2["RC"][:, 0, i:i + 1], None, ALU.mult).then_inc(*mark("mla_p", (h, qt)))
                maxima(0)
                weights(0)
                for h in range(MLA_H):
                    if h + 1 < MLA_H:
                        maxima(h + 1)
                        weights(h + 1)
                    attended(("mo", h), HLO[:, h, :], HHI[:, h, :], "mla_ohi", "mla_o", h)
                    if h == MLA_H // 2:
                        split_first("mlao")
                residual("mlao", ("b2", 0), 5, BOTH, 0)

            def attended(key, lo, hi, before, after, h):
                v.wait_ge(*done(before, h))
                TTN(lo, bank_of(key)[:, 0:lo.shape[-1]], hi.bitcast(F32), ALU.subtract).then_inc(*freed(key, after, h))

            def swa_dve():
                for k in range(12):
                    split("qkv", 0, k + SLOTS)
                    if k == 1:
                        v.wait_ge(*done("swa_kab", 1))
                        rope_keys(b3["KAB"], b3["KR"], b3["KZ"], b3["TMP"], "swa_kz")
                    elif k < 10 and k % 2:
                        g = (k - 3) // 2
                        v.wait_ge(*done("swa_qs", 2 * g + 1))
                        ins = rope(b3["QX"][:, 2 * g:2 * g + 2, :], b3["QS"][:, 2 * g:2 * g + 2, :], cst("cos2"), cst("sin2"),
                                   b3["TMP"][:, 0:2, 0:SEQ], b3["TMP"][:, 2:4, 0:SEQ])
                        ins.then_inc(*mark("swa_qx", g))
                        v.wait_ge(*done("swa_qx", g))

                def maxima(t):
                    for h in (2 * t, 2 * t + 1):
                        for qt in range(2):
                            i = 2 * (h % 4) + qt
                            v.wait_ge(*done("filled", ("ws", h, qt)))
                            bank = bank_of(("ws", h, qt))
                            nm = b3["NM"][:, 0, i:i + 1]
                            ln(v.tensor_reduce(nm, bank, AX_X, ALU.max))
                            ln(TS(nm, nm, SWA_SCALE, prm("sink", 0)[:, h:h + 1], ALU.mult, ALU.max))
                            TS(nm, nm, -1.0, None, ALU.mult).then_inc(*mark("swa_nm", (h, qt)))

                def weights(t):
                    for h in (2 * t, 2 * t + 1):
                        for qt in range(2):
                            i = 2 * (h % 4) + qt
                            rs = b3["RS"][:, 0, i:i + 1]
                            v.wait_ge(*done("swa_es", (h, qt)))
                            v.wait_ge(*done("swa_e", (h, qt)))
                            ln(TTN(rs, rs, b3["ES"][:, 0, i:i + 1], ALU.add))
                            ln(v.reciprocal(rs, rs))
                            TS(b3["PR"][:, i, :], b3["PR"][:, i, :], rs, None, ALU.mult).then_inc(*mark("swa_p", (h, qt)))
                maxima(0)
                weights(0)
                for t in range(8):
                    if t < 7:
                        maxima(t + 1)
                        weights(t + 1)
                    attended(("wo2", t), HLO[:, t, 0:SEQ], HHI[:, t, 0:SEQ], "swa_ohi", "swa_o", t)
                residual("swao", ("b2", 1), 5, SEQ, 1)

            v.wait_ge(*done("const_loaded", 0))
            v.wait_ge(*done("par_loaded", 0))
            ln(v.memset(R[:, 0:SEQ], 0.0))
            v.wait_ge(*done("x_loaded", 0))
            for k in range(KT):
                add_square(("n1", 0), SEQ, k, k)
            split_first("proj0")
            for l in range(DEPTH):
                norm(("n1", l), SEQ, "ln1", l)
                if l == 0:
                    angles()
                project(l)
                gla_dve(l)
                ret_dve(l)
                ssd_dve(l)
                merge_dve(l)
                norm(("n2", l), SEQ, "ln2", l)
                mods(l)
                ffn(f"ffi{l}", f"ffo{l}", ("n2", l), SEQ, *((("b0", 0), BOTH) if l else (("n1", 1), SEQ)))
            v.wait_ge(*done("ctx_loaded", 0))
            for l in range(DEPTH):
                norm(("b0", l), BOTH, None, l, 0)
                ffn(f"ffi2{l}0", f"ffo2{l}0", ("b0", l), BOTH, ("b1", l), BOTH, 2, l)
                norm(("b1", l), BOTH, None, l, 1)
                (mla_dve, swa_dve)[l]()
                n = BOTH if l == 0 else SEQ
                norm(("b2", l), n, None, l, 2)
                ffn(f"ffi2{l}1", f"ffo2{l}1", ("b2", l), n, *((("b0", 1), BOTH) if l == 0 else ("final", SEQ)), 8, l)
            norm("final", SEQ, "final_g", 0)
    return plan


def constants():
    t, t1 = np.zeros((P, N_CONST), np.float32), np.zeros((P, N_CONST1), np.float32)

    def put(name, v):
        a, b = C1[name] if name in C1 else C[name]
        (t1 if name in C1 else t)[:v.shape[0], a:b] = v.reshape(v.shape[0], -1)
    r, c = np.arange(P)[:, None], np.arange(P)[None, :]
    put("ident", (r == c).astype(np.float32))
    put("ones", np.ones((P, P)))
    put("heads64", (r // HD == c // HD).astype(np.float32))
    put("mask_low", np.where(c <= r, 0.0, NEG))
    put("mask_up", np.where(r <= c, 0.0, NEG))
    put("chunk_up", ((r <= c) & (r // CHUNK == c // CHUNK)).astype(np.float32))
    put("reset", np.tile(np.arange(SEQ) % CHUNK != 0, (P, 1)).astype(np.float32))
    gamma = np.log(1.0 - 2.0 ** (-5.0 - np.arange(HEADS)))
    rel = np.concatenate([np.arange(SEQ)[None, :] - r, c - r], axis=1)
    put("decay", np.where(rel[:, None, :] >= 0, 0.125 * np.exp(np.maximum(rel, 0)[:, None, :] * gamma[None, :, None]), 0.0))
    i = np.arange(P) % 32
    tok = np.arange(SEQ)
    inv = np.exp(-np.log(10000.0) * (i % 16) / 16)
    ang = np.where(i < 16, 1, 0)[:, None] * (tok // 64)[None, :] * inv[:, None] \
        + np.where(i < 16, 0, 1)[:, None] * (tok % 64)[None, :] * inv[:, None]
    put("cos2", np.cos(ang))
    put("sin2", np.sin(ang))
    put("inv", (10000.0 ** (-i / 32.0))[:, None])
    put("eps", np.full((P, 1), 1e-6))
    put("one", np.ones((P, 1)))
    put("half", (r // HD == np.arange(2)).astype(np.float32))
    put("half8", 0.125 * (r // HD == np.arange(2)))
    put("quarter", (r // 32 == np.arange(4)).astype(np.float32))
    return t, t1


def kernel(**inputs):
    import concourse.bacc as bacc
    from concourse.bass_utils import run_bass_kernel_spmd

    g = {k: np.asarray(v) for k, v in inputs.items()}
    asc = np.ascontiguousarray

    def lots_of(w, cols, per):
        kt = w.shape[0] // P
        t = w[:, cols].reshape(kt, P, -1, per, P)
        return asc(t.transpose(2, 1, 3, 0, 4)).reshape(t.shape[2], P, per * kt * P)

    def wide(w, cols):
        t = w[:, cols].reshape(w.shape[0] // P, P, -1)
        return asc(t.transpose(1, 0, 2)).reshape(1, P, -1)

    def halved(w):
        return asc(w.reshape(P, 2, SLOT).transpose(1, 0, 2))

    def mod_lots(w):
        t = w.reshape(4, 2, P, MOD_G, MOD_N)
        return asc(t.transpose(3, 0, 2, 1, 4)).reshape(4 * MOD_G, P, SLOT)

    def cols_of(v):
        return v.reshape(-1, P).T

    halves = lambda base, heads, step, off: np.concatenate([base + h * step + off + np.arange(32) for h in heads])
    ar = np.arange
    start = {}
    at = 0
    for name, n in (("fq", 256), ("fk", 256), ("fv", 256), ("ff", 4), ("gq", 256), ("gk", 256), ("gv", 256), ("glr", 16),
                    ("gr", 256), ("rq", 256), ("rk", 256), ("rv", 256), ("rg", 256), ("z", 512), ("x", 768), ("dt", 8),
                    ("gates", 4096)):
        start[name] = at
        at += n

    def tile_cols(name):
        if name[:2] in ("rq", "rk"):
            return halves(start[name[:2]], range(4), 64, 32 if name[2] == "b" else 0)
        return start[name[:-1]] + int(name[-1]) * P + ar(P)

    proj, gate = [], []
    for l in range(DEPTH):
        w = g["w_in"][l]
        rows = []
        for name in PROJ_LOTS:
            if name == "misc":
                m = np.zeros((D, P), np.float32)
                for part, a, n in (("ff", 0, 4), ("glr", 32, 16), ("dt", 64, 8)):
                    m[:, a:a + n] = w[:, start[part]:start[part] + n]
                rows.append(lots_of(m, ar(P), 1))
            elif name[3:] == "0":
                rows.append(halved(wide(w, start[name[:2]] + ar(256))))
            elif "." not in name:
                rows.append(lots_of(w, tile_cols(name), 1))
        proj.append(np.concatenate(rows))
        gate.append(lots_of(w, np.concatenate([start["gates"] + q * D + m * P + ar(P) for m in range(KT) for q in range(4)]), 1))
    up = np.stack([asc(lots_of(np.concatenate([g[f"w_up_{b}"][l] for b in "abcd"]), ar(D), 8).reshape(P, 10, SLOT).transpose(1, 0, 2))
                   for l in range(DEPTH)])
    pairs = np.concatenate([np.concatenate([FF + j * P + ar(P), j * P + ar(P)]) for j in range(FT)])
    uq_cols = np.concatenate([h * 192 + ar(P) for h in range(8)]
                             + [halves(128, range(4 * j, 4 * j + 4), 192, o) for j in range(2) for o in (0, 32)])
    ukv = g["mla_w_ukv_2"][0]
    q_cols = np.concatenate([halves(D, range(4), 64, o) for o in (0, 32)]
                            + [halves(0, [j * 4 + gg for j in range(4)], 64, o) for gg in range(4) for o in (0, 32)])
    down_cols = np.concatenate([ar(768), np.tile(768 + ar(32), 4), np.tile(800 + ar(32), 4)])
    par = np.zeros((P, N_PAR), np.float32)

    def put(name, l, v):
        a, b = PAR[name, l]
        par[:v.shape[0], a:b] = v.reshape(v.shape[0], -1)
    for l in range(DEPTH):
        put("ln1", l, cols_of(g["ln1"][l]))
        put("ln2", l, cols_of(g["ln2"][l]))
        for name in ("fox_qn", "fox_kn", "gla_norm", "ret_norm"):
            put(name, l, np.tile(g[name][l], 2)[:, None])
        put("gla_b", l, cols_of(g["gla_b"][l]))
        put("conv_w", l, g["ssd_conv_w"][l].reshape(CONV, XBC_T, P).transpose(2, 1, 0))
        put("conv_b", l, cols_of(g["ssd_conv_b"][l]))
        put("ssd_d", l, cols_of(np.repeat(g["ssd_d"][l], HD)))
        put("ssd_norm", l, cols_of(g["ssd_norm"][l]))
        put("fox_bf", l, g["fox_bf"][l][:, None])
        put("dt_bias", l, g["ssd_dt_bias"][l][:, None])
        put("a_log", l, g["ssd_a_log"][l][:, None])
        put("gla_w2", l, g["gla_w2"][l])
        put("mod_b", l, cols_of(g["mod_b_2"][l]))
        put("norm_g", l, cols_of(g["norm_g_2"][l]))
    put("final_g", 0, cols_of(g["final_norm_g_2"]))
    put("q_norm", 0, cols_of(g["mla_q_norm_2"][0]))
    put("kv_norm", 0, cols_of(g["mla_kv_norm_2"][0]))
    put("sink", 0, np.tile(g["swa_sink_2"][0], (P, 1)))
    put("cond", 0, np.stack([cols_of(g["c_2"][0]), cols_of(g["c_ctx_2"])], axis=2))

    ffo = lambda w: asc(w.reshape(FT, P, KT, P).transpose(2, 1, 0, 3)).reshape(KT, P, FT * P)
    seq = lambda x: asc(x[0].T.reshape(KT, P, SEQ).transpose(1, 0, 2))
    const, const1 = constants()
    arrays = {
        "x_in": seq(g["x"]), "ctx_in": seq(g["ctx_2"]), "pos_in": asc(g["positions"]), "const_in": const, "const1_in": const1, "par_in": par,
        "w_proj": np.stack(proj), "w_gate": np.stack(gate), "w_up": up,
        "w_out": np.stack([lots_of(g["w_out"][l], ar(D), 1) for l in range(DEPTH)]),
        "ffn_in1": np.stack([lots_of(g["w_ffn_in"][l], pairs, 1) for l in range(DEPTH)]),
        "ffn_out1": np.stack([ffo(g["w_ffn_out"][l]) for l in range(DEPTH)]),
        "mod_w": np.stack([mod_lots(g["mod_w_2"][l]) for l in range(DEPTH)]),
        "ffn_in2": np.stack([np.stack([lots_of(g["ffn_w_in_2"][l, i], pairs, 1) for i in range(2)]) for l in range(DEPTH)]),
        "ffn_out2": np.stack([np.stack([ffo(g["ffn_w_out_2"][l, i]) for i in range(2)]) for l in range(DEPTH)]),
        "w_down": lots_of(g["mla_w_down_2"][0], down_cols, 1),
        "w_uq": lots_of(g["mla_w_uq_2"][0], uq_cols, 2),
        "w_ukv": np.concatenate([lots_of(ukv, np.concatenate([h * 256 + ar(P) for h in range(8)]), 4)]
                                + [wide(ukv, np.concatenate([h * 256 + P + ar(P) for h in range(4 * i, 4 * i + 4)])) for i in range(2)]),
        "w_mla_o": lots_of(g["mla_w_o_2"][0], ar(D), 1),
        "w_qkv": np.concatenate([lots_of(g["swa_w_qkv_2"][0], q_cols, 1), halved(wide(g["swa_w_qkv_2"][0], D + 256 + ar(256)))]),
        "w_swa_o": lots_of(g["swa_w_o_2"][0], ar(D), 1),
    }

    def program(old):
        nc = bacc.Bacc("TRN2", target_bir_lowering=False, num_devices=1)
        args = [nc.dram_tensor(name, a.shape, mybir.dt.from_np(a.dtype), kind="ExternalInput").ap() for name, a in arrays.items()]
        out = nc.dram_tensor("out", (P, KT, SEQ), F32, kind="ExternalOutput").ap()
        return nc, build(nc, old, *args_in_order(dict(zip(arrays, args))), out)

    plan = None
    for _ in range(3):
        nc, plan = program(plan)
    r = run_bass_kernel_spmd(nc, [arrays], core_ids=[0])
    return asc(np.asarray(r.results[0]["out"]).transpose(2, 1, 0)).reshape(1, SEQ, D)


def args_in_order(a):
    return [a[n] for n in ("x_in", "ctx_in", "pos_in", "const_in", "const1_in", "par_in", "w_proj", "w_gate", "w_up", "w_out", "ffn_in1",
                           "ffn_out1", "mod_w", "ffn_in2", "ffn_out2", "w_down", "w_uq", "w_ukv", "w_mla_o", "w_qkv", "w_swa_o")]
```
